# Optimizing a Trainium2 kernel written in Bass

```python
import math
import jax, jax.numpy as jnp
from jax import lax
import numpy as np
import jax
import jax.numpy as jnp

D_MODEL = 1024
BATCH = 1
SEQ = 512
DEPTH = 1

D_MIX = D_MODEL
EPS = 1e-6
ROPE_THETA = 10000.0

MLA_HEADS = 8
MLA_QK_NOPE = 64
MLA_QK_ROPE = 32
MLA_QK_DIM = MLA_QK_NOPE + MLA_QK_ROPE
MLA_V_DIM = 64
MLA_Q_RANK = 256
MLA_KV_RANK = 128
MLA_WIDTH = MLA_HEADS * MLA_V_DIM
ATTN_BLOCK = 128

RET_HEADS = 8
RET_HEAD_DIM = 64
RET_WIDTH = RET_HEADS * RET_HEAD_DIM
RET_CHUNK = 128

IN_SPLITS = (
    MLA_Q_RANK,
    MLA_KV_RANK,
    MLA_QK_ROPE,
    RET_WIDTH, RET_WIDTH, RET_WIDTH, RET_WIDTH,
)
IN_COLS = sum(IN_SPLITS)

PEER_HEADS = 8
PEER_N_KEYS = 128
PEER_N_EXPERTS = PEER_N_KEYS * PEER_N_KEYS
PEER_KEY_DIM = 256
PEER_HALF = PEER_KEY_DIM // 2
PEER_TOPK = 16
PEER_TOKEN_BLOCK = 128


def rms_norm(x, g):
    xf = x.astype(jnp.float32)
    y = xf * lax.rsqrt(jnp.mean(xf * xf, axis=-1, keepdims=True) + EPS)
    return (y * g.astype(jnp.float32)).astype(x.dtype)

def rope(x, positions):
    d = x.shape[-1]
    inv = ROPE_THETA ** (-jnp.arange(0, d, 2, dtype=jnp.float32) / d)
    ang = positions.astype(jnp.float32)[:, :, None, None] * inv
    cos, sin = jnp.cos(ang), jnp.sin(ang)
    x1, x2 = jnp.split(x.astype(jnp.float32), 2, axis=-1)
    out = jnp.concatenate([x1 * cos - x2 * sin, x1 * sin + x2 * cos], axis=-1)
    return out.astype(x.dtype)

def mla_group(q_lat, kv_lat, k_rope, positions, g_q_norm, w_uq, g_kv_norm, w_ukv):
    B, S, _ = q_lat.shape
    q = (rms_norm(q_lat, g_q_norm) @ w_uq).reshape(B, S, MLA_HEADS, MLA_QK_DIM)
    q_nope, q_rope = q[..., :MLA_QK_NOPE], q[..., MLA_QK_NOPE:]
    q_rope = rope(q_rope, positions)
    kv = (rms_norm(kv_lat, g_kv_norm) @ w_ukv).reshape(B, S, MLA_HEADS, MLA_QK_NOPE + MLA_V_DIM)
    k_nope, v = kv[..., :MLA_QK_NOPE], kv[..., MLA_QK_NOPE:]
    k_r = rope(k_rope[:, :, None, :], positions)
    k = jnp.concatenate([k_nope, jnp.broadcast_to(k_r, (B, S, MLA_HEADS, MLA_QK_ROPE))], axis=-1)
    qh = jnp.concatenate([q_nope, q_rope], axis=-1) * (MLA_QK_DIM ** -0.5)

    nb = S // ATTN_BLOCK
    q_blocks = qh.reshape(B, nb, ATTN_BLOCK, MLA_HEADS, MLA_QK_DIM).transpose(1, 0, 2, 3, 4)
    key_pos = jnp.arange(S)

    def one_block(args):
        qb, bi = args
        s = jnp.einsum('bqhd,bkhd->bhqk', qb, k).astype(jnp.float32)
        q_pos = bi * ATTN_BLOCK + jnp.arange(ATTN_BLOCK)
        mask = key_pos[None, :] <= q_pos[:, None]
        s = jnp.where(mask[None, None], s, -jnp.inf)
        p = jax.nn.softmax(s, axis=-1).astype(v.dtype)
        return jnp.einsum('bhqk,bkhd->bqhd', p, v)

    out = lax.map(one_block, (q_blocks, jnp.arange(nb)))
    return out.transpose(1, 0, 2, 3, 4).reshape(B, S, MLA_WIDTH)

def retention_group(q, k, v, gate, positions, g_ret_norm):
    B, S, _ = q.shape
    H, d, C = RET_HEADS, RET_HEAD_DIM, RET_CHUNK
    nc = S // C
    q = rope(q.reshape(B, S, H, d), positions)
    k = rope(k.reshape(B, S, H, d), positions) * (d ** -0.5)
    v = v.reshape(B, S, H, d)

    gamma = 1.0 - 2.0 ** (-5.0 - jnp.arange(H, dtype=jnp.float32))
    log_g = jnp.log(gamma)
    idx = jnp.arange(C, dtype=jnp.float32)
    diff = idx[:, None] - idx[None, :]
    dmask = jnp.where(diff >= 0, jnp.exp(log_g[:, None, None] * jnp.maximum(diff, 0.0)), 0.0)

    qc = q.reshape(B, nc, C, H, d).astype(jnp.float32)
    kc = k.reshape(B, nc, C, H, d).astype(jnp.float32)
    vc = v.reshape(B, nc, C, H, d).astype(jnp.float32)

    scores = jnp.einsum('bnihd,bnjhd->bnhij', qc, kc) * dmask
    y_inner = jnp.einsum('bnhij,bnjhd->bnihd', scores, vc)

    zeta = jnp.exp(log_g[:, None] * (C - 1.0 - idx))
    kv_chunk = jnp.einsum('bnjhk,hj,bnjhv->bnhkv', kc, zeta, vc)
    chunk_decay = jnp.exp(log_g * C)

    def step(state, kv_n):
        return state * chunk_decay[None, :, None, None] + kv_n, state

    _, prev = lax.scan(step, jnp.zeros((B, H, d, d), jnp.float32), kv_chunk.transpose(1, 0, 2, 3, 4))
    prev = prev.transpose(1, 0, 2, 3, 4)
    xi = jnp.exp(log_g[:, None] * (idx + 1.0))
    y_cross = jnp.einsum('bnihk,bnhkv,hi->bnihv', qc, prev, xi)

    y = (y_inner + y_cross).reshape(B, S, H, d)
    mu = jnp.mean(y, axis=-1, keepdims=True)
    var = jnp.mean(jnp.square(y - mu), axis=-1, keepdims=True)
    yn = ((y - mu) * lax.rsqrt(var + EPS)).reshape(B, S, RET_WIDTH) * g_ret_norm.astype(jnp.float32)
    return (jax.nn.silu(gate.astype(jnp.float32)) * yn).astype(gate.dtype)

def peer(h, w_query, sub_keys, expert_u, expert_v):
    B, S, D = h.shape
    T = B * S
    K = PEER_TOPK
    xt = h.reshape(T, D)
    q = (xt @ w_query).reshape(T, PEER_HEADS, 2, PEER_HALF)
    s = jnp.einsum('thpd,pkd->thpk', q, sub_keys).astype(jnp.float32)
    s_top, i_top = lax.top_k(s, K)
    cand = (s_top[:, :, 0, :, None] + s_top[:, :, 1, None, :]).reshape(T, PEER_HEADS, K * K)
    cand_idx = (i_top[:, :, 0, :, None] * PEER_N_KEYS + i_top[:, :, 1, None, :]).reshape(T, PEER_HEADS, K * K)
    best, pos = lax.top_k(cand, K)
    eidx = jnp.take_along_axis(cand_idx, pos, axis=-1)
    g = jax.nn.softmax(best, axis=-1)

    nb = T // PEER_TOKEN_BLOCK

    def one_block(args):
        xb, ib, gb = args
        u = expert_u[ib]
        a = jax.nn.gelu(jnp.einsum('thkd,td->thk', u, xb).astype(jnp.float32), approximate=False)
        w = (gb * a).astype(expert_v.dtype)
        return jnp.einsum('thk,thkd->td', w, expert_v[ib])

    out = lax.map(one_block, (xt.reshape(nb, PEER_TOKEN_BLOCK, D),
                              eidx.reshape(nb, PEER_TOKEN_BLOCK, PEER_HEADS, K),
                              g.reshape(nb, PEER_TOKEN_BLOCK, PEER_HEADS, K)))
    return out.reshape(B, S, D)

def first_inputs(seed: int = 0) -> dict:
    key = jax.random.key(seed)
    ks = jax.random.split(key, 20)
    L, D = DEPTH, D_MODEL
    nrm = lambda k, shape, scale: jax.random.normal(k, shape, jnp.float32) * scale
    gain = lambda k, shape: 1.0 + 0.02 * jax.random.normal(k, shape, jnp.float32)
    return {
        "x": nrm(ks[0], (BATCH, SEQ, D), 1.0),
        "c": nrm(ks[1], (BATCH, D), 1.0),
        "positions": jnp.broadcast_to(jnp.arange(SEQ, dtype=jnp.int32), (BATCH, SEQ)),
        "w_ada": nrm(ks[2], (L, D, 6 * D), D ** -0.5),
        "b_ada": nrm(ks[3], (L, 6 * D), 0.01),
        "g_norm1": gain(ks[4], (L, D)),
        "w_in": nrm(ks[5], (L, D, IN_COLS), D ** -0.5),
        "g_q_norm": gain(ks[6], (L, MLA_Q_RANK)),
        "w_uq": nrm(ks[7], (L, MLA_Q_RANK, MLA_HEADS * MLA_QK_DIM), MLA_Q_RANK ** -0.5),
        "g_kv_norm": gain(ks[8], (L, MLA_KV_RANK)),
        "w_ukv": nrm(ks[9], (L, MLA_KV_RANK, MLA_HEADS * (MLA_QK_NOPE + MLA_V_DIM)), MLA_KV_RANK ** -0.5),
        "g_ret_norm": gain(ks[10], (L, RET_WIDTH)),
        "w_out": nrm(ks[11], (L, MLA_WIDTH + RET_WIDTH, D), (MLA_WIDTH + RET_WIDTH) ** -0.5),
        "g_norm2": gain(ks[12], (L, D)),
        "w_query": nrm(ks[13], (L, D, PEER_HEADS * PEER_KEY_DIM), D ** -0.5),
        "sub_keys": nrm(ks[14], (L, 2, PEER_N_KEYS, PEER_HALF), PEER_HALF ** -0.5),
        "expert_u": nrm(ks[15], (L, PEER_N_EXPERTS, D), D ** -0.5),
        "expert_v": nrm(ks[16], (L, PEER_N_EXPERTS, D), 0.5),
        "g_final": gain(ks[17], (D,)),
    }

def first_block(x, c, positions, w_ada, b_ada, g_norm1, w_in, g_q_norm, w_uq, g_kv_norm, w_ukv,
              g_ret_norm, w_out, g_norm2, w_query, sub_keys, expert_u, expert_v, g_final):
    offs = np.cumsum(IN_SPLITS)[:-1].tolist()
    for l in range(DEPTH):
        mod = jax.nn.silu(c) @ w_ada[l] + b_ada[l]
        sh1, sc1, gt1, sh2, sc2, gt2 = [m[:, None, :] for m in jnp.split(mod, 6, axis=-1)]

        h = rms_norm(x, g_norm1[l]) * (1.0 + sc1) + sh1
        proj = h @ w_in[l]
        q_lat, kv_lat, k_rope, rq, rk, rv, rg = jnp.split(proj, offs, axis=-1)
        y_mla = mla_group(q_lat, kv_lat, k_rope, positions, g_q_norm[l], w_uq[l], g_kv_norm[l], w_ukv[l])
        y_ret = retention_group(rq, rk, rv, rg, positions, g_ret_norm[l])
        mixed = jnp.concatenate([y_mla.astype(x.dtype), y_ret.astype(x.dtype)], axis=-1) @ w_out[l]
        x = x + gt1 * mixed

        h2 = rms_norm(x, g_norm2[l]) * (1.0 + sc2) + sh2
        x = x + gt2 * peer(h2, w_query[l], sub_keys[l], expert_u[l], expert_v[l]).astype(x.dtype)
    return rms_norm(x, g_final)


D_MIX_2 = D_MODEL
DA_HEADS = 4
DA_HEAD_DIM = 64
DA_VAL_DIM = 2 * DA_HEAD_DIM
DA_QK = DA_HEADS * 2 * DA_HEAD_DIM
DA_WIDTH = DA_HEADS * DA_VAL_DIM
ML_HEADS = 4
ML_HEAD_DIM = (D_MIX_2 - DA_WIDTH) // ML_HEADS
ML_WIDTH = ML_HEADS * ML_HEAD_DIM
ML_CONV = 4
ML_CHUNK = 64
IN_SPLITS_2 = (DA_QK, DA_QK, DA_WIDTH, ML_WIDTH, ML_WIDTH, ML_WIDTH, ML_WIDTH, ML_HEADS, ML_HEADS)
N_IN = sum(IN_SPLITS_2)
MEM_LEN = 256
X_HEADS = 4
X_HEAD_DIM = D_MODEL // X_HEADS
N_GROUPS = 4
EXPERTS_PER_GROUP = 8
N_EXPERTS = N_GROUPS * EXPERTS_PER_GROUP
TOP_K = 2
D_EXPERT = 512
MOE_BLOCK = 128
Q_BLOCK = 128


def rms_norm_2(x, g):
    xf = x.astype(jnp.float32)
    y = xf * lax.rsqrt(jnp.mean(xf * xf, axis=-1, keepdims=True) + EPS)
    return (y * g.astype(jnp.float32)).astype(x.dtype)

def rotary(t, pos):
    d = t.shape[-1]
    inv_freq = ROPE_THETA ** (-jnp.arange(0, d, 2, dtype=jnp.float32) / d)
    ang = pos.astype(jnp.float32)[:, None] * inv_freq[None, :]
    cos = jnp.cos(ang).astype(t.dtype)
    sin = jnp.sin(ang).astype(t.dtype)
    t1, t2 = t[..., : d // 2], t[..., d // 2:]
    return jnp.concatenate([t1 * cos - t2 * sin, t2 * cos + t1 * sin], axis=-1)

def diff_attention(q, k, v, lam, subln_g, lam_init):
    bsz, seq = q.shape[0], q.shape[1]
    pos = jnp.arange(seq)
    q = rotary(q.transpose(0, 2, 3, 1, 4), pos) * (DA_HEAD_DIM ** -0.5)
    k = rotary(k.transpose(0, 2, 3, 1, 4), pos)
    v = v.transpose(0, 2, 1, 3)
    n_blk = seq // Q_BLOCK
    q_blocks = q.reshape(bsz, DA_HEADS, 2, n_blk, Q_BLOCK, DA_HEAD_DIM).transpose(3, 0, 1, 2, 4, 5)
    k_pos = jnp.arange(seq)

    def one_block(args):
        q_blk, start = args
        s = jnp.einsum('bhmqd,bhmkd->bhmqk', q_blk, k).astype(jnp.float32)
        q_pos = start + jnp.arange(Q_BLOCK)
        causal = k_pos[None, :] <= q_pos[:, None]
        p = jax.nn.softmax(jnp.where(causal, s, -jnp.inf), axis=-1)
        a = p[:, :, 0] - lam * p[:, :, 1]
        return jnp.einsum('bhqk,bhkd->bhqd', a.astype(v.dtype), v)

    o = lax.map(one_block, (q_blocks, jnp.arange(n_blk) * Q_BLOCK))
    o = o.transpose(1, 0, 3, 2, 4).reshape(bsz, seq, DA_HEADS, DA_VAL_DIM)
    o = rms_norm_2(o, subln_g) * (1.0 - lam_init)
    return o.reshape(bsz, seq, DA_WIDTH)

def causal_depthwise_conv(u, w, b):
    c = u.shape[-1]
    y = lax.conv_general_dilated(u, w.astype(u.dtype), window_strides=(1,),
                                 padding=[(ML_CONV - 1, 0)],
                                 dimension_numbers=('NWC', 'WIO', 'NWC'),
                                 feature_group_count=c)
    return y + b.astype(u.dtype)

def mlstm_chunkwise(q, k, v, o_pre, i_pre, f_pre, norm_g):
    f32 = jnp.float32
    bsz, seq = q.shape[0], q.shape[1]
    n_ch = seq // ML_CHUNK

    def heads(t):
        return t.astype(f32).reshape(bsz, n_ch, ML_CHUNK, ML_HEADS, ML_HEAD_DIM).transpose(1, 0, 3, 2, 4)

    def gates(t):
        return t.astype(f32).reshape(bsz, n_ch, ML_CHUNK, ML_HEADS).transpose(1, 0, 3, 2)

    qc, kc, vc = heads(q), heads(k) * (ML_HEAD_DIM ** -0.5), heads(v)
    ic = gates(i_pre)
    lfc = jax.nn.log_sigmoid(gates(f_pre))
    tri = jnp.tril(jnp.ones((ML_CHUNK, ML_CHUNK), dtype=bool))

    def step(carry, xs):
        c_mat, n_vec, m_prev = carry
        qj, ks, vs, ig, lf = xs
        a = jnp.cumsum(lf, axis=-1)
        log_d = jnp.where(tri, a[..., :, None] - a[..., None, :] + ig[..., None, :], -jnp.inf)
        log_inter = a + m_prev[..., None]
        m_row = jnp.maximum(log_inter, jnp.max(log_d, axis=-1))
        w_intra = jnp.exp(log_d - m_row[..., None])
        w_inter = jnp.exp(log_inter - m_row)
        s = jnp.einsum('bhjd,bhsd->bhjs', qj, ks) * w_intra
        num = (w_inter[..., None] * jnp.einsum('bhjd,bhde->bhje', qj, c_mat)
               + jnp.einsum('bhjs,bhse->bhje', s, vs))
        den = w_inter * jnp.einsum('bhjd,bhd->bhj', qj, n_vec) + jnp.sum(s, axis=-1)
        h = num / jnp.maximum(jnp.abs(den), jnp.exp(-m_row))[..., None]
        g = a[..., -1]
        log_w = g[..., None] - a + ig
        m_new = jnp.maximum(g + m_prev, jnp.max(log_w, axis=-1))
        w_state = jnp.exp(log_w - m_new[..., None])
        decay = jnp.exp(g + m_prev - m_new)
        c_new = decay[..., None, None] * c_mat + jnp.einsum('bhs,bhsd,bhse->bhde', w_state, ks, vs)
        n_new = decay[..., None] * n_vec + jnp.einsum('bhs,bhsd->bhd', w_state, ks)
        return (c_new, n_new, m_new), h

    init = (jnp.zeros((bsz, ML_HEADS, ML_HEAD_DIM, ML_HEAD_DIM), f32),
            jnp.zeros((bsz, ML_HEADS, ML_HEAD_DIM), f32),
            jnp.zeros((bsz, ML_HEADS), f32))
    _, h = lax.scan(step, init, (qc, kc, vc, ic, lfc))
    h = h.transpose(1, 0, 3, 2, 4).reshape(bsz, seq, ML_HEADS, ML_HEAD_DIM)
    mu = jnp.mean(h, axis=-1, keepdims=True)
    var = jnp.mean(jnp.square(h - mu), axis=-1, keepdims=True)
    hn = (h - mu) * lax.rsqrt(var + EPS) * norm_g.astype(f32).reshape(ML_HEADS, ML_HEAD_DIM)
    o = jax.nn.sigmoid(o_pre.astype(f32)).reshape(bsz, seq, ML_HEADS, ML_HEAD_DIM)
    return (o * hn).reshape(bsz, seq, ML_WIDTH).astype(q.dtype)

def hybrid_mixer(h, w_in, w_out, da_lambda, da_subln_g, lam_init, ml_conv_w, ml_conv_b, ml_gate_b, ml_norm_g):
    bsz, seq = h.shape[0], h.shape[1]
    proj = h @ w_in
    dq, dk, dv, mq, mk, mv, mo, mi, mf = jnp.split(proj, np.cumsum(IN_SPLITS_2)[:-1].tolist(), axis=-1)
    lv = da_lambda.astype(jnp.float32)
    lam = jnp.exp(jnp.sum(lv[0] * lv[1])) - jnp.exp(jnp.sum(lv[2] * lv[3])) + lam_init
    y_da = diff_attention(dq.reshape(bsz, seq, DA_HEADS, 2, DA_HEAD_DIM),
                          dk.reshape(bsz, seq, DA_HEADS, 2, DA_HEAD_DIM),
                          dv.reshape(bsz, seq, DA_HEADS, DA_VAL_DIM), lam, da_subln_g, lam_init)
    qk = jax.nn.silu(causal_depthwise_conv(jnp.concatenate([mq, mk], axis=-1), ml_conv_w, ml_conv_b))
    mq_c, mk_c = jnp.split(qk, 2, axis=-1)
    y_ml = mlstm_chunkwise(mq_c, mk_c, mv, mo,
                           mi + ml_gate_b[0].astype(mi.dtype), mf + ml_gate_b[1].astype(mf.dtype), ml_norm_g)
    return jnp.concatenate([y_da, y_ml], axis=-1) @ w_out

def cross_attention(h, mem_n, wq, wk, wv, wo):
    bsz, seq = h.shape[0], h.shape[1]
    m_len = mem_n.shape[1]
    q = (h @ wq).reshape(bsz, seq, X_HEADS, X_HEAD_DIM)
    k = (mem_n @ wk).reshape(bsz, m_len, X_HEADS, X_HEAD_DIM)
    v = (mem_n @ wv).reshape(bsz, m_len, X_HEADS, X_HEAD_DIM)
    s = jnp.einsum('bqhd,bkhd->bhqk', q, k).astype(jnp.float32) * (X_HEAD_DIM ** -0.5)
    p = jax.nn.softmax(s, axis=-1)
    o = jnp.einsum('bhqk,bkhd->bqhd', p.astype(v.dtype), v).reshape(bsz, seq, D_MODEL)
    return o @ wo

def hierarchical_moe(h, w_rg, b_rg, w_re, b_re, w1, w3, w2):
    f32 = jnp.float32
    bsz, seq, d = h.shape
    n_tok = bsz * seq
    xt = h.reshape(n_tok, d)
    g_prob = jax.nn.softmax((xt @ w_rg).astype(f32) + b_rg.astype(f32), axis=-1)
    g_idx = jnp.argmax(g_prob, axis=-1).astype(jnp.int32)
    g_w = jnp.take_along_axis(g_prob, g_idx[:, None], axis=-1)[:, 0]
    e_logits = ((xt @ w_re).astype(f32) + b_re.astype(f32)).reshape(n_tok, N_GROUPS, EXPERTS_PER_GROUP)
    e_logits = jnp.take_along_axis(e_logits, g_idx[:, None, None], axis=1)[:, 0]
    top_p, top_i = lax.top_k(jax.nn.softmax(e_logits, axis=-1), TOP_K)
    comb = g_w[:, None] * top_p / jnp.sum(top_p, axis=-1, keepdims=True)
    expert = g_idx[:, None] * EXPERTS_PER_GROUP + top_i.astype(jnp.int32)
    n_asg = n_tok * TOP_K
    flat_e = expert.reshape(-1)
    flat_tok = jnp.repeat(jnp.arange(n_tok, dtype=jnp.int32), TOP_K)
    flat_w = comb.reshape(-1)
    order = jnp.argsort(flat_e)
    sorted_e, sorted_tok, sorted_w = flat_e[order], flat_tok[order], flat_w[order]
    counts = jnp.bincount(flat_e, length=N_EXPERTS).astype(jnp.int32)
    padded = (counts + MOE_BLOCK - 1) // MOE_BLOCK * MOE_BLOCK
    starts = jnp.cumsum(counts) - counts
    pad_ends = jnp.cumsum(padded)
    pad_starts = pad_ends - padded
    dest = pad_starts[sorted_e] + jnp.arange(n_asg, dtype=jnp.int32) - starts[sorted_e]
    n_blocks = -(-n_asg // MOE_BLOCK) + N_EXPERTS
    n_rows = n_blocks * MOE_BLOCK
    buf_tok = jnp.full((n_rows,), n_tok, jnp.int32).at[dest].set(sorted_tok)
    buf_w = jnp.zeros((n_rows,), f32).at[dest].set(sorted_w)
    block_e = jnp.clip(jnp.searchsorted(pad_ends, jnp.arange(n_blocks, dtype=jnp.int32) * MOE_BLOCK, side='right'),
                       0, N_EXPERTS - 1).astype(jnp.int32)
    xpad = jnp.concatenate([xt, jnp.zeros((1, d), xt.dtype)], axis=0)
    xb = xpad[buf_tok].reshape(n_blocks, MOE_BLOCK, d)

    def run_block(args):
        x_blk, e = args
        return (jax.nn.silu(x_blk @ w1[e]) * (x_blk @ w3[e])) @ w2[e]

    yb = lax.map(run_block, (xb, block_e)).reshape(n_rows, d)
    yb = yb * buf_w[:, None].astype(yb.dtype)
    out = jnp.zeros((n_tok + 1, d), yb.dtype).at[buf_tok].add(yb)[:n_tok]
    return out.reshape(bsz, seq, d)

def second_inputs(seed: int = 0) -> dict:
    key = jax.random.key(seed)
    ks = jax.random.split(key, 32)
    f32 = jnp.float32
    L = DEPTH

    def nrm(k, shape, scale):
        return jax.random.normal(k, shape, f32) * scale

    def gain(k, shape):
        return 1.0 + 0.02 * jax.random.normal(k, shape, f32)

    f_bias = jnp.linspace(3.0, 6.0, ML_HEADS, dtype=f32)
    ml_gate_b = jnp.stack([nrm(ks[9], (L, ML_HEADS), 0.1),
                           f_bias[None, :] + nrm(ks[10], (L, ML_HEADS), 0.1)], axis=1)
    return {
        'x': nrm(ks[0], (BATCH, SEQ, D_MODEL), 1.0),
        'mem': nrm(ks[1], (BATCH, MEM_LEN, D_MODEL), 1.0),
        'norm_mix_g': gain(ks[2], (L, D_MODEL)),
        'w_in': nrm(ks[3], (L, D_MODEL, N_IN), D_MODEL ** -0.5),
        'w_out': nrm(ks[4], (L, D_MIX_2, D_MODEL), D_MIX_2 ** -0.5),
        'da_lambda': nrm(ks[5], (L, 4, DA_HEAD_DIM), 0.1),
        'da_subln_g': gain(ks[6], (L, DA_VAL_DIM)),
        'ml_conv_w': nrm(ks[7], (L, ML_CONV, 1, 2 * ML_WIDTH), ML_CONV ** -0.5),
        'ml_conv_b': nrm(ks[8], (L, 2 * ML_WIDTH), 0.02),
        'ml_gate_b': ml_gate_b,
        'ml_norm_g': gain(ks[11], (L, ML_WIDTH)),
        'norm_x_g': gain(ks[12], (L, D_MODEL)),
        'norm_mem_g': gain(ks[13], (L, D_MODEL)),
        'w_xq': nrm(ks[14], (L, D_MODEL, D_MODEL), D_MODEL ** -0.5),
        'w_xk': nrm(ks[15], (L, D_MODEL, D_MODEL), D_MODEL ** -0.5),
        'w_xv': nrm(ks[16], (L, D_MODEL, D_MODEL), D_MODEL ** -0.5),
        'w_xo': nrm(ks[17], (L, D_MODEL, D_MODEL), D_MODEL ** -0.5),
        'norm_ffn_g': gain(ks[18], (L, D_MODEL)),
        'w_router_group': nrm(ks[19], (L, D_MODEL, N_GROUPS), D_MODEL ** -0.5),
        'b_router_group': nrm(ks[20], (L, N_GROUPS), 0.01),
        'w_router_expert': nrm(ks[21], (L, D_MODEL, N_EXPERTS), D_MODEL ** -0.5),
        'b_router_expert': nrm(ks[22], (L, N_EXPERTS), 0.01),
        'w1': nrm(ks[23], (L, N_EXPERTS, D_MODEL, D_EXPERT), D_MODEL ** -0.5),
        'w3': nrm(ks[24], (L, N_EXPERTS, D_MODEL, D_EXPERT), D_MODEL ** -0.5),
        'w2': nrm(ks[25], (L, N_EXPERTS, D_EXPERT, D_MODEL), D_EXPERT ** -0.5),
        'norm_final_g': gain(ks[26], (D_MODEL,)),
    }

def second_block(x, mem, norm_mix_g, w_in, w_out, da_lambda, da_subln_g, ml_conv_w, ml_conv_b, ml_gate_b,
              ml_norm_g, norm_x_g, norm_mem_g, w_xq, w_xk, w_xv, w_xo, norm_ffn_g, w_router_group,
              b_router_group, w_router_expert, b_router_expert, w1, w3, w2, norm_final_g):
    for l in range(DEPTH):
        lam_init = 0.8 - 0.6 * math.exp(-0.3 * l)
        x = x + hybrid_mixer(rms_norm_2(x, norm_mix_g[l]), w_in[l], w_out[l], da_lambda[l], da_subln_g[l],
                             lam_init, ml_conv_w[l], ml_conv_b[l], ml_gate_b[l], ml_norm_g[l])
        x = x + cross_attention(rms_norm_2(x, norm_x_g[l]), rms_norm_2(mem, norm_mem_g[l]),
                                w_xq[l], w_xk[l], w_xv[l], w_xo[l])
        x = x + hierarchical_moe(rms_norm_2(x, norm_ffn_g[l]), w_router_group[l], b_router_group[l],
                                 w_router_expert[l], b_router_expert[l], w1[l], w3[l], w2[l])
    return rms_norm_2(x, norm_final_g)


def setup_inputs(seed=0):
    out = dict(first_inputs(seed))
    for name, value in second_inputs(seed + 1).items():
        if name != "x":
            out[name + "_2"] = value
    return out


def reference(
    x, c, positions, w_ada, b_ada, g_norm1, w_in, g_q_norm, w_uq, g_kv_norm, w_ukv, g_ret_norm,
    w_out, g_norm2, w_query, sub_keys, expert_u, expert_v, g_final, mem_2, norm_mix_g_2, w_in_2,
    w_out_2, da_lambda_2, da_subln_g_2, ml_conv_w_2, ml_conv_b_2, ml_gate_b_2, ml_norm_g_2,
    norm_x_g_2, norm_mem_g_2, w_xq_2, w_xk_2, w_xv_2, w_xo_2, norm_ffn_g_2, w_router_group_2,
    b_router_group_2, w_router_expert_2, b_router_expert_2, w1_2, w3_2, w2_2, norm_final_g_2,
):
    x = first_block(
        x, c, positions, w_ada, b_ada, g_norm1, w_in, g_q_norm, w_uq, g_kv_norm, w_ukv,
        g_ret_norm, w_out, g_norm2, w_query, sub_keys, expert_u, expert_v, g_final,
    )
    return second_block(
        x, mem_2, norm_mix_g_2, w_in_2, w_out_2, da_lambda_2, da_subln_g_2, ml_conv_w_2,
        ml_conv_b_2, ml_gate_b_2, ml_norm_g_2, norm_x_g_2, norm_mem_g_2, w_xq_2, w_xk_2, w_xv_2,
        w_xo_2, norm_ffn_g_2, w_router_group_2, b_router_group_2, w_router_expert_2,
        b_router_expert_2, w1_2, w3_2, w2_2, norm_final_g_2,
    )


_drawn_inputs = setup_inputs


def setup_inputs(seed=0):
    import zlib

    import numpy as np

    out = dict(_drawn_inputs(seed))
    spreads = {}
    factors = {'g_q_norm': 4.183,
     'da_lambda_2': 3.204,
     'da_subln_g_2': 3.056,
     'ml_conv_b_2': 3.594,
     'ml_norm_g_2': 4.397,
     'norm_x_g_2': 7.05,
     'norm_mem_g_2': 7.979,
     'b_router_group_2': 53.416,
     'b_router_expert_2': 44.504,
     'norm_final_g_2': 7.564,
     'norm_ffn_g_2': 8.0}
    for name, (base, spread) in spreads.items():
        noise = np.random.default_rng([zlib.crc32(name.encode()), seed]).standard_normal(out[name].shape)
        drawn = base * np.exp(spread * noise) if base else spread * noise
        out[name] = jnp.asarray(drawn.astype(out[name].dtype))
    for name, factor in factors.items():
        out[name] = (out[name] * factor).astype(out[name].dtype)
    return out
```

```python
from contextlib import ExitStack, contextmanager

import numpy as np

import concourse.bass as bass
from concourse import mybir

F32 = mybir.dt.float32
BF16 = mybir.dt.bfloat16
I32 = mybir.dt.int32
U32 = mybir.dt.uint32
ALU = mybir.AluOpType
ACT = mybir.ActivationFunctionType
AX_X = mybir.AxisListType.X

P = 128
T = 512
TT = T // P
D = 1024
DC = D // P
EPS = 1e-6
THETA = 10000.0
NEG = -1e30
BANK = 512

HEADS = 8
NOPE, ROPE, VD = 64, 32, 64
QK = NOPE + ROPE
Q_RANK, KV_RANK = 256, 128
C_QL, C_KV, C_KR = 0, 256, 384
C_RQ, C_RK, C_RV, C_RG = 416, 928, 1440, 1952
IN_COLS = 2464
RD = 64
HALF = 32
PH, PK, TOPK = 8, 128, 16

DA_H, DV_W = 4, 128
ML_H, ML_D = 4, 128
CONV = 4
MEM = 256
X_H, X_D = 4, 256
NG, EG = 4, 8
NE = NG * EG
FE = 512
FC = FE // P
CAP = T

RING = 4


class InOrder:

    def __init__(self, eng, done):
        self.eng, self.done, self.count = eng, done, 0

    def __call__(self, ins):
        self.count += 1
        ins.then_inc(self.done, 1)
        self.eng.wait_ge(self.done, self.count)


NAMED = {}


def fresh(name):
    NAMED[name] = NAMED.get(name, 0) + 1
    return f"{name}_{NAMED[name]}"


PAST = []


@contextmanager
def stage(nc, names):
    sems = {n: nc.alloc_semaphore(fresh(n)) for n in names.split()}
    if PAST:
        nc.clear_and_free_semaphores(list(PAST))
    PAST[:] = sems.values()
    with nc.Block() as block:
        yield block, sems


class Core:

    def __init__(self, nc, ctx, a):
        self.nc, self.a = nc, a
        self.bank = [ctx.enter_context(nc.psum_tensor(f"bank{i}", [P, BANK], F32)) for i in range(8)]

        def sb(name, shape, dt=F32):
            return ctx.enter_context(nc.sbuf_tensor(name, shape, dt))

        self.ident = sb("ident", [P, P])
        self.ones = sb("ones", [P, P])
        self.causal_neg = sb("causal_neg", [P, P])
        self.causal_t = sb("causal_t", [P, P])
        self.iota_p = sb("iota_p", [P, P])
        self.diff = sb("diff", [P, T])
        self.eps = sb("eps", [P, 1])
        self.inv_freq = sb("inv_freq", [P, HALF])
        self.cos = sb("cos", [P, 2, TT, HALF])
        self.sin = sb("sin", [P, 2, TT, HALF])
        self.x = sb("x_res", [P, TT, D])
        self.ht = sb("ht", [P, DC, T])
        self.ring = [sb(f"ring{i}", [P, DC, BANK]) for i in range(RING)]
        self.ring_loaded = [nc.alloc_semaphore(f"ring_loaded{i}") for i in range(RING)]
        self.dense = nc.alloc_semaphore("dense")
        self.units = []
        self.through = []
        self.loads = 0
        self.taken = 0

    def plan(self, w, c0, cols, groups=TT):
        rows = w.shape[0]
        src = w.rearrange("(k p) n -> p k n", p=P)[:, :, c0:c0 + cols]
        self.units.append((src, rows // P, cols))
        self.through.append((self.through[-1] if self.through else 0) + groups)

    def prefetch(self, sp, upto):
        while self.loads < min(upto, len(self.units)):
            u = self.loads
            src, k, cols = self.units[u]
            if u >= RING:
                sp.wait_ge(self.dense, self.through[u - RING])
            sp.dma_start(self.ring[u % RING][:, 0:k, 0:cols], src).then_inc(self.ring_loaded[u % RING], 16)
            self.loads += 1

    def before(self, u):
        return self.through[u - 1] if u else 0

    def weights(self, pe, u):
        pe.wait_ge(self.ring_loaded[u % RING], 16 * (u // RING + 1))
        return self.ring[u % RING]


ADA = 1024
ADA_SLOTS = 4


def load_ada(sp, a, ada_in, ada_loaded, ada_used, group):
    for k in range(DC):
        n = DC * group + k
        if n >= ADA_SLOTS:
            sp.wait_ge(ada_used, n - ADA_SLOTS + 1)
        sp.dma_start(ada_in[:, n % ADA_SLOTS, :],
                     a["w_ada"][0, k * P:(k + 1) * P, group * ADA:(group + 1) * ADA]
                     ).then_inc(ada_loaded[n % ADA_SLOTS], 16)


def sum_ada(dve, c_act, ada_in, ada_acc, ada_loaded, ada_used, group):
    acc = ada_acc[:, group * ADA:(group + 1) * ADA]
    for k in range(DC):
        n = DC * group + k
        dve.wait_ge(ada_loaded[n % ADA_SLOTS], 16 * (n // ADA_SLOTS + 1))
        if k == 0:
            dve.tensor_scalar(acc, ada_in[:, n % ADA_SLOTS, :], c_act[:, k:k + 1], None,
                              ALU.mult).then_inc(ada_used, 1)
        else:
            dve.wait_ge(ada_used, n)
            dve.scalar_tensor_tensor(acc, ada_in[:, n % ADA_SLOTS, :], c_act[:, k:k + 1], acc,
                                     ALU.mult, ALU.add).then_inc(ada_used, 1)


def prelude(g, proj, ada_in, ada_acc, c_act, col, ada_loaded, ada_used):
    nc, a = g.nc, g.a
    with ExitStack() as ctx:
        def sb(name, shape, dt=F32):
            return ctx.enter_context(nc.sbuf_tensor(name, shape, dt))
        pos_i = sb("pos_i", [P, TT], I32)
        pos_f = sb("pos_f", [P, 2, TT])
        ang = sb("ang", [P, 2, TT, HALF])
        turn = sb("turn", [P, 2, TT, HALF])
        turn_i = sb("turn_i", [P, 2, TT, HALF], I32)
        over = sb("over", [P, 2, TT, HALF])
        iota_i = sb("iota_i", [P, T], I32)
        c_in = sb("c_in", [P, DC])
        bias = sb("bias", [P, 16])
        gain = sb("gain", [P, DC])
        ss = sb("ss", [P, TT])
        rstd = sb("rstd", [P, TT])
        rms = sb("rms", [P, TT])
        xn = proj[:, :, 0:D]
        with stage(nc, "a_x a_small a_pool a_consts a_dve a_c a_trig a_sq a_rstd a_root a_xn a_xt a_ev a_cols a_col_ready a_ht") as (block, s):
            @block.sync
            def _(sp):
                sp.dma_start(c_in[:, :], a["c"].rearrange("o (k p) -> p (o k)", p=P)).then_inc(s["a_c"], 16)
                sp.dma_start(g.x[:, :, :], a["x"][0].rearrange("(i p) d -> p i d", p=P)).then_inc(s["a_x"], 16)
                load_ada(sp, a, ada_in, ada_loaded, ada_used, 0)
                load_ada(sp, a, ada_in, ada_loaded, ada_used, 1)
                g.prefetch(sp, RING)

            @block.gpsimd
            def _(pool):
                pool.dma_start(pos_i[:, :], a["positions"][0].rearrange("(i p) -> p i", p=P)).then_inc(s["a_small"], 16)
                pool.dma_start(bias[:, :], a["b_ada"][0, 0:2 * D].rearrange("(j p) -> p j", p=P)).then_inc(s["a_small"], 16)
                pool.dma_start(gain[:, :], a["g_norm1"][0].rearrange("(k p) -> p k", p=P)).then_inc(s["a_small"], 16)
                step = InOrder(pool, s["a_pool"])
                for i in range(HALF):
                    f = float(np.float32(THETA) ** np.float32(-2 * i / 64))
                    pool.memset(g.inv_freq[:, i:i + 1], f)
                pool.memset(g.eps[:, :], EPS)
                step(pool.memset(g.ones[:, :], 1.0))
                step(pool.memset(g.ident[:, :], 0.0))
                step(pool.affine_select(out=g.ident[:, :], in_=g.ident[:, :], compare_op=ALU.not_equal,
                                        fill=1.0, base=0, pattern=[[-1, P]], channel_multiplier=1))
                step(pool.memset(g.causal_neg[:, :], 0.0))
                step(pool.affine_select(out=g.causal_neg[:, :], in_=g.causal_neg[:, :], compare_op=ALU.is_ge,
                                        fill=NEG, base=0, pattern=[[-1, P]], channel_multiplier=1))
                step(pool.affine_select(out=g.causal_t[:, :], in_=g.ones[:, :], compare_op=ALU.is_ge,
                                        fill=0.0, base=0, pattern=[[1, P]], channel_multiplier=-1))
                step(pool.iota(iota_i[:, :], pattern=[[1, T]], base=0, channel_multiplier=0))
                step(pool.tensor_copy(g.iota_p[:, :], iota_i[:, 0:P]))
                step(pool.iota(iota_i[:, :], pattern=[[1, T]], base=0, channel_multiplier=-1))
                step(pool.tensor_copy(g.diff[:, :], iota_i[:, :]))
                step(pool.iota(iota_i[:, 0:TT], pattern=[[P, TT]], base=0, channel_multiplier=1))
                step(pool.tensor_copy(pos_f[:, 1, :], iota_i[:, 0:TT]))
                pool.wait_ge(s["a_small"], 48)
                pool.tensor_copy(pos_f[:, 0, :], pos_i[:, :]).then_inc(s["a_consts"], 1)

            @block.vector
            def _(dve):
                step = InOrder(dve, s["a_dve"])
                dve.wait_ge(s["a_consts"], 1)
                two_pi = 2 * np.pi
                c1 = 6.28125
                c2 = float(np.float32(two_pi - c1))
                c3 = float(two_pi - c1 - np.float64(np.float32(two_pi - c1)))
                pi = float(np.nextafter(np.float32(np.pi), np.float32(0)))

                def wrap(v):
                    step(dve.tensor_scalar(over[:], v, pi, two_pi, ALU.is_gt, ALU.mult))
                    step(dve.tensor_tensor(v, v, over[:], ALU.subtract))
                    step(dve.tensor_scalar(over[:], v, -pi, two_pi, ALU.is_lt, ALU.mult))
                    step(dve.tensor_tensor(v, v, over[:], ALU.add))
                    step(dve.tensor_scalar(v, v, pi, -pi, ALU.min, ALU.max))

                step(dve.tensor_tensor(ang[:], pos_f[:].unsqueeze(3).to_broadcast([P, 2, TT, HALF]),
                                       g.inv_freq[:].unsqueeze(1).unsqueeze(1).to_broadcast([P, 2, TT, HALF]), ALU.mult))
                step(dve.tensor_scalar(turn[:], ang[:], 1.0 / two_pi, None, ALU.mult))
                step(dve.tensor_copy(turn_i[:], turn[:]))
                step(dve.tensor_copy(turn[:], turn_i[:]))
                for c in (c1, c2, c3):
                    step(dve.scalar_tensor_tensor(ang[:], turn[:], -c, ang[:], ALU.mult, ALU.add))
                wrap(ang[:])
                step(dve.tensor_scalar(turn[:], ang[:], float(np.pi / 2), None, ALU.add))
                wrap(turn[:])
                dve.tensor_copy(over[:], turn[:]).then_inc(s["a_trig"], 1)
                dve.wait_ge(s["a_root"], 1)
                dve.reciprocal(rstd[:, :], rms[:, :]).then_inc(s["a_rstd"], 1)
                dve.wait_ge(s["a_c"], 17)
                for group in range(2):
                    sum_ada(dve, c_act, ada_in, ada_acc, ada_loaded, ada_used, group)
                dve.wait_ge(s["a_cols"], 1)
                step(dve.tensor_tensor(col[:, 0:16], g.bank[6][:, 0:16], bias[:, :], ALU.add))
                dve.scalar_tensor_tensor(col[:, 8:16], col[:, 8:16], 1.0, gain[:, :], ALU.add,
                                         ALU.mult).then_inc(s["a_col_ready"], 1)

            @block.scalar
            def _(act):
                act.wait_ge(s["a_c"], 16)
                act.activation(c_act[:, :], c_in[:, :], ACT.Silu).then_inc(s["a_c"], 1)
                act.wait_ge(s["a_x"], 16)
                for i in range(TT):
                    act.activation(xn[:, i, :], g.x[:, i, :], ACT.Square, accum_out=ss[:, i:i + 1]).then_inc(s["a_sq"], 1)
                act.wait_ge(s["a_consts"], 1)
                act.wait_ge(s["a_sq"], TT)
                act.activation(rms[:, :], ss[:, :], ACT.Sqrt, scale=1.0 / D, bias=g.eps[:, :]).then_inc(s["a_root"], 1)
                act.wait_ge(s["a_rstd"], 1)
                for i in range(TT):
                    act.activation(xn[:, i, :], g.x[:, i, :], ACT.Copy, scale=rstd[:, i:i + 1]).then_inc(s["a_xn"], 1)
                act.wait_ge(s["a_trig"], 1)
                act.activation(g.sin[:], ang[:], ACT.Sin)
                act.activation(g.cos[:], over[:], ACT.Sin)
                act.wait_ge(s["a_col_ready"], 1)
                for k in range(DC):
                    act.wait_ge(s["a_xt"], k + 1)
                    act.activation(g.ht[:, k, :], g.bank[k % 6][:, :], ACT.Identity, bias=col[:, k:k + 1],
                                   scale=col[:, 8 + k:9 + k]).then_inc(s["a_ev"], 1)

            @block.tensor
            def _(pe):
                pe.wait_ge(s["a_consts"], 1)
                pe.wait_ge(s["a_xn"], TT)

                def flip(k):
                    if k >= 6:
                        pe.wait_ge(s["a_ev"], k - 5)
                    for i in range(TT):
                        last = pe.transpose(g.bank[k % 6][:, i * P:(i + 1) * P], xn[:, i, k * P:(k + 1) * P], g.ident[:, :])
                    last.then_inc(s["a_xt"], 1)
                for k in range(6):
                    flip(k)
                pe.wait_ge(ada_used, 2 * DC)
                for j in range(16):
                    last = pe.matmul(g.bank[6][:, j:j + 1], ada_acc[:, j * P:(j + 1) * P], g.ones[:, 0:1],
                                     start=True, stop=True)
                last.then_inc(s["a_cols"], 1)
                for k in range(6, DC):
                    flip(k)


def project(g, proj, ada_in, ada_acc, c_act, col, gate_row, ada_loaded, ada_used):
    nc, a = g.nc, g.a
    units = [(c0, n) for c0, n in [(0, C_RQ)] + [(C_RQ + i * BANK, BANK) for i in range(4)]]
    with ExitStack() as ctx:
        bias = ctx.enter_context(nc.sbuf_tensor("bias2", [P, 16], F32))
        gain = ctx.enter_context(nc.sbuf_tensor("gain2", [P, DC], F32))
        brow = ctx.enter_context(nc.sbuf_tensor("brow", [P, 2, D], F32))
        with stage(nc, "b_small b_ev b_cols b_rows b_dve") as (block, s):
            @block.sync
            def _(sp):
                sp.dma_start(bias[:, :], a["b_ada"][0, 3 * D:5 * D].rearrange("(j p) -> p j", p=P)).then_inc(s["b_small"], 16)
                sp.dma_start(gain[:, :], a["g_norm2"][0].rearrange("(k p) -> p k", p=P)).then_inc(s["b_small"], 16)
                for n, c0 in enumerate((2 * D, 5 * D)):
                    sp.dma_start(brow[:, n, :], a["b_ada"][0:1, c0:c0 + D].partition_broadcast(P)).then_inc(s["b_small"], 16)
                for group in range(2, 6):
                    load_ada(sp, a, ada_in, ada_loaded, ada_used, group)
                g.prefetch(sp, 5 + RING)

            @block.tensor
            def _(pe):
                n = 0
                for u, (c0, cols) in enumerate(units):
                    w = g.weights(pe, g.taken)
                    for i in range(TT):
                        if n >= 6:
                            pe.wait_ge(s["b_ev"], n - 5)
                        for k in range(DC):
                            last = pe.matmul(g.bank[n % 6][:, 0:cols], g.ht[:, k, i * P:(i + 1) * P], w[:, k, 0:cols],
                                             start=(k == 0), stop=(k == DC - 1))
                        last.then_inc(g.dense, 1)
                        n += 1
                    g.taken += 1
                pe.wait_ge(ada_used, 6 * DC)
                for j in range(16):
                    last = pe.matmul(g.bank[6][:, j:j + 1], ada_acc[:, 3 * D + j * P:3 * D + (j + 1) * P], g.ones[:, 0:1],
                                     start=True, stop=True)
                last.then_inc(s["b_cols"], 1)
                for n, c0 in enumerate((2 * D, 2 * D + BANK, 5 * D, 5 * D + BANK)):
                    if n:
                        pe.wait_ge(s["b_rows"], 2 * n)
                    pe.matmul(g.bank[7][:, :], g.ones[:, :], ada_acc[:, c0:c0 + BANK], start=True,
                              stop=True).then_inc(s["b_rows"], 1)

            @block.scalar
            def _(act):
                n = 0
                for u, (c0, cols) in enumerate(units):
                    for i in range(TT):
                        act.wait_ge(g.dense, n + 1)
                        act.activation(proj[:, i, c0:c0 + cols], g.bank[n % 6][:, 0:cols], ACT.Copy).then_inc(s["b_ev"], 1)
                        n += 1

            @block.vector
            def _(dve):
                step = InOrder(dve, s["b_dve"])
                for group in range(2, 6):
                    sum_ada(dve, c_act, ada_in, ada_acc, ada_loaded, ada_used, group)
                dve.wait_ge(s["b_small"], 64)
                dve.wait_ge(s["b_cols"], 1)
                step(dve.tensor_tensor(col[:, 16:32], g.bank[6][:, 0:16], bias[:, :], ALU.add))
                step(dve.scalar_tensor_tensor(col[:, 24:32], col[:, 24:32], 1.0, gain[:, :], ALU.add, ALU.mult))
                for n in range(4):
                    dve.wait_ge(s["b_rows"], 2 * n + 1)
                    dve.tensor_tensor(gate_row[:, n // 2, (n % 2) * BANK:(n % 2 + 1) * BANK], g.bank[7][:, :],
                                      brow[:, n // 2, (n % 2) * BANK:(n % 2 + 1) * BANK], ALU.add).then_inc(s["b_rows"], 1)


def rotate(eng, step, x1, x2, cos, sin, tmp):
    a, b, c, d = tmp
    step(eng.tensor_tensor(a, x1, cos, ALU.mult))
    step(eng.tensor_tensor(b, x2, sin, ALU.mult))
    step(eng.tensor_tensor(c, x1, sin, ALU.mult))
    step(eng.tensor_tensor(d, x2, cos, ALU.mult))
    step(eng.tensor_tensor(x1, a, b, ALU.subtract))
    step(eng.tensor_tensor(x2, c, d, ALU.add))


def rotate_heads(eng, step, x, table, g, tmp):
    v = x.rearrange("p i (h w) -> p i h w", w=RD)
    shape = [P, TT, HEADS, HALF]
    cos = g.cos[:, table].unsqueeze(2).to_broadcast(shape)
    sin = g.sin[:, table].unsqueeze(2).to_broadcast(shape)
    rotate(eng, step, v[:, :, :, 0:HALF], v[:, :, :, HALF:RD], cos, sin, tmp)


def flip_pairs(pe, g, s, q, k, n0=0):
    for n in range(8):
        x = q if n < 4 else k
        if n >= 4:
            pe.wait_ge(s["flip_out"], n - 3)
        for i in range(TT):
            last = pe.transpose(g.bank[n % 4][:, i * P:(i + 1) * P], x[:, i, (n % 4) * P:(n % 4 + 1) * P], g.ident[:, :])
        last.then_inc(s["flipped"], 1)


def head_norm(dve, act, step, y, out, gain):
    pass


def retention(g, proj):
    nc, a = g.nc, g.a
    gamma = [1.0 - 2.0 ** (-5.0 - h) for h in range(HEADS)]
    qt, kt = g.ht[:, 0:4, :], g.ht[:, 4:8, :]
    with ExitStack() as ctx:
        def sb(name, shape, dt=F32):
            return ctx.enter_context(nc.sbuf_tensor(name, shape, dt))
        decay = sb("decay", [P, HEADS, T])
        span = sb("span", [P, T])
        y = sb("y_ret", [P, TT, BANK])
        sd = sb("sd", [P, 2, TT, T])
        gain = sb("ret_gain", [P, BANK])
        mu = sb("mu", [P, TT * HEADS])
        var = sb("var", [P, TT * HEADS])
        rms = sb("ret_rms", [P, TT * HEADS])
        rs = sb("ret_rs", [P, TT * HEADS])
        q, k, v, rg = (proj[:, :, c:c + BANK] for c in (C_RQ, C_RK, C_RV, C_RG))
        tmp = [sd[:, n // 2, 2 * (n % 2):2 * (n % 2) + 2, :].rearrange("p a (b c) -> p (a b) c", b=2).rearrange("p i (h w) -> p i h w", w=HALF)
               for n in range(4)]
        with stage(nc, "c_gain c_dve rotated span_ready exps decay_ready flipped flip_out scored weighed summed y_out sq_done root_done rs_ready gate_done") as (block, s):
            @block.sync
            def _(sp):
                sp.dma_start(gain[:, :], a["g_ret_norm"][0:1, :].partition_broadcast(P)).then_inc(s["c_gain"], 16)

            @block.vector
            def _(dve):
                step = InOrder(dve, s["c_dve"])
                dve.tensor_scalar(span[:, :], g.diff[:, :], 0.0, None, ALU.max).then_inc(s["span_ready"], 1)
                rotate_heads(dve, step, q, 0, g, tmp)
                dve.sem_inc(s["rotated"], 1)
                rotate_heads(dve, step, k, 0, g, tmp)
                dve.sem_inc(s["rotated"], 1)
                dve.wait_ge(s["decay_ready"], 1)
                for h in range(HEADS):
                    for j in range(TT):
                        n = TT * h + j
                        w = T - j * P
                        dve.wait_ge(s["scored"], n + 1)
                        if h >= 2 and j == 0:
                            dve.wait_ge(s["summed"], h - 1)
                        dve.scalar_tensor_tensor(sd[:, h % 2, j, 0:w], g.bank[n % 4][:, 0:w], RD ** -0.5,
                                                 decay[:, h, 0:w], ALU.mult, ALU.mult).then_inc(s["weighed"], 1)
                dve.wait_ge(s["y_out"], HEADS)
                yv = y[:, :, :].rearrange("p i (h w) -> p (i h) w", w=RD)
                whole = [P, TT * HEADS, RD]
                sq = q.rearrange("p i (h w) -> p i h w", w=RD)
                step(dve.tensor_reduce(mu[:, :], yv, AX_X, ALU.add))
                step(dve.tensor_scalar(mu[:, :], mu[:, :], 1.0 / RD, None, ALU.mult))
                step(dve.tensor_tensor(yv, yv, mu[:, :].unsqueeze(2).to_broadcast(whole), ALU.subtract))
                step(dve.tensor_tensor(q, y[:, :, :], y[:, :, :], ALU.mult))
                dve.tensor_reduce(var[:, :].rearrange("p (i h) -> p i h", h=HEADS), sq, AX_X, ALU.add).then_inc(s["sq_done"], 1)
                dve.wait_ge(s["root_done"], 1)
                step(dve.reciprocal(rs[:, :], rms[:, :]))
                step(dve.tensor_tensor(yv, yv, rs[:, :].unsqueeze(2).to_broadcast(whole), ALU.mult))
                dve.wait_ge(s["c_gain"], 16)
                step(dve.tensor_tensor(y[:, :, :], y[:, :, :], gain[:, :].unsqueeze(1).to_broadcast([P, TT, BANK]), ALU.mult))
                dve.wait_ge(s["gate_done"], 1)
                step(dve.tensor_tensor(rg, y[:, :, :], rg, ALU.mult))

            @block.gpsimd
            def _(pool):
                pool.wait_ge(s["exps"], HEADS)
                pool.tensor_tensor(decay[:, :, 0:P], decay[:, :, 0:P],
                                   g.causal_t[:, :].unsqueeze(1).to_broadcast([P, HEADS, P]), ALU.mult).then_inc(s["decay_ready"], 1)

            @block.scalar
            def _(act):
                act.wait_ge(s["span_ready"], 1)
                for h in range(HEADS):
                    act.activation(decay[:, h, :], span[:, :], ACT.Exp, scale=float(np.log(gamma[h]))).then_inc(s["exps"], 1)
                for n in range(8):
                    act.wait_ge(s["flipped"], n + 1)
                    act.activation(g.ht[:, n, :], g.bank[n % 4][:, :], ACT.Copy).then_inc(s["flip_out"], 1)
                for h in range(HEADS):
                    act.wait_ge(s["summed"], h + 1)
                    act.activation(y[:, :, h * RD:(h + 1) * RD], g.bank[4 + h % 2][:, 0:TT * RD].rearrange("p (i w) -> p i w", w=RD),
                                   ACT.Copy).then_inc(s["y_out"], 1)
                act.activation(rg, rg, ACT.Silu).then_inc(s["gate_done"], 1)
                act.wait_ge(s["sq_done"], 1)
                act.activation(rms[:, :], var[:, :], ACT.Sqrt, scale=1.0 / RD, bias=g.eps[:, :]).then_inc(s["root_done"], 1)

            @block.tensor
            def _(pe):
                pe.wait_ge(s["rotated"], 2)
                flip_pairs(pe, g, s, q, k)
                pe.wait_ge(s["flip_out"], 8)

                def sums(h):
                    pe.wait_ge(s["weighed"], TT * (h + 1))
                    if h >= 2:
                        pe.wait_ge(s["y_out"], h - 1)
                    for i in range(TT):
                        for j in range(i + 1):
                            last = pe.matmul(g.bank[4 + h % 2][:, i * RD:(i + 1) * RD], sd[:, h % 2, j, (i - j) * P:(i - j + 1) * P],
                                             v[:, j, h * RD:(h + 1) * RD], start=(j == 0), stop=(j == i))
                    last.then_inc(s["summed"], 1)
                for h in range(HEADS):
                    lo = RD * (h % 2)
                    for j in range(TT):
                        n = TT * h + j
                        if n >= 4:
                            pe.wait_ge(s["weighed"], n - 3)
                        pe.matmul(g.bank[n % 4][:, 0:T - j * P], kt[lo:lo + RD, h // 2, j * P:(j + 1) * P],
                                  qt[lo:lo + RD, h // 2, j * P:T], start=True, stop=True).then_inc(s["scored"], 1)
                    if h:
                        sums(h - 1)
                sums(HEADS - 1)


ATTN_SEMS = " at_scored at_max at_exp at_flipped at_pt at_summed at_out at_dve"


class Attention:

    def __init__(self, g, ctx, units, scale, s):
        self.g, self.units, self.scale, self.s = g, units, scale, s

        def sb(name, shape):
            return ctx.enter_context(g.nc.sbuf_tensor(fresh(name), shape, F32))
        self.p = sb("at_p", [P, 2, T])
        self.pt = sb("at_pt", [P, 2, T])
        n = len(units)
        self.mx = sb("at_mx", [P, n])
        self.nmx = sb("at_nmx", [P, n])
        self.sum = sb("at_sum", [P, n])
        self.inv = sb("at_inv", [P, n])

    def pe(self, pe):
        g, s, units = self.g, self.s, self.units

        def scores(u):
            q, k, keys, _, _, _ = units[u]
            if u >= 2:
                pe.wait_ge(s["at_exp"], u - 1)
            for n, (qc, kc) in enumerate(zip(q, k)):
                last = pe.matmul(g.bank[u % 2][:, 0:keys], qc, kc, start=(n == 0), stop=(n == len(q) - 1))
            last.then_inc(s["at_scored"], 1)

        def flip(u):
            keys = units[u][2]
            pe.wait_ge(s["at_exp"], u + 1)
            if u >= 2:
                pe.wait_ge(s["at_pt"], u - 1)
            for j in range(keys // P):
                last = pe.transpose(g.bank[2 + u % 2][:, j * P:(j + 1) * P], self.p[:, u % 2, j * P:(j + 1) * P], g.ident[:, :])
            last.then_inc(s["at_flipped"], 1)

        def sums(u):
            _, _, keys, _, v, out = units[u]
            pe.wait_ge(s["at_pt"], u + 1)
            if u >= 2:
                pe.wait_ge(s["at_out"], u - 1)
            for j in range(keys // P):
                last = pe.matmul(g.bank[4 + u % 2][:, 0:v[j].shape[-1]], self.pt[:, u % 2, j * P:(j + 1) * P], v[j],
                                 start=(j == 0), stop=(j == keys // P - 1))
            last.then_inc(s["at_summed"], 1)
        N = len(units)
        scores(0)
        for u in range(N):
            if u + 1 < N:
                scores(u + 1)
            flip(u)
            if u:
                sums(u - 1)
        sums(N - 1)

    def dve(self, dve):
        g, s, units = self.g, self.s, self.units
        step = InOrder(dve, s["at_dve"])

        def maxima(u):
            _, _, keys, causal, _, _ = units[u]
            dve.wait_ge(s["at_scored"], u + 1)
            if causal:
                step(dve.tensor_tensor(g.bank[u % 2][:, keys - P:keys], g.bank[u % 2][:, keys - P:keys], g.causal_neg[:, :], ALU.add))
            step(dve.tensor_reduce(self.mx[:, u:u + 1], g.bank[u % 2][:, 0:keys], AX_X, ALU.max))
            dve.tensor_scalar(self.nmx[:, u:u + 1], self.mx[:, u:u + 1], -self.scale, None, ALU.mult).then_inc(s["at_max"], 1)

        def finish(u):
            v, out = units[u][4:]
            dve.wait_ge(s["at_exp"], u + 1)
            step(dve.reciprocal(self.inv[:, u:u + 1], self.sum[:, u:u + 1]))
            dve.wait_ge(s["at_summed"], u + 1)
            dve.tensor_scalar(out, g.bank[4 + u % 2][:, 0:v[0].shape[-1]], self.inv[:, u:u + 1], None, ALU.mult).then_inc(s["at_out"], 1)
        N = len(units)
        maxima(0)
        for u in range(N):
            if u + 1 < N:
                maxima(u + 1)
            if u:
                finish(u - 1)
        finish(N - 1)

    def act(self, act):
        g, s, units = self.g, self.s, self.units

        def exps(u):
            keys = units[u][2]
            act.wait_ge(s["at_max"], u + 1)
            if u >= 2:
                act.wait_ge(s["at_flipped"], u - 1)
            act.activation(self.p[:, u % 2, 0:keys], g.bank[u % 2][:, 0:keys], ACT.Exp, bias=self.nmx[:, u:u + 1],
                           scale=self.scale, accum_out=self.sum[:, u:u + 1]).then_inc(s["at_exp"], 1)

        def evac(u):
            keys = units[u][2]
            act.wait_ge(s["at_flipped"], u + 1)
            if u >= 2:
                act.wait_ge(s["at_summed"], u - 1)
            act.activation(self.pt[:, u % 2, 0:keys], g.bank[2 + u % 2][:, 0:keys], ACT.Copy).then_inc(s["at_pt"], 1)
        N = len(units)
        exps(0)
        for u in range(N):
            if u + 1 < N:
                exps(u + 1)
            evac(u)


def latent_attention(g, proj):
    nc, a = g.nc, g.a
    q = proj[:, :, C_RQ:C_RQ + HEADS * QK]
    k = proj[:, :, C_RQ + HEADS * QK:C_RQ + 2 * HEADS * QK]
    qh = q.rearrange("p i (h w) -> p i h w", w=QK)
    kh = k.rearrange("p i (h w) -> p i h w", w=QK)
    y = proj[:, :, C_RQ:C_RQ + BANK]
    with ExitStack() as ctx:
        def sb(name, shape, dt=F32):
            return ctx.enter_context(nc.sbuf_tensor(name, shape, dt))
        v = sb("mla_v", [P, TT, HEADS, VD])
        kt = sb("mla_kt", [P, HEADS, T])
        qt = g.ht
        with ExitStack() as early:
            def eb(name, shape, dt=F32):
                return early.enter_context(nc.sbuf_tensor(name, shape, dt))
            w_uq = eb("w_uq_sb", [P, 2, HEADS * QK])
            w_ukv = eb("w_ukv_sb", [P, HEADS * 2 * VD])
            lat = eb("lat", [P, 3, T])
            gains = eb("lat_gain", [P, 3])
            scratch = eb("lat_sq", [P, TT, C_KR])
            tmp = eb("mla_tmp", [P, 4, TT, HEADS, ROPE // 2])
            ss, rms, rs = (eb(n, [P, 2, TT]) for n in ("lat_ss", "lat_rms", "lat_rs"))
            with stage(nc, "d_w d_sq d_root d_scaled d_flipped d_lat d_mm d_qk d_v d_dve d_turned d_pt d_pc") as (block, s):
                @block.sync
                def _(sp):
                    sp.dma_start(w_uq[:, :, :], a["w_uq"][0].rearrange("(k p) n -> p k n", p=P)).then_inc(s["d_w"], 16)
                    sp.dma_start(w_ukv[:, :], a["w_ukv"][0]).then_inc(s["d_w"], 16)
                    sp.dma_start(gains[:, 0:2], a["g_q_norm"][0].rearrange("(k p) -> p k", p=P)).then_inc(s["d_w"], 16)
                    sp.dma_start(gains[:, 2:3], a["g_kv_norm"][0].rearrange("(k p) -> p k", p=P)).then_inc(s["d_w"], 16)

                @block.scalar
                def _(act):
                    for i in range(TT):
                        act.activation(scratch[:, i, 0:Q_RANK], proj[:, i, C_QL:C_KV], ACT.Square, accum_out=ss[:, 0, i:i + 1]).then_inc(s["d_sq"], 1)
                        act.activation(scratch[:, i, Q_RANK:C_KR], proj[:, i, C_KV:C_KR], ACT.Square, accum_out=ss[:, 1, i:i + 1]).then_inc(s["d_sq"], 1)
                    act.wait_ge(s["d_sq"], 2 * TT)
                    act.activation(rms[:, 0, :], ss[:, 0, :], ACT.Sqrt, scale=1.0 / Q_RANK, bias=g.eps[:, :]).then_inc(s["d_root"], 1)
                    act.activation(rms[:, 1, :], ss[:, 1, :], ACT.Sqrt, scale=1.0 / KV_RANK, bias=g.eps[:, :]).then_inc(s["d_root"], 1)
                    act.wait_ge(s["d_w"], 64)
                    for c in range(3):
                        act.wait_ge(s["d_flipped"], c + 1)
                        act.activation(lat[:, c, :], g.bank[c][:, :], ACT.Copy, scale=gains[:, c:c + 1]).then_inc(s["d_lat"], 1)
                    for n in range(8):
                        i, half = n // 2, n % 2
                        act.wait_ge(s["d_mm"], n + 1)
                        act.activation(q[:, i, half * 384:(half + 1) * 384], g.bank[3 + n % 4][:, 0:384], ACT.Copy).then_inc(s["d_qk"], 1)
                    for n in range(8):
                        i, half = n // 2, n % 2
                        act.wait_ge(s["d_mm"], 8 + n + 1)
                        act.activation(v[:, i, 4 * half:4 * half + 4, :],
                                       g.bank[3 + n % 4][:, :].rearrange("p (h w) -> p h w", w=2 * VD)[:, :, VD:2 * VD],
                                       ACT.Copy).then_inc(s["d_v"], 1)
                    for n in range(16):
                        act.wait_ge(s["d_pt"], n + 1)
                        dst = qt if n < 8 else kt
                        act.activation(dst[0:QK, n % 8, :], g.bank[n % 3][0:QK, :], ACT.Copy).then_inc(s["d_pc"], 1)

                @block.vector
                def _(dve):
                    step = InOrder(dve, s["d_dve"])
                    shape = [P, TT, ROPE // 2]
                    few = [tt[:, 0, :, 0:HALF:2] for tt in (g.cos, g.sin)]
                    kr = proj[:, :, C_KR:C_RQ]
                    rotate(dve, step, kr[:, :, 0:ROPE // 2], kr[:, :, ROPE // 2:ROPE], few[0], few[1],
                           [tmp[:, n, :, 0, :] for n in range(4)])
                    step(dve.tensor_copy(kh[:, :, :, NOPE:QK], kr.unsqueeze(2).to_broadcast([P, TT, HEADS, ROPE])))
                    dve.wait_ge(s["d_root"], 2)
                    step(dve.reciprocal(rs[:, :, :], rms[:, :, :]))
                    for i in range(TT):
                        dve.tensor_scalar(proj[:, i, C_QL:C_KV], proj[:, i, C_QL:C_KV], rs[:, 0, i:i + 1], None, ALU.mult).then_inc(s["d_scaled"], 1)
                        dve.tensor_scalar(proj[:, i, C_KV:C_KR], proj[:, i, C_KV:C_KR], rs[:, 1, i:i + 1], None, ALU.mult).then_inc(s["d_scaled"], 1)
                    dve.wait_ge(s["d_qk"], 8)
                    shape = [P, TT, HEADS, ROPE // 2]
                    rotate(dve, step, qh[:, :, :, NOPE:NOPE + ROPE // 2], qh[:, :, :, NOPE + ROPE // 2:QK],
                           few[0].unsqueeze(2).to_broadcast(shape), few[1].unsqueeze(2).to_broadcast(shape),
                           [tmp[:, n] for n in range(4)])
                    dve.sem_inc(s["d_turned"], 1)
                    for n in range(8):
                        i, half = n // 2, n % 2
                        dve.wait_ge(s["d_v"], n + 1)
                        dve.tensor_copy(kh[:, i, 4 * half:4 * half + 4, 0:NOPE],
                                        g.bank[3 + n % 4][:, :].rearrange("p (h w) -> p h w", w=2 * VD)[:, :, 0:NOPE]).then_inc(s["d_turned"], 1)

                @block.tensor
                def _(pe):
                    pe.wait_ge(s["d_scaled"], 2 * TT)
                    for c in range(3):
                        for i in range(TT):
                            last = pe.transpose(g.bank[c][:, i * P:(i + 1) * P], proj[:, i, c * P:(c + 1) * P], g.ident[:, :])
                        last.then_inc(s["d_flipped"], 1)
                    pe.wait_ge(s["d_lat"], 3)
                    for n in range(8):
                        i, half = n // 2, n % 2
                        if n >= 4:
                            pe.wait_ge(s["d_qk"], n - 3)
                        for c in range(2):
                            last = pe.matmul(g.bank[3 + n % 4][:, 0:384], lat[:, c, i * P:(i + 1) * P], w_uq[:, c, half * 384:(half + 1) * 384],
                                             start=(c == 0), stop=(c == 1))
                        last.then_inc(s["d_mm"], 1)
                    for n in range(8):
                        i, half = n // 2, n % 2
                        if n < 4:
                            pe.wait_ge(s["d_qk"], n + 5)
                        else:
                            pe.wait_ge(s["d_v"], n - 3)
                            pe.wait_ge(s["d_turned"], 1 + n - 3)
                        pe.matmul(g.bank[3 + n % 4][:, :], lat[:, 2, i * P:(i + 1) * P], w_ukv[:, half * BANK:(half + 1) * BANK],
                                  start=True, stop=True).then_inc(s["d_mm"], 1)
                    for n in range(16):
                        pe.wait_ge(s["d_turned"], 1 if n < 8 else 9)
                        if n >= 3:
                            pe.wait_ge(s["d_pc"], n - 2)
                        src = q if n < 8 else k
                        for i in range(TT):
                            last = pe.transpose(g.bank[n % 3][0:QK, i * P:(i + 1) * P], src[:, i, (n % 8) * QK:(n % 8 + 1) * QK], g.ident[:, :])
                        last.then_inc(s["d_pt"], 1)
        units = [([qt[0:QK, h, i * P:(i + 1) * P]], [kt[0:QK, h, 0:(i + 1) * P]], (i + 1) * P, True,
                  [v[:, j, h, :] for j in range(i + 1)], y[:, i, h * VD:(h + 1) * VD])
                 for h in range(HEADS) for i in range(TT)]
        with stage(nc, ATTN_SEMS) as (block, s):
            at = Attention(g, ctx, units, QK ** -0.5, s)

            @block.sync
            def _(sp):
                pass

            @block.tensor
            def _(pe):
                at.pe(pe)

            @block.vector
            def _(dve):
                at.dve(dve)

            @block.scalar
            def _(act):
                at.act(act)


def mix_out(g, chunks, first_unit, gate, local):
    nc = g.nc
    tmp = local.enter_context(nc.sbuf_tensor(fresh("mix_tmp"), [P, 2, BANK], F32))
    with stage(nc, "e_flipped e_ht e_added e_dve") as (block, s):
        @block.sync
        def _(sp):
            g.prefetch(sp, first_unit + 2 + RING)

        @block.tensor
        def _(pe):
            for k in range(DC):
                if k >= 4:
                    pe.wait_ge(s["e_ht"], k - 3)
                for i in range(TT):
                    last = pe.transpose(g.bank[4 + k % 4][:, i * P:(i + 1) * P], chunks(k)[:, i, :], g.ident[:, :])
                last.then_inc(s["e_flipped"], 1)
            pe.wait_ge(s["e_ht"], DC)
            n = 0
            for u in range(first_unit, first_unit + 2):
                w = g.weights(pe, u)
                for i in range(TT):
                    if n >= 4:
                        pe.wait_ge(s["e_added"], n - 3)
                    for k in range(DC):
                        last = pe.matmul(g.bank[n % 4][:, :], g.ht[:, k, i * P:(i + 1) * P], w[:, k, :], start=(k == 0), stop=(k == DC - 1))
                    last.then_inc(g.dense, 1)
                    n += 1

        @block.scalar
        def _(act):
            for k in range(DC):
                act.wait_ge(s["e_flipped"], k + 1)
                act.activation(g.ht[:, k, :], g.bank[4 + k % 4][:, :], ACT.Copy).then_inc(s["e_ht"], 1)

        @block.vector
        def _(dve):
            step = InOrder(dve, s["e_dve"])
            n = 0
            for u in range(2):
                for i in range(TT):
                    dve.wait_ge(g.dense, g.before(first_unit) + n + 1)
                    at = g.x[:, i, u * BANK:(u + 1) * BANK]
                    if gate is None:
                        dve.tensor_tensor(at, g.bank[n % 4][:, :], at, ALU.add).then_inc(s["e_added"], 1)
                    else:
                        if n >= 2:
                            dve.wait_ge(s["e_added"], n - 1)
                        step(dve.tensor_tensor(tmp[:, n % 2, :], g.bank[n % 4][:, :], gate[:, u * BANK:(u + 1) * BANK], ALU.mult))
                        dve.tensor_tensor(at, tmp[:, n % 2, :], at, ALU.add).then_inc(s["e_added"], 1)
                    n += 1


def norm_transposed(g, scale, shift, local, source=None, gain_src=None, keep=None, upto=0, tiles=TT, dst=None,
                    gain_keep=None):
    nc = g.nc
    x = g.x if source is None else source
    dst = g.ht if dst is None else dst
    gain = None
    if gain_src is not None:
        gain = gain_keep if gain_keep is not None else local.enter_context(nc.sbuf_tensor(fresh("nt_gain"), [P, DC], F32))
        scale = gain
    xn = local.enter_context(nc.sbuf_tensor(fresh("nt_xn"), [P, tiles, D], F32)) if keep is None else keep
    ss, rms, rs = (local.enter_context(nc.sbuf_tensor(fresh(n), [P, tiles], F32)) for n in ("nt_ss", "nt_rms", "nt_rs"))
    with stage(nc, "f_gain f_sq f_root f_rs f_xn f_flipped f_out") as (block, s):
        @block.sync
        def _(sp):
            if gain is not None:
                sp.dma_start(gain[:, :], gain_src.rearrange("(k p) -> p k", p=P)).then_inc(s["f_gain"], 16)
            g.prefetch(sp, upto)

        @block.vector
        def _(dve):
            for i in range(tiles):
                dve.wait_ge(s["f_root"], i + 1)
                dve.reciprocal(rs[:, i:i + 1], rms[:, i:i + 1]).then_inc(s["f_rs"], 1)
                dve.wait_ge(s["f_rs"], i + 1)
                dve.tensor_scalar(xn[:, i, :], x[:, i, :], rs[:, i:i + 1], None, ALU.mult).then_inc(s["f_xn"], 1)

        @block.scalar
        def _(act):
            for i in range(tiles):
                act.activation(xn[:, i, :], x[:, i, :], ACT.Square, accum_out=ss[:, i:i + 1]).then_inc(s["f_sq"], 1)
            for i in range(tiles):
                act.wait_ge(s["f_sq"], i + 1)
                act.activation(rms[:, i:i + 1], ss[:, i:i + 1], ACT.Sqrt, scale=1.0 / D, bias=g.eps[:, :]).then_inc(s["f_root"], 1)
            if gain is not None:
                act.wait_ge(s["f_gain"], 16)
            for k in range(DC):
                act.wait_ge(s["f_flipped"], k + 1)
                if shift is None:
                    act.activation(dst[:, k, 0:tiles * P], g.bank[k][:, 0:tiles * P], ACT.Copy, scale=scale[:, k:k + 1]).then_inc(s["f_out"], 1)
                else:
                    act.activation(dst[:, k, 0:tiles * P], g.bank[k][:, 0:tiles * P], ACT.Identity, bias=shift[:, k:k + 1],
                                   scale=scale[:, k:k + 1]).then_inc(s["f_out"], 1)

        @block.tensor
        def _(pe):
            pe.wait_ge(s["f_xn"], tiles)
            for k in range(DC):
                for i in range(tiles):
                    last = pe.transpose(g.bank[k][:, i * P:(i + 1) * P], xn[:, i, k * P:(k + 1) * P], g.ident[:, :])
                last.then_inc(s["f_flipped"], 1)


LOW = -3.0e38


def top16(dve, count, done, rows):
    def all_done():
        count[0] += len(rows)
        dve.wait_ge(done, count[0])
    for v, work, top, at in rows:
        dve.max(top[:, 0:8], v).then_inc(done, 1)
    all_done()
    for v, work, top, at in rows:
        dve.max_index(at[:, 0:8], top[:, 0:8], v).then_inc(done, 1)
    all_done()
    for v, work, top, at in rows:
        dve.match_replace(work, top[:, 0:8], v, LOW).then_inc(done, 1)
    all_done()
    for v, work, top, at in rows:
        dve.max(top[:, 8:16], work).then_inc(done, 1)
    all_done()
    for v, work, top, at in rows:
        dve.max_index(at[:, 8:16], top[:, 8:16], work).then_inc(done, 1)
    all_done()


def top_keys(g, top_v, top_i, first_unit):
    nc, a = g.nc, g.a
    HP = 2 * PH
    with ExitStack() as ctx:
        keys = ctx.enter_context(nc.sbuf_tensor("keys_t", [P, 2, PK], F32))
        qf = ctx.enter_context(nc.sbuf_tensor("peer_q", [P, 2, T], F32))
        work = ctx.enter_context(nc.sbuf_tensor("top_work", [P, TT, PK], F32))
        with stage(nc, "g_keys g_q g_scored g_topped g_dve") as (block, s):
            @block.sync
            def _(sp):
                sp.dma_start(keys[:, :, :], a["sub_keys_t"].rearrange("h d k -> d h k")).then_inc(s["g_keys"], 16)
                g.prefetch(sp, first_unit + 4 + RING)

            @block.tensor
            def _(pe):
                pe.wait_ge(s["g_keys"], 16)

                def scores(n):
                    pe.wait_ge(s["g_q"], n + 1)
                    if n >= 2:
                        pe.wait_ge(s["g_topped"], n - 1)
                    for i in range(TT):
                        last = pe.matmul(g.bank[2 + n % 2][:, i * PK:(i + 1) * PK], qf[:, n % 2, i * P:(i + 1) * P], keys[:, n % 2, :],
                                         start=True, stop=True)
                    last.then_inc(s["g_scored"], 1)
                for n in range(HP):
                    w = g.weights(pe, first_unit + n // 4)
                    if n >= 2:
                        pe.wait_ge(s["g_q"], n - 1)
                    for k in range(DC):
                        last = pe.matmul(g.bank[n % 2][:, :], w[:, k, (n % 4) * P:(n % 4 + 1) * P], g.ht[:, k, :], start=(k == 0), stop=(k == DC - 1))
                    last.then_inc(g.dense, 1)
                    if n:
                        scores(n - 1)
                scores(HP - 1)

            @block.scalar
            def _(act):
                for n in range(HP):
                    act.wait_ge(g.dense, g.before(first_unit) + n + 1)
                    if n >= 2:
                        act.wait_ge(s["g_scored"], n - 1)
                    act.activation(qf[:, n % 2, :], g.bank[n % 2][:, :], ACT.Copy).then_inc(s["g_q"], 1)

            @block.vector
            def _(dve):
                count = [0]
                for n in range(HP):
                    dve.wait_ge(s["g_scored"], n + 1)
                    top16(dve, count, s["g_dve"], [(g.bank[2 + n % 2][:, i * PK:(i + 1) * PK], work[:, i, :], top_v[:, i, n, :], top_i[:, i, n, :])
                                                   for i in range(TT)])
                    dve.sem_inc(s["g_topped"], 1)


def choose_experts(g, top_v, top_i, key1_t, key2_t, gate_t):
    nc = g.nc
    with ExitStack() as ctx:
        def sb(name, shape, dt=F32):
            return ctx.enter_context(nc.sbuf_tensor(name, shape, dt))
        sums = sb("sums", [P, 2, PH, TOPK, TOPK])
        work = sb("sum_work", [P, 4, TOPK * TOPK])
        best = sb("best", [P, TT, PH, TOPK])
        place = sb("place", [P, TT, PH, TOPK], U32)
        rank_i = sb("rank_i", [P, 2, TT, PH, TOPK], U32)
        rank = sb("rank", [P, 2, TT, PH, TOPK])
        key_f = sb("key_f", [P, TT, 2 * PH, TOPK])
        hit = sb("hit", [P, 2, PH, TOPK, TOPK])
        key = sb("key", [P, 2, TT, PH, TOPK])
        gate = sb("gate", [P, TT, PH, TOPK])
        total = sb("total", [P, TT, PH])
        inv = sb("inv_total", [P, TT, PH])
        v = top_v[:, :, :, :].rearrange("p i (h s) k -> p i h s k", s=2)
        kf = key_f[:, :, :, :].rearrange("p i (h s) k -> p i h s k", s=2)
        wide = [P, PH, TOPK, TOPK]
        with stage(nc, "h_sums h_dve h_chain h_top h_shift h_exp h_gate h_keyed h_pool h_key2 h_red h_flipped h_out") as (block, s):
            @block.sync
            def _(sp):
                pass

            @block.gpsimd
            def _(pool):
                step = InOrder(pool, s["h_pool"])
                for i in range(TT):
                    if i >= 2:
                        pool.wait_ge(s["h_top"], i - 1)
                    pool.tensor_tensor(sums[:, i % 2], v[:, i, :, 0, :].unsqueeze(3).to_broadcast(wide),
                                       v[:, i, :, 1, :].unsqueeze(2).to_broadcast(wide), ALU.add).then_inc(s["h_sums"], 1)
                pool.tensor_copy(key_f[:, :, :, :], top_i[:, :, :, :]).then_inc(s["h_keyed"], 1)

            @block.vector
            def _(dve):
                count = [0]
                for i in range(TT):
                    dve.wait_ge(s["h_sums"], i + 1)
                    for h in range(0, PH, 4):
                        top16(dve, count, s["h_dve"], [(sums[:, i % 2, h + j].rearrange("p a b -> p (a b)"), work[:, j, :],
                                                        best[:, i, h + j, :], place[:, i, h + j, :]) for j in range(4)])
                    dve.sem_inc(s["h_top"], 1)
                step = InOrder(dve, s["h_chain"])
                dve.tensor_tensor(gate[:], best[:], best[:, :, :, 0:1].to_broadcast([P, TT, PH, TOPK]), ALU.subtract).then_inc(s["h_shift"], 1)
                step(dve.tensor_scalar(rank_i[:, 0], place[:], 4, None, ALU.arith_shift_right))
                step(dve.tensor_scalar(rank_i[:, 1], place[:], 15, None, ALU.bitwise_and))
                step(dve.tensor_copy(rank[:], rank_i[:]))
                dve.wait_ge(s["h_exp"], 1)
                step(dve.tensor_reduce(total[:], gate[:], AX_X, ALU.add))
                step(dve.reciprocal(inv[:], total[:]))
                dve.tensor_tensor(gate[:], gate[:], inv[:].unsqueeze(3).to_broadcast([P, TT, PH, TOPK]), ALU.mult).then_inc(s["h_gate"], 1)
                dve.wait_ge(s["h_keyed"], 1)
                for i in range(TT):
                    for half in range(2):
                        step(dve.tensor_tensor(hit[:, half], rank[:, half, i].unsqueeze(3).to_broadcast(wide),
                                               g.iota_p[:, 0:TOPK].unsqueeze(1).unsqueeze(1).to_broadcast(wide), ALU.is_equal))
                        step(dve.tensor_tensor(hit[:, half], hit[:, half], kf[:, i, :, half, :].unsqueeze(2).to_broadcast(wide), ALU.mult))
                        dve.tensor_reduce(key[:, half, i], hit[:, half], AX_X, ALU.add).then_inc(s["h_red"], 1)
                        dve.wait_ge(s["h_red"], 2 * i + half + 1)

            @block.scalar
            def _(act):
                act.wait_ge(s["h_shift"], 1)
                act.activation(gate[:], gate[:], ACT.Exp).then_inc(s["h_exp"], 1)
                for n, dst in enumerate((gate_t, key1_t, key2_t)):
                    act.wait_ge(s["h_flipped"], n + 1)
                    act.activation(dst[:, :], g.bank[n][:, :], ACT.Copy).then_inc(s["h_out"], 1)

            @block.tensor
            def _(pe):
                pe.wait_ge(s["h_gate"], 1)
                for n, src in enumerate((gate[:], key[:, 0], key[:, 1])):
                    if n:
                        pe.wait_ge(s["h_red"], 2 * TT)
                    for i in range(TT):
                        last = pe.transpose(g.bank[n][:, i * P:(i + 1) * P], src[:, i].rearrange("p h k -> p (h k)"), g.ident[:, :])
                    last.then_inc(s["h_flipped"], 1)


F16 = mybir.dt.float16
LIFT = 1024.0
GB = 64
GQ = GB // 4


def spread_gates(g, key1_t, key2_t, gate_t, gates):
    nc = g.nc
    with ExitStack() as ctx:
        def sb(name, shape, dt=F32):
            return ctx.enter_context(nc.sbuf_tensor(name, shape, dt))
        lifted = sb("lifted", [P, T])
        part = sb("part", [P, T], F16)
        hi = sb("gate_hi", [P, T])
        lo = sb("gate_lo", [P, T])
        iota = sb("iota_half", [P, P], F16)
        now = sb("now", [P, 2, 4, GB])
        one1 = sb("one1", [P, 2, 4, 2, P], F16)
        one2 = sb("one2", [P, 2, 4, P], F16)
        out = sb("spread", [P, 2, P, GB])
        with stage(nc, "i_dve i_parts i_now i_one1 i_one2 i_mm i_out i_stored0 i_stored1 i_paced") as (block, s):
            stored = (s["i_stored0"], s["i_stored1"])

            @block.vector
            def _(dve):
                step = InOrder(dve, s["i_dve"])
                step(dve.tensor_scalar(lifted[:, :], gate_t[:, :], LIFT, None, ALU.mult))
                step(dve.tensor_copy(part[:, :], lifted[:, :]))
                step(dve.tensor_copy(hi[:, :], part[:, :]))
                step(dve.tensor_tensor(lo[:, :], lifted[:, :], hi[:, :], ALU.subtract))
                step(dve.tensor_copy(iota[:, :], g.iota_p[:, :]))
                with dve.Fori(0, T // GB // 2) as it:
                    for b in range(2):
                        blk = it * 2 + b
                        for n, src in enumerate((key1_t, key2_t, hi, lo)):
                            last = dve.tensor_copy(now[:, b, n, :], src[:, bass.ds(blk * GB, GB)])
                            last.then_inc(s["i_now"], 1)
                        dve.wait_ge(s["i_now"], blk * 4 + 4)
                        for q in range(GQ):
                            n = blk * GQ + q
                            dve.wait_ge(s["i_mm"], n + 1)
                            for j in range(4):
                                c = q * 4 + j
                                for part_n in range(2):
                                    last = dve.tensor_scalar(one1[:, q % 2, j, part_n, :], iota[:, :], now[:, b, 0, c:c + 1],
                                                             now[:, b, 2 + part_n, c:c + 1], ALU.is_equal, ALU.mult)
                            last.then_inc(s["i_one1"], 1)

            @block.gpsimd
            def _(pool):
                with pool.Fori(0, T // GB // 2) as it:
                    for b in range(2):
                        blk = it * 2 + b
                        pool.wait_ge(s["i_now"], blk * 4 + 4)
                        for q in range(GQ):
                            pool.wait_ge(s["i_mm"], blk * GQ + q + 1)
                            pool.sem_inc(s["i_paced"], 1)
                            for j in range(4):
                                c = q * 4 + j
                                last = pool.tensor_scalar(one2[:, q % 2, j, :], g.iota_p[:, :], now[:, b, 1, c:c + 1], None, ALU.is_equal)
                            last.then_inc(s["i_one2"], 1)

            @block.tensor
            def _(pe):
                pe.sem_inc(s["i_mm"], 2)
                with pe.Fori(0, T // GB // 2) as it:
                    for b in range(2):
                        blk = it * 2 + b
                        for q in range(GQ):
                            n = blk * GQ + q
                            pe.wait_ge(s["i_one1"], n + 1)
                            pe.wait_ge(s["i_one2"], n + 1)
                            pe.wait_ge(s["i_out"], n + 1)
                            for j in range(4):
                                for part_n in range(2):
                                    last = pe.matmul(g.bank[q % 4][:, j * P:(j + 1) * P], one2[:, q % 2, j, :], one1[:, q % 2, j, part_n, :],
                                                     start=(part_n == 0), stop=(part_n == 1))
                            last.then_inc(s["i_mm"], 1)

            @block.scalar
            def _(act):
                act.sem_inc(s["i_out"], 4)
                with act.Fori(0, T // GB // 2) as it:
                    for b in range(2):
                        blk = it * 2 + b
                        act.wait_ge(stored[b], it * 16 + 16)
                        for q in range(GQ):
                            n = blk * GQ + q
                            act.wait_ge(s["i_mm"], n + 3)
                            act.activation(out[:, b, :, q * 4:q * 4 + 4].rearrange("p k t -> p t k"),
                                           g.bank[q % 4][:, :].rearrange("p (t k) -> p t k", k=P), ACT.Copy, scale=1.0 / LIFT).then_inc(s["i_out"], 1)

            @block.sync
            def _(sp):
                for b in range(2):
                    sp.sem_inc(stored[b], 16)
                with sp.Fori(0, T // GB // 2) as it:
                    for b in range(2):
                        blk = it * 2 + b
                        sp.wait_ge(s["i_out"], (blk + 1) * GQ + 4)
                        sp.dma_start(gates[:, :, bass.ds(blk * GB, GB)].rearrange("k p t -> p k t"), out[:, b]).then_inc(stored[b], 16)
                for b in range(2):
                    sp.wait_ge(stored[b], 16 * (T // GB // 2 + 1))


def experts(g, gates, acc):
    nc, a = g.nc, g.a
    GT = 4
    Q = PK // GT
    NO = 2 * TT
    with ExitStack() as ctx:
        def sb(name, shape, dt=F32):
            return ctx.enter_context(nc.sbuf_tensor(name, shape, dt))
        u_in = sb("u_in", [P, GT, DC, P])
        v_in = sb("v_in", [P, 2, GT, D])
        gate_in = sb("gate_in", [P, GT, T])
        gel = sb("gel", [P, 2, T])
        w = sb("peer_w", [P, 2, GT, T])
        names = " ".join([f"j_u{e}" for e in range(GT)] + [f"j_g{e}" for e in range(GT)] + ["j_v0", "j_v1"])
        with stage(nc, names + " j_zero j_a j_gelu j_w j_o j_added") as (block, s):
            u_loaded = [s[f"j_u{e}"] for e in range(GT)]
            g_loaded = [s[f"j_g{e}"] for e in range(GT)]
            v_loaded = [s["j_v0"], s["j_v1"]]

            def load(sp, q, par, first, second):
                for e in range(GT):
                    if not first:
                        sp.wait_ge(s["j_a"], (q - 1) * GT + e + 1)
                    sp.dma_start(u_in[:, e], a["u_tiles"][bass.ds(q * GT + e, 1)].rearrange("o p c e -> p (o c) e")).then_inc(u_loaded[e], 16)
                    if not first:
                        sp.wait_ge(s["j_w"], (q - 1) * GT + e + 1)
                    sp.dma_start(gate_in[:, e], gates[bass.ds(q * GT + e, 1)].rearrange("o p t -> p (o t)")).then_inc(g_loaded[e], 16)
                if not (first or second):
                    sp.wait_ge(s["j_o"], (q - 1) * NO)
                sp.dma_start(v_in[:, par], a["expert_v"][0].rearrange("(t p) d -> p t d", p=P)[:, bass.ds(q * GT, GT), :]).then_inc(v_loaded[par], 16)

            @block.sync
            def _(sp):
                load(sp, 0, 0, True, False)
                load(sp, 1, 1, False, True)
                with sp.Fori(1, Q // 2) as it:
                    load(sp, it * 2, 0, False, False)
                    load(sp, it * 2 + 1, 1, False, False)

            @block.gpsimd
            def _(pool):
                pool.memset(acc[:, :, :], 0.0).then_inc(s["j_zero"], 1)

            def up(pe, q, par, first):
                for e in range(GT):
                    pe.wait_ge(u_loaded[e], (q + 1) * 16)
                    if not first:
                        pe.wait_ge(s["j_gelu"], (q - 1) * GT + e + 1)
                    for k in range(DC):
                        last = pe.matmul(g.bank[e][:, :], u_in[:, e, k, :], g.ht[:, k, :], start=(k == 0), stop=(k == DC - 1))
                    last.then_inc(s["j_a"], 1)

            def down(pe, q, par, half, first):
                pe.wait_ge(s["j_w"], (q + 1) * GT)
                pe.wait_ge(v_loaded[par], (half + 1) * 16)
                for o in range(NO):
                    i, c = o // 2, o % 2
                    if not (first and o < 4):
                        pe.wait_ge(s["j_added"], q * NO + o - 3)
                    for e in range(GT):
                        last = pe.matmul(g.bank[4 + o % 4][:, :], w[:, par, e, i * P:(i + 1) * P], v_in[:, par, e, c * BANK:(c + 1) * BANK],
                                         start=(e == 0), stop=(e == GT - 1))
                    last.then_inc(s["j_o"], 1)

            @block.tensor
            def _(pe):
                up(pe, 0, 0, True)
                up(pe, 1, 1, False)
                down(pe, 0, 0, 0, True)
                with pe.Fori(1, Q // 2) as it:
                    up(pe, it * 2, 0, False)
                    down(pe, it * 2 - 1, 1, it - 1, False)
                    up(pe, it * 2 + 1, 1, False)
                    down(pe, it * 2, 0, it, False)
                down(pe, Q - 1, 1, Q // 2 - 1, False)

            def gelu(act, q, first):
                for e in range(GT):
                    act.wait_ge(s["j_a"], q * GT + e + 1)
                    if not (first and e < 2):
                        act.wait_ge(s["j_w"], q * GT + e - 1)
                    act.activation(gel[:, e % 2, :], g.bank[e][:, :], ACT.Gelu).then_inc(s["j_gelu"], 1)

            @block.scalar
            def _(act):
                gelu(act, 0, True)
                with act.Fori(1, Q) as q:
                    gelu(act, q, False)

            def weigh(dve, q, par, early):
                if not early:
                    dve.wait_ge(s["j_o"], (q - 1) * NO)
                for e in range(GT):
                    dve.wait_ge(s["j_gelu"], q * GT + e + 1)
                    dve.wait_ge(g_loaded[e], (q + 1) * 16)
                    dve.tensor_tensor(w[:, par, e, :], gel[:, e % 2, :], gate_in[:, e, :], ALU.mult).then_inc(s["j_w"], 1)

            def add(dve, q):
                for o in range(NO):
                    i, c = o // 2, o % 2
                    dve.wait_ge(s["j_o"], q * NO + o + 1)
                    at = acc[:, i, c * BANK:(c + 1) * BANK]
                    dve.tensor_tensor(at, g.bank[4 + o % 4][:, :], at, ALU.add).then_inc(s["j_added"], 1)

            @block.vector
            def _(dve):
                dve.wait_ge(s["j_zero"], 1)
                weigh(dve, 0, 0, True)
                weigh(dve, 1, 1, True)
                add(dve, 0)
                with dve.Fori(1, Q // 2) as it:
                    weigh(dve, it * 2, 0, False)
                    add(dve, it * 2 - 1)
                    weigh(dve, it * 2 + 1, 1, False)
                    add(dve, it * 2)
                add(dve, Q - 1)


def close_first(g, acc, gate, upto):
    nc, a = g.nc, g.a
    with ExitStack() as ctx:
        gain = ctx.enter_context(nc.sbuf_tensor("final_gain", [P, D], F32))
        sq = ctx.enter_context(nc.sbuf_tensor("final_sq", [P, TT, D], F32))
        ss, rms, rs = (ctx.enter_context(nc.sbuf_tensor(n, [P, TT], F32)) for n in ("fin_ss", "fin_rms", "fin_rs"))
        with stage(nc, "k_gain k_dve k_sum k_sq k_root k_end") as (block, s):
            @block.sync
            def _(sp):
                sp.dma_start(gain[:, :], a["g_final"].unsqueeze(0).partition_broadcast(P)).then_inc(s["k_gain"], 16)
                g.prefetch(sp, upto)

            @block.vector
            def _(dve):
                step = InOrder(dve, s["k_dve"])
                for i in range(TT):
                    step(dve.tensor_tensor(acc[:, i, :], acc[:, i, :], gate, ALU.mult))
                    dve.tensor_tensor(g.x[:, i, :], acc[:, i, :], g.x[:, i, :], ALU.add).then_inc(s["k_sum"], 1)
                dve.wait_ge(s["k_gain"], 16)
                for i in range(TT):
                    dve.wait_ge(s["k_root"], i + 1)
                    step(dve.reciprocal(rs[:, i:i + 1], rms[:, i:i + 1]))
                    dve.scalar_tensor_tensor(g.x[:, i, :], g.x[:, i, :], rs[:, i:i + 1], gain[:, :], ALU.mult, ALU.mult).then_inc(s["k_end"], 1)

            @block.scalar
            def _(act):
                for i in range(TT):
                    act.wait_ge(s["k_sum"], i + 1)
                    act.activation(sq[:, i, :], g.x[:, i, :], ACT.Square, accum_out=ss[:, i:i + 1]).then_inc(s["k_sq"], 1)
                for i in range(TT):
                    act.wait_ge(s["k_sq"], i + 1)
                    act.activation(rms[:, i:i + 1], ss[:, i:i + 1], ACT.Sqrt, scale=1.0 / D, bias=g.eps[:, :]).then_inc(s["k_root"], 1)


W2_DQ, W2_DK, W2_DV, W2_MQ, W2_MK, W2_MV, W2_MO, W2_GATES = (i * BANK for i in range(8))


def project_second(g, tok, mv, conv, mi, mf, first_unit):
    nc, a = g.nc, g.a
    with ExitStack() as ctx:
        def sb(name, shape, dt=F32):
            return ctx.enter_context(nc.sbuf_tensor(name, shape, dt))
        raw = sb("conv_in", [P, 8, T])
        taps = sb("taps", [P, CONV, 8])
        cbias = sb("conv_bias", [P, 8])
        gbias = sb("gate_bias", [ML_H, 2])
        tmp_ctx = sb("rot_tmp", [P, 2, TT, 4 * HALF])
        tmp_ctx2 = sb("rot_tmp2", [P, 2, TT, 4 * HALF])
        with stage(nc, "l_par l_raw l_conv l_cdone l_tok l_small l_ones l_dve l_rot") as (block, s):
            @block.sync
            def _(sp):
                sp.dma_start(taps[:, :, :], a["ml_conv_w_2"][0].rearrange("j o (c p) -> p (j o) c", p=P)).then_inc(s["l_par"], 16)
                sp.dma_start(cbias[:, :], a["ml_conv_b_2"][0].rearrange("(c p) -> p c", p=P)).then_inc(s["l_par"], 16)
                sp.dma_start(gbias[:, :], a["ml_gate_b_2"][0].rearrange("g h -> h g")).then_inc(s["l_par"], 16)
                g.prefetch(sp, first_unit + 8 + RING)

            @block.gpsimd
            def _(pool):
                pool.memset(mv[:, :, :, ML_D:ML_D + 1], 1.0).then_inc(s["l_ones"], 1)

            @block.tensor
            def _(pe):
                n = 0
                for u in range(2):
                    w = g.weights(pe, first_unit + u)
                    for m in range(4):
                        if n >= 6:
                            pe.wait_ge(s["l_raw"], n - 5)
                        for k in range(DC):
                            last = pe.matmul(g.bank[n % 6][:, :], w[:, k, m * P:(m + 1) * P], g.ht[:, k, :], start=(k == 0), stop=(k == DC - 1))
                        last.then_inc(g.dense, 1)
                        n += 1
                for u in range(2, 7):
                    w = g.weights(pe, first_unit + u)
                    for i in range(TT):
                        if n - 6 < 8:
                            pe.wait_ge(s["l_raw"], n - 5)
                        else:
                            pe.wait_ge(s["l_tok"], n - 6 - 8 + 1)
                        for k in range(DC):
                            last = pe.matmul(g.bank[n % 6][:, :], g.ht[:, k, i * P:(i + 1) * P], w[:, k, :], start=(k == 0), stop=(k == DC - 1))
                        last.then_inc(g.dense, 1)
                        n += 1
                w = g.weights(pe, first_unit + 7)
                for c in range(2):
                    for k in range(DC):
                        last = pe.matmul(g.bank[6 + c][0:ML_H, :], w[:, k, c * ML_H:(c + 1) * ML_H], g.ht[:, k, :], start=(k == 0), stop=(k == DC - 1))
                    last.then_inc(g.dense, 1)

            @block.scalar
            def _(act):
                base = g.before(first_unit)
                n = 0
                for c in range(8):
                    act.wait_ge(g.dense, base + n + 1)
                    act.activation(raw[:, c, :], g.bank[n % 6][:, :], ACT.Copy).then_inc(s["l_raw"], 1)
                    n += 1
                for u in range(5):
                    for i in range(TT):
                        act.wait_ge(g.dense, base + n + 1)
                        if u < 4:
                            act.activation(tok[:, i, u * BANK:(u + 1) * BANK], g.bank[n % 6][:, :], ACT.Copy).then_inc(s["l_tok"], 1)
                        else:
                            act.activation(mv[:, i, :, 0:ML_D], g.bank[n % 6][:, :].rearrange("p (h w) -> p h w", w=ML_D), ACT.Copy).then_inc(s["l_tok"], 1)
                        n += 1
                act.wait_ge(s["l_par"], 48)
                for c, dst in enumerate((mi, mf)):
                    act.wait_ge(g.dense, base + n + c + 1)
                    act.activation(dst[:, :], g.bank[6 + c][0:ML_H, :], ACT.Identity, bias=gbias[:, c:c + 1]).then_inc(s["l_small"], 1)
                act.wait_ge(s["l_conv"], 4 * 8)
                for c in range(8):
                    act.activation(conv[:, c, :], conv[:, c, :], ACT.Silu).then_inc(s["l_cdone"], 1)

            @block.vector
            def _(dve):
                dve.wait_ge(s["l_par"], 48)
                for c in range(8):
                    dve.wait_ge(s["l_raw"], c + 1)
                    dve.tensor_scalar(conv[:, c, :], raw[:, c, :], taps[:, 3, c:c + 1], cbias[:, c:c + 1], ALU.mult, ALU.add).then_inc(s["l_conv"], 1)
                    for back in range(1, CONV):
                        dve.wait_ge(s["l_conv"], 4 * c + back)
                        dve.scalar_tensor_tensor(conv[:, c, back:T], raw[:, c, 0:T - back], taps[:, 3 - back, c:c + 1], conv[:, c, back:T],
                                                 ALU.mult, ALU.add).then_inc(s["l_conv"], 1)
                step = InOrder(dve, s["l_dve"])
                shape = [P, TT, 4, HALF]
                tmp = [t[:, n].rearrange("p i (h w) -> p i h w", w=HALF) for t in (tmp_ctx, tmp_ctx2) for n in range(2)]
                for half in range(4):
                    dve.wait_ge(s["l_tok"], 4 if half < 2 else 8)
                    v = tok[:, :, half * 256:(half + 1) * 256].rearrange("p i (h w) -> p i h w", w=RD)
                    rotate(dve, step, v[:, :, :, 0:HALF], v[:, :, :, HALF:RD], g.cos[:, 1].unsqueeze(2).to_broadcast(shape),
                           g.sin[:, 1].unsqueeze(2).to_broadcast(shape), tmp)
                dve.sem_inc(s["l_rot"], 1)


def differential(g, tok):
    nc, a = g.nc, g.a
    q, k, v, y = tok[:, :, 0:BANK], tok[:, :, BANK:2 * BANK], tok[:, :, 2 * BANK:3 * BANK], tok[:, :, 0:BANK]
    qt, kt = g.ht[:, 0:4, :], g.ht[:, 4:8, :]
    units = [(h, i) for h in range(DA_H) for i in range(TT)]
    N = len(units)
    LAM0 = 0.8 - 0.6
    with ExitStack() as ctx:
        def sb(name, shape, dt=F32):
            return ctx.enter_context(nc.sbuf_tensor(name, shape, dt))
        p = sb("da_p", [P, 2, 2, T])
        diff = sb("da_a", [P, 2, T])
        pt = sb("da_pt", [P, 2, T])
        mx, nmx, tot, inv = (sb(n, [P, 2, N]) for n in ("da_mx", "da_nmx", "da_sum", "da_inv"))
        lv = sb("da_lv", [P, 4, RD])
        prod = sb("da_prod", [P, 2, RD])
        dots, nlam = sb("da_dots", [P, 2]), sb("da_nlam", [P, 2])
        gain = sb("subln", [P, DV_W])
        ms, rms, rs = (sb(n, [P, TT * DA_H]) for n in ("da_ms", "da_rms", "da_rs"))
        with stage(nc, "m_par m_dve m_lam m_lexp flipped flip_out m_s0 m_s1 m_max m_e0 m_e1 m_a m_t m_pt m_o m_y m_sq m_root m_gain") as (block, s):
            @block.sync
            def _(sp):
                sp.dma_start(lv[:, :, :], a["da_lambda_2"].partition_broadcast(P) if False else a["da_lambda_2"][0:1].rearrange("o j w -> o (j w)").partition_broadcast(P)).then_inc(s["m_par"], 16)
                sp.dma_start(gain[:, :], a["da_subln_g_2"][0:1, :].partition_broadcast(P)).then_inc(s["m_par"], 16)

            @block.tensor
            def _(pe):
                flip_pairs(pe, g, s, q, k)
                pe.wait_ge(s["flip_out"], 8)

                def scores(u):
                    h, i = units[u]
                    keys = (i + 1) * P
                    for m in range(2):
                        if u >= 2:
                            pe.wait_ge(s[f"m_e{m}"], u - 1)
                        lo = RD * m
                        pe.matmul(g.bank[2 * m + u % 2][:, 0:keys], qt[lo:lo + RD, h, i * P:(i + 1) * P], kt[lo:lo + RD, h, 0:keys],
                                  start=True, stop=True).then_inc(s[f"m_s{m}"], 1)

                def flip(u):
                    keys = (units[u][1] + 1) * P
                    pe.wait_ge(s["m_a"], u + 1)
                    if u >= 2:
                        pe.wait_ge(s["m_pt"], u - 1)
                    for j in range(keys // P):
                        last = pe.transpose(g.bank[4 + u % 2][:, j * P:(j + 1) * P], diff[:, u % 2, j * P:(j + 1) * P], g.ident[:, :])
                    last.then_inc(s["m_t"], 1)

                def sums(u):
                    h, i = units[u]
                    pe.wait_ge(s["m_pt"], u + 1)
                    if u >= 2:
                        pe.wait_ge(s["m_y"], u - 1)
                    for j in range(i + 1):
                        last = pe.matmul(g.bank[6 + u % 2][:, 0:DV_W], pt[:, u % 2, j * P:(j + 1) * P], v[:, j, h * DV_W:(h + 1) * DV_W],
                                         start=(j == 0), stop=(j == i))
                    last.then_inc(s["m_o"], 1)
                scores(0)
                for u in range(N):
                    if u + 1 < N:
                        scores(u + 1)
                    flip(u)
                    if u:
                        sums(u - 1)
                sums(N - 1)

            @block.scalar
            def _(act):
                act.wait_ge(s["m_lam"], 1)
                act.activation(nlam[:, :], dots[:, :], ACT.Exp).then_inc(s["m_lexp"], 1)
                for n in range(8):
                    act.wait_ge(s["flipped"], n + 1)
                    act.activation(g.ht[:, n, :], g.bank[n % 4][:, :], ACT.Copy).then_inc(s["flip_out"], 1)

                def exps(u):
                    keys = (units[u][1] + 1) * P
                    for m in range(2):
                        act.wait_ge(s["m_max"], 2 * u + m + 1)
                        if u >= 2:
                            act.wait_ge(s["m_a"], u - 1)
                        act.activation(p[:, u % 2, m, 0:keys], g.bank[2 * m + u % 2][:, 0:keys], ACT.Exp, bias=nmx[:, m, u:u + 1],
                                       scale=RD ** -0.5, accum_out=tot[:, m, u:u + 1]).then_inc(s[f"m_e{m}"], 1)

                def evac(u):
                    keys = (units[u][1] + 1) * P
                    act.wait_ge(s["m_t"], u + 1)
                    if u >= 2:
                        act.wait_ge(s["m_o"], u - 1)
                    act.activation(pt[:, u % 2, 0:keys], g.bank[4 + u % 2][:, 0:keys], ACT.Copy).then_inc(s["m_pt"], 1)

                def out(u):
                    h, i = units[u]
                    act.wait_ge(s["m_o"], u + 1)
                    act.activation(y[:, i, h * DV_W:(h + 1) * DV_W], g.bank[6 + u % 2][:, 0:DV_W], ACT.Copy).then_inc(s["m_y"], 1)
                exps(0)
                for u in range(N):
                    if u + 1 < N:
                        exps(u + 1)
                    evac(u)
                    if u:
                        out(u - 1)
                out(N - 1)
                act.wait_ge(s["m_sq"], 1)
                act.activation(rms[:, :], ms[:, :], ACT.Sqrt, scale=1.0 / DV_W, bias=g.eps[:, :]).then_inc(s["m_root"], 1)

            @block.vector
            def _(dve):
                step = InOrder(dve, s["m_dve"])
                dve.wait_ge(s["m_par"], 32)
                step(dve.tensor_tensor(prod[:, :, :], lv[:, 0:4:2, :], lv[:, 1:4:2, :], ALU.mult))
                dve.tensor_reduce(dots[:, :], prod[:, :, :], AX_X, ALU.add).then_inc(s["m_lam"], 1)
                dve.wait_ge(s["m_lexp"], 1)
                step(dve.tensor_tensor(nlam[:, 0:1], nlam[:, 1:2], nlam[:, 0:1], ALU.subtract))
                step(dve.tensor_scalar(nlam[:, 0:1], nlam[:, 0:1], LAM0, None, ALU.subtract))

                def maxima(u):
                    keys = (units[u][1] + 1) * P
                    for m in range(2):
                        b = g.bank[2 * m + u % 2]
                        dve.wait_ge(s[f"m_s{m}"], u + 1)
                        step(dve.tensor_tensor(b[:, keys - P:keys], b[:, keys - P:keys], g.causal_neg[:, :], ALU.add))
                        step(dve.tensor_reduce(mx[:, m, u:u + 1], b[:, 0:keys], AX_X, ALU.max))
                        dve.tensor_scalar(nmx[:, m, u:u + 1], mx[:, m, u:u + 1], -RD ** -0.5, None, ALU.mult).then_inc(s["m_max"], 1)

                def combine(u):
                    keys = (units[u][1] + 1) * P
                    dve.wait_ge(s["m_e0"], u + 1)
                    dve.wait_ge(s["m_e1"], u + 1)
                    step(dve.reciprocal(inv[:, :, u:u + 1], tot[:, :, u:u + 1]))
                    step(dve.tensor_tensor(inv[:, 1, u:u + 1], inv[:, 1, u:u + 1], nlam[:, 0:1], ALU.mult))
                    if u >= 2:
                        dve.wait_ge(s["m_t"], u - 1)
                    step(dve.tensor_scalar(diff[:, u % 2, 0:keys], p[:, u % 2, 0, 0:keys], inv[:, 0, u:u + 1], None, ALU.mult))
                    dve.scalar_tensor_tensor(diff[:, u % 2, 0:keys], p[:, u % 2, 1, 0:keys], inv[:, 1, u:u + 1], diff[:, u % 2, 0:keys],
                                             ALU.mult, ALU.add).then_inc(s["m_a"], 1)
                maxima(0)
                for u in range(N):
                    if u + 1 < N:
                        maxima(u + 1)
                    combine(u)
                dve.wait_ge(s["m_y"], N)
                whole = [P, TT, DA_H, DV_W]
                yv = y.rearrange("p i (h w) -> p i h w", w=DV_W)
                sq = k
                step(dve.tensor_tensor(sq, y, y, ALU.mult))
                dve.tensor_reduce(ms[:, :].rearrange("p (i h) -> p i h", h=DA_H), sq.rearrange("p i (h w) -> p i h w", w=DV_W), AX_X, ALU.add).then_inc(s["m_sq"], 1)
                dve.wait_ge(s["m_root"], 1)
                step(dve.reciprocal(rs[:, :], rms[:, :]))
                step(dve.tensor_scalar(gain[:, :], gain[:, :], 1.0 - LAM0, None, ALU.mult))
                step(dve.tensor_tensor(yv, yv, rs[:, :].rearrange("p (i h) -> p i h", h=DA_H).unsqueeze(3).to_broadcast(whole), ALU.mult))
                step(dve.tensor_tensor(yv, yv, gain[:, :].unsqueeze(1).unsqueeze(1).to_broadcast(whole), ALU.mult))


def mlstm(g, tok, mv, conv, mi, mf):
    nc, a = g.nc, g.a
    qt, kt = conv[:, 0:4, :], conv[:, 4:8, :]
    mo = tok[:, :, 3 * BANK:4 * BANK]
    with ExitStack() as ctx:
        def sb(name, shape, dt=F32):
            return ctx.enter_context(nc.sbuf_tensor(name, shape, dt))
        row = [sb(f"ml_row{n}", [ML_H, T]) for n in range(6)]
        sel = sb("ml_sel", [ML_H, ML_H, P])
        key_u = sb("ml_u", [P, TT, ML_H])
        floor = sb("ml_floor", [P, TT, ML_H])
        gap = sb("ml_gap", [P, 2, T])
        sd = sb("ml_sd", [P, 2, TT, T])
        y = sb("ml_y", [P, TT, ML_H, ML_D + 1])
        gain = sb("ml_gain", [P, BANK])
        den, neg, mu, var, rms, rs = (sb(n, [P, TT, ML_H]) for n in ("ml_den", "ml_neg", "ml_mu", "ml_var", "ml_rms", "ml_rs"))
        ones_row, absf, ex, logs, cum, run = row
        with stage(nc, "n_par n_pool n_sel n_abs n_exp n_log n_dve n_u n_m n_em n_em2 n_t n_tc n_mb n_gap n_e n_diag n_s n_sd n_o n_y n_sq n_root n_gate") as (block, s):
            @block.sync
            def _(sp):
                sp.dma_start(gain[:, :], a["ml_norm_g_2"][0:1, :].partition_broadcast(P)).then_inc(s["n_par"], 16)

            @block.gpsimd
            def _(pool):
                step = InOrder(pool, s["n_pool"])
                step(pool.memset(ones_row[:, :], 1.0))
                step(pool.memset(sel[:, :, :], 0.0))
                pool.affine_select(out=sel[:, :, :], in_=sel[:, :, :], compare_op=ALU.not_equal, fill=1.0, base=0,
                                   pattern=[[-1, ML_H], [0, P]], channel_multiplier=1).then_inc(s["n_sel"], 1)
                for h in range(ML_H):
                    for j in range(TT):
                        n = TT * h + j
                        pool.wait_ge(s["n_e"], n + 1)
                        pool.tensor_tensor(sd[:, h % 2, j, 0:P], sd[:, h % 2, j, 0:P], g.causal_t[:, :], ALU.mult).then_inc(s["n_diag"], 1)

            def weigh(dve, n):
                h, j = n // TT, n % TT
                w = T - j * P
                dve.wait_ge(s["n_s"], n + 1)
                dve.wait_ge(s["n_diag"], n + 1)
                at = sd[:, h % 2, j, 0:w]
                dve.scalar_tensor_tensor(at, g.bank[2 + n % 2][:, 0:w], ML_D ** -0.5, at, ALU.mult, ALU.mult).then_inc(s["n_sd"], 1)

            @block.vector
            def _(dve):
                step = InOrder(dve, s["n_dve"])
                dve.wait_ge(s["n_sel"], 1)
                dve.wait_ge(s["n_log"], 1)
                step(dve.tensor_scalar(absf[:, :], mf[:, :], 0.0, None, ALU.min))
                step(dve.tensor_tensor(logs[:, :], absf[:, :], logs[:, :], ALU.subtract))
                step(dve.tensor_tensor_scan(cum[:, :], ones_row[:, :], logs[:, :], 0.0, ALU.mult, ALU.add))
                step(dve.tensor_tensor(ex[:, :], mi[:, :], cum[:, :], ALU.subtract))
                step(dve.tensor_tensor_scan(run[:, :], ones_row[:, :], ex[:, :], 0.0, ALU.mult, ALU.max))
                dve.tensor_tensor(cum[:, :], cum[:, :], run[:, :], ALU.add).then_inc(s["n_m"], 1)
                dve.wait_ge(s["n_tc"], 2)
                for h in range(ML_H):
                    for j in range(TT):
                        n = TT * h + j
                        w = T - j * P
                        dve.wait_ge(s["n_mb"], h + 1)
                        if n >= 2:
                            dve.wait_ge(s["n_e"], n - 1)
                        dve.tensor_scalar(gap[:, n % 2, 0:w], g.bank[h % 2][:, j * P:T], key_u[:, j, h:h + 1], 0.0, ALU.subtract, ALU.max).then_inc(s["n_gap"], 1)
                        if n:
                            weigh(dve, n - 1)
                weigh(dve, ML_H * TT - 1)
                dve.wait_ge(s["n_y"], 2 * ML_H)
                whole = [P, TT, ML_H, ML_D]
                num = y[:, :, :, 0:ML_D]
                step(dve.tensor_scalar(neg[:], y[:, :, :, ML_D:ML_D + 1].rearrange("p i h o -> p i (h o)"), -1.0, None, ALU.mult))
                step(dve.tensor_tensor(den[:], neg[:], y[:, :, :, ML_D:ML_D + 1].rearrange("p i h o -> p i (h o)"), ALU.max))
                step(dve.tensor_tensor(den[:], den[:], floor[:], ALU.max))
                step(dve.reciprocal(neg[:], den[:]))
                step(dve.tensor_tensor(num, num, neg[:].unsqueeze(3).to_broadcast(whole), ALU.mult))
                step(dve.tensor_reduce(mu[:], num, AX_X, ALU.add))
                step(dve.tensor_scalar(mu[:], mu[:], 1.0 / ML_D, None, ALU.mult))
                step(dve.tensor_tensor(num, num, mu[:].unsqueeze(3).to_broadcast(whole), ALU.subtract))
                sq = sd[:, 0].rearrange("p i (h w) -> p i h w", w=ML_D)
                step(dve.tensor_tensor(sq, num, num, ALU.mult))
                dve.tensor_reduce(var[:], sq, AX_X, ALU.add).then_inc(s["n_sq"], 1)
                dve.wait_ge(s["n_root"], 1)
                step(dve.reciprocal(rs[:], rms[:]))
                step(dve.tensor_tensor(num, num, rs[:].unsqueeze(3).to_broadcast(whole), ALU.mult))
                dve.wait_ge(s["n_par"], 16)
                step(dve.tensor_tensor(num, num, gain[:, :].rearrange("p (h w) -> p h w", w=ML_D).unsqueeze(1).to_broadcast(whole), ALU.mult))
                dve.wait_ge(s["n_gate"], 1)
                mo4 = mo.rearrange("p i (h w) -> p i h w", w=ML_D)
                step(dve.tensor_tensor(mo4, num, mo4, ALU.mult))

            def outs(act, h):
                for b in range(2):
                    act.wait_ge(s["n_o"], 2 * h + b + 1)
                    act.activation(y[:, 2 * b:2 * b + 2, h, :], g.bank[4 + 2 * (h % 2) + b][:, 0:2 * (ML_D + 1)].rearrange("p (i w) -> p i w", w=ML_D + 1),
                                   ACT.Copy).then_inc(s["n_y"], 1)

            @block.scalar
            def _(act):
                act.activation(absf[:, :], mf[:, :], ACT.Abs).then_inc(s["n_abs"], 1)
                act.wait_ge(s["n_abs"], 1)
                act.activation(ex[:, :], absf[:, :], ACT.Exp, scale=-1.0).then_inc(s["n_exp"], 1)
                act.wait_ge(s["n_exp"], 1)
                act.activation(logs[:, :], ex[:, :], ACT.Ln, bias=g.ones[0:ML_H, 0:1]).then_inc(s["n_log"], 1)
                act.wait_ge(s["n_m"], 1)
                act.activation(cum[:, :], cum[:, :], ACT.Exp, scale=-1.0).then_inc(s["n_em"], 1)
                act.wait_ge(s["n_t"], 1)
                act.activation(key_u[:], g.bank[4][:, 0:TT * ML_H].rearrange("p (i h) -> p i h", h=ML_H), ACT.Copy).then_inc(s["n_tc"], 1)
                act.activation(floor[:], g.bank[4][:, 256:256 + TT * ML_H].rearrange("p (i h) -> p i h", h=ML_H), ACT.Copy).then_inc(s["n_tc"], 1)
                for h in range(ML_H):
                    for j in range(TT):
                        n = TT * h + j
                        w = T - j * P
                        act.wait_ge(s["n_gap"], n + 1)
                        if h >= 2 and j == 0:
                            act.wait_ge(s["n_o"], 2 * (h - 1))
                        act.activation(sd[:, h % 2, j, 0:w], gap[:, n % 2, 0:w], ACT.Exp, scale=-1.0).then_inc(s["n_e"], 1)
                    if h:
                        outs(act, h - 1)
                outs(act, ML_H - 1)
                act.activation(mo, mo, ACT.Sigmoid).then_inc(s["n_gate"], 1)
                act.wait_ge(s["n_sq"], 1)
                act.activation(rms[:], var[:], ACT.Sqrt, scale=1.0 / ML_D, bias=g.eps[:, :]).then_inc(s["n_root"], 1)

            @block.tensor
            def _(pe):
                pe.wait_ge(s["n_em"], 1)
                for i in range(TT):
                    pe.transpose(g.bank[4][:, i * ML_H:(i + 1) * ML_H], ex[:, i * P:(i + 1) * P], g.ident[0:ML_H, 0:ML_H])
                    last = pe.transpose(g.bank[4][:, 256 + i * ML_H:256 + (i + 1) * ML_H], cum[:, i * P:(i + 1) * P], g.ident[0:ML_H, 0:ML_H])
                last.then_inc(s["n_t"], 1)

                def rows(h):
                    if h >= 2:
                        pe.wait_ge(s["n_gap"], TT * (h - 1))
                    pe.matmul(g.bank[h % 2][:, :], sel[:, h, :], run[:, :], start=True, stop=True).then_inc(s["n_mb"], 1)

                def sums(h):
                    pe.wait_ge(s["n_sd"], TT * (h + 1))
                    if h >= 2:
                        pe.wait_ge(s["n_y"], 2 * (h - 1))
                    for b in range(2):
                        for i in (2 * b, 2 * b + 1):
                            for j in range(i + 1):
                                last = pe.matmul(g.bank[4 + 2 * (h % 2) + b][:, (i % 2) * (ML_D + 1):(i % 2 + 1) * (ML_D + 1)],
                                                 sd[:, h % 2, j, (i - j) * P:(i - j + 1) * P], mv[:, j, h, :], start=(j == 0), stop=(j == i))
                        last.then_inc(s["n_o"], 1)
                rows(0)
                rows(1)
                pe.wait_ge(s["n_tc"], 2)
                for h in range(ML_H):
                    for j in range(TT):
                        n = TT * h + j
                        if n >= 2:
                            pe.wait_ge(s["n_sd"], n - 1)
                        pe.matmul(g.bank[2 + n % 2][:, 0:T - j * P], kt[:, h, j * P:(j + 1) * P], qt[:, h, j * P:T], start=True, stop=True).then_inc(s["n_s"], 1)
                    if h + 2 < ML_H:
                        rows(h + 2)
                    if h:
                        sums(h - 1)
                sums(ML_H - 1)


def cross_attention(g, first_unit):
    nc, a = g.nc, g.a
    MT = MEM // P
    base = g.before(first_unit)
    with ExitStack() as ctx:
        def sb(name, shape, dt=F32):
            return ctx.enter_context(nc.sbuf_tensor(name, shape, dt))
        kt = sb("x_kt", [P, DC, MEM])
        v = sb("x_v", [P, MT, D])
        qt = sb("x_qt", [P, DC, T])
        with ExitStack() as local:
            mem_t = local.enter_context(nc.sbuf_tensor("mem_t", [P, DC, MEM], F32))
            with ExitStack() as inner:
                mem = inner.enter_context(nc.sbuf_tensor("mem_sb", [P, MT, D], F32))
                with stage(nc, "o_mem") as (block, s):
                    @block.sync
                    def _(sp):
                        sp.dma_start(mem[:, :, :], a["mem_2"][0].rearrange("(i p) d -> p i d", p=P)).then_inc(s["o_mem"], 16)
                        sp.wait_ge(s["o_mem"], 16)
                norm_transposed(g, None, None, inner, source=mem, gain_src=a["norm_mem_g_2"][0], tiles=MT, dst=mem_t)
            with ExitStack() as inner:
                norm_transposed(g, None, None, inner, gain_src=a["norm_x_g_2"][0])
            with stage(nc, "p_out") as (block, s):
                @block.sync
                def _(sp):
                    g.prefetch(sp, first_unit + 6 + RING)

                @block.tensor
                def _(pe):
                    n = 0
                    for u in range(6):
                        w = g.weights(pe, first_unit + u)
                        for m in range(4 if u < 4 else MT):
                            if n >= 8:
                                pe.wait_ge(s["p_out"], n - 7)
                            for k in range(DC):
                                if u < 2:
                                    last = pe.matmul(g.bank[n % 8][:, :], w[:, k, m * P:(m + 1) * P], g.ht[:, k, :], start=(k == 0), stop=(k == DC - 1))
                                elif u < 4:
                                    last = pe.matmul(g.bank[n % 8][:, 0:MEM], w[:, k, m * P:(m + 1) * P], mem_t[:, k, :], start=(k == 0), stop=(k == DC - 1))
                                else:
                                    last = pe.matmul(g.bank[n % 8][:, :], mem_t[:, k, m * P:(m + 1) * P], w[:, k, :], start=(k == 0), stop=(k == DC - 1))
                            last.then_inc(g.dense, 1)
                            n += 1

                @block.scalar
                def _(act):
                    n = 0
                    for u in range(6):
                        for m in range(4 if u < 4 else MT):
                            act.wait_ge(g.dense, base + n + 1)
                            if u < 2:
                                dst, src = qt[:, 4 * u + m, :], g.bank[n % 8][:, :]
                            elif u < 4:
                                dst, src = kt[:, 4 * (u - 2) + m, :], g.bank[n % 8][:, 0:MEM]
                            else:
                                dst, src = v[:, m, (u - 4) * BANK:(u - 3) * BANK], g.bank[n % 8][:, :]
                            act.activation(dst, src, ACT.Copy).then_inc(s["p_out"], 1)
                            n += 1
        y = sb("x_y", [P, TT, D])
        units = [([qt[:, 2 * h + c, i * P:(i + 1) * P] for c in range(2)], [kt[:, 2 * h + c, :] for c in range(2)], MEM, False,
                  [v[:, j, h * X_D:(h + 1) * X_D] for j in range(MT)], y[:, i, h * X_D:(h + 1) * X_D])
                 for h in range(X_H) for i in range(TT)]
        with stage(nc, ATTN_SEMS) as (block, s):
            at = Attention(g, ctx, units, X_D ** -0.5, s)

            @block.sync
            def _(sp):
                pass

            @block.tensor
            def _(pe):
                at.pe(pe)

            @block.vector
            def _(dve):
                at.dve(dve)

            @block.scalar
            def _(act):
                at.act(act)
        with ExitStack() as local:
            mix_out(g, lambda k: y[:, :, k * P:(k + 1) * P], first_unit + 6, None, local)


RG = NG + NE


def route(g, xn_tiles, x_rows, table, slot, result, weight, slots, over):
    nc, a = g.nc, g.a
    with ExitStack() as ctx:
        def sb(name, shape, dt=F32):
            return ctx.enter_context(nc.sbuf_tensor(name, shape, dt))
        w = sb("router_w", [P, DC, RG])
        bias = sb("router_b", [P, RG])
        logit = sb("logit", [P, TT, RG])
        gl = sb("group_logit", [P, TT, 8])
        g_top, e_top = sb("g_top", [P, TT, 8]), sb("e_top", [P, TT, 8])
        g_at, e_at = sb("g_at", [P, TT, 8], U32), sb("e_at", [P, TT, 8], U32)
        g_num, e_num = sb("g_num", [P, TT, 1]), sb("e_num", [P, TT, 2])
        ex = sb("g_exp", [P, TT, NG])
        gw, ratio, one_plus = sb("g_w", [P, TT, 1]), sb("ratio", [P, TT, 1]), sb("one_plus", [P, TT, 1])
        pick = sb("pick", [P, TT, NG])
        cross = sb("cross", [P, TT, EG, NG])
        el = sb("e_logit", [P, TT, EG])
        hit = sb("e_hit", [P, 2, TT, NE])
        both = sb("e_both", [P, TT, NE])
        before = sb("strictly_before", [P, P])
        pos = sb("e_pos", [P, TT, NE])
        prod = sb("e_prod", [P, TT, NE])
        place = sb("e_place", [P, TT, 2])
        at_row, blk = sb("e_row", [P, TT, 2]), sb("e_blk", [P, TT, 2])
        token = sb("token", [P, TT])
        token_i = sb("token_i", [P, TT], I32)
        zero = sb("zeros", [P, P])
        rows = sb("list_rows", [P, P])
        count, most = sb("count", [P, NE]), sb("most", [P, 1])
        whole8 = [P, TT, 8]
        with stage(nc, "q_w q_pool q_ready q_zero q_mm q_dve q_pair q_red q_exp q_exp2 q_hits q_pos q_slot q_sent q_clear q_rows q_flip q_x") as (block, s):
            @block.sync
            def _(sp):
                sp.dma_start(w[:, :, 0:NG], a["w_router_group_2"][0].rearrange("(k p) n -> p k n", p=P)).then_inc(s["q_w"], 16)
                sp.dma_start(w[:, :, NG:RG], a["w_router_expert_2"][0].rearrange("(k p) n -> p k n", p=P)).then_inc(s["q_w"], 16)
                sp.dma_start(bias[:, 0:NG], a["b_router_group_2"][0:1, :].partition_broadcast(P)).then_inc(s["q_w"], 16)
                sp.dma_start(bias[:, NG:RG], a["b_router_expert_2"][0:1, :].partition_broadcast(P)).then_inc(s["q_w"], 16)
                sp.dma_start(x_rows.rearrange("(i p) d -> p i d", p=P), xn_tiles[:, :, :]).then_inc(s["q_x"], 16)
                sp.wait_ge(s["q_zero"], 1)
                sp.dma_start(table.rearrange("(r p) o -> r (p o)", p=P), zero[:, :]).then_inc(s["q_clear"], 16)
                sp.wait_ge(s["q_sent"], 16 * 2 * TT)
                sp.dma_start(rows[:, :], table.rearrange("(r p) o -> r (p o)", p=P)).then_inc(s["q_rows"], 16)
                sp.wait_ge(s["q_x"], 16)

            @block.gpsimd
            def _(pool):
                step = InOrder(pool, s["q_pool"])
                pool.memset(zero[:, :], 0.0).then_inc(s["q_zero"], 1)
                step(pool.memset(gl[:, :, :], LOW))
                step(pool.iota(token_i[:, :], pattern=[[P, TT]], base=0, channel_multiplier=1))
                step(pool.tensor_copy(token[:, :], token_i[:, :]))
                pool.tensor_tensor(before[:, :], g.causal_t[:, :], g.ident[:, :], ALU.subtract).then_inc(s["q_ready"], 1)
                pool.wait_ge(s["q_slot"], 1)
                pool.wait_ge(s["q_clear"], 16)
                for i in range(TT):
                    for c in range(2):
                        pool.indirect_dma_start(out=table, out_offset=bass.IndirectOffsetOnAxis(ap=slot[:, c, i:i + 1], axis=0),
                                                in_=token[:, i:i + 1], in_offset=None).then_inc(s["q_sent"], 16)

            @block.tensor
            def _(pe):
                pe.wait_ge(s["q_w"], 64)
                for i in range(TT):
                    for k in range(DC):
                        last = pe.matmul(g.bank[0][:, i * 64:i * 64 + RG], g.ht[:, k, i * P:(i + 1) * P], w[:, k, :], start=(k == 0), stop=(k == DC - 1))
                last.then_inc(s["q_mm"], 1)
                pe.wait_ge(s["q_hits"], 1)
                pe.wait_ge(s["q_ready"], 1)
                for i in range(TT):
                    for j in range(i + 1):
                        pe.matmul(g.bank[1][:, i * NE:(i + 1) * NE], before[:, :] if j == i else g.ones[:, :], both[:, j, :],
                                  start=(j == 0), stop=(j == i))
                for j in range(TT):
                    last = pe.matmul(g.bank[1][:, TT * NE:(TT + 1) * NE], g.ones[:, :], both[:, j, :], start=(j == 0), stop=(j == TT - 1))
                last.then_inc(s["q_pos"], 1)
                pe.wait_ge(s["q_rows"], 16)
                pe.transpose(g.bank[2][:, 0:P], rows[:, :], g.ident[:, :]).then_inc(s["q_flip"], 1)

            @block.scalar
            def _(act):
                act.wait_ge(s["q_exp"], 1)
                act.activation(ex[:], ex[:], ACT.Exp).then_inc(s["q_exp"], 1)
                act.wait_ge(s["q_exp2"], 1)
                act.activation(ratio[:], ratio[:], ACT.Exp).then_inc(s["q_exp2"], 1)

            @block.vector
            def _(dve):
                step = InOrder(dve, s["q_dve"])
                dve.wait_ge(s["q_mm"], 1)
                step(dve.tensor_tensor(logit[:], g.bank[0][:, 0:TT * 64].rearrange("p (i n) -> p i n", n=64)[:, :, 0:RG],
                                       bias[:, :].unsqueeze(1).to_broadcast([P, TT, RG]), ALU.add))
                dve.wait_ge(s["q_ready"], 1)
                step(dve.tensor_copy(gl[:, :, 0:NG], logit[:, :, 0:NG]))
                for i in range(TT):
                    step(dve.max(g_top[:, i, :], gl[:, i, :]))
                    step(dve.max_index(g_at[:, i, :], g_top[:, i, :], gl[:, i, :]))
                dve.tensor_tensor(ex[:], logit[:, :, 0:NG], g_top[:, :, 0:1].to_broadcast([P, TT, NG]), ALU.subtract).then_inc(s["q_exp"], 1)
                step(dve.tensor_copy(g_num[:], g_at[:, :, 0:1]))
                step(dve.tensor_tensor(pick[:], g.iota_p[:, 0:NG].unsqueeze(1).to_broadcast([P, TT, NG]), g_num[:].to_broadcast([P, TT, NG]), ALU.is_equal))
                step(dve.tensor_tensor(cross[:], logit[:, :, NG:RG].rearrange("p i (g e) -> p i e g", e=EG),
                                       pick[:].unsqueeze(2).to_broadcast([P, TT, EG, NG]), ALU.mult))
                step(dve.tensor_reduce(el[:], cross[:], AX_X, ALU.add))
                for i in range(TT):
                    step(dve.max(e_top[:, i, :], el[:, i, :]))
                    step(dve.max_index(e_at[:, i, :], e_top[:, i, :], el[:, i, :]))
                dve.tensor_tensor(ratio[:], e_top[:, :, 1:2], e_top[:, :, 0:1], ALU.subtract).then_inc(s["q_exp2"], 1)
                step(dve.tensor_copy(e_num[:], e_at[:, :, 0:2]))
                step(dve.scalar_tensor_tensor(e_num[:], g_num[:].to_broadcast([P, TT, 2]), float(EG), e_num[:], ALU.mult, ALU.add))
                for c in range(2):
                    step(dve.tensor_tensor(hit[:, c], g.iota_p[:, 0:NE].unsqueeze(1).to_broadcast([P, TT, NE]),
                                           e_num[:, :, c:c + 1].to_broadcast([P, TT, NE]), ALU.is_equal))
                dve.tensor_tensor(both[:], hit[:, 0], hit[:, 1], ALU.add).then_inc(s["q_hits"], 1)
                dve.wait_ge(s["q_exp"], 2)
                step(dve.tensor_reduce(gw[:].rearrange("p i o -> p (i o)"), ex[:], AX_X, ALU.add))
                dve.wait_ge(s["q_exp2"], 2)
                step(dve.tensor_scalar(one_plus[:], ratio[:], 1.0, None, ALU.add))
                step(dve.tensor_tensor(one_plus[:], one_plus[:], gw[:], ALU.mult))
                step(dve.reciprocal(weight[:, :, 0:1], one_plus[:]))
                step(dve.tensor_tensor(weight[:, :, 1:2], weight[:, :, 0:1], ratio[:], ALU.mult))
                dve.wait_ge(s["q_pos"], 1)
                step(dve.tensor_copy(pos[:], g.bank[1][:, 0:TT * NE].rearrange("p (i e) -> p i e", e=NE)))
                step(dve.tensor_copy(count[:, :], g.bank[1][:, TT * NE:(TT + 1) * NE]))
                for c in range(2):
                    step(dve.tensor_tensor(prod[:], hit[:, c], pos[:], ALU.mult))
                    step(dve.tensor_reduce(place[:, :, c:c + 1].rearrange("p i o -> p (i o)"), prod[:], AX_X, ALU.add))
                step(dve.tensor_copy(at_row[:], place[:]))
                step(dve.scalar_tensor_tensor(place[:], e_num[:], float(CAP), place[:], ALU.mult, ALU.add))
                dve.tensor_copy(slot[:, :, :], place[:].rearrange("p i c -> p c i")).then_inc(s["q_slot"], 1)
                step(dve.tensor_scalar(blk[:], at_row[:], float(P), None, ALU.is_ge))
                for b in range(2, CAP // P):
                    step(dve.scalar_tensor_tensor(blk[:], at_row[:], float(b * P), blk[:], ALU.is_ge, ALU.add))
                step(dve.scalar_tensor_tensor(at_row[:], blk[:], float((NE - 1) * P), at_row[:], ALU.mult, ALU.add))
                step(dve.scalar_tensor_tensor(at_row[:], e_num[:], float(P), at_row[:], ALU.mult, ALU.add))
                step(dve.tensor_copy(result[:, :, :], at_row[:].rearrange("p i c -> p c i")))
                step(dve.tensor_reduce(most[:, :], count[:, :], AX_X, ALU.max))
                step(dve.tensor_scalar(most[:, :], most[:, :], float(P), None, ALU.is_gt))
                step(dve.tensor_copy(over[:, :], most[:, :]))
                dve.wait_ge(s["q_flip"], 1)
                step(dve.tensor_copy(slots[:, :], g.bank[2][:, 0:P]))


MOE_SEMS = (" r_w1_0 r_w1_1 r_w3_0 r_w3_1 r_w2_0 r_w2_1 r_x0 r_x1 r_st0 r_st1 r_paced r_idx r_xt r_xc r_h1 r_h3"
            " r_act r_z r_zt r_zc r_y r_yc")


class Experts:

    def __init__(self, g, ctx, s, w13, w2, slots, x_rows, y_rows, gain):
        self.g, self.s, self.w13, self.w2, self.slots = g, s, w13, w2, slots
        self.x_rows, self.y_rows, self.gain = x_rows, y_rows, gain

        def sb(name, shape, dt=F32):
            return ctx.enter_context(g.nc.sbuf_tensor(fresh(name), shape, dt))
        self.idx = sb("moe_idx", [P, 2], U32)
        self.rows = sb("moe_rows", [P, 2, D])
        self.xt = sb("moe_xt", [P, 2, DC, P])
        self.sil = sb("moe_silu", [P, 2, FE])
        self.z = sb("moe_z", [P, 2, FE])
        self.zt = sb("moe_zt", [P, 2, FC, P])
        self.y = sb("moe_y", [P, 2, D])

    def load(self, sp, e, n, par, first):
        s, a = self.s, self.g.a
        if not first:
            sp.wait_ge(s["r_h1"], n - 1)
        sp.dma_start(self.w13[par][0][:, :, :], a["w1_2"][0][bass.ds(e, 1)].rearrange("o (k p) n -> p (o k) n", p=P)).then_inc(s[f"r_w1_{par}"], 16)
        if not first:
            sp.wait_ge(s["r_h3"], n - 1)
        sp.dma_start(self.w13[par][1][:, :, :], a["w3_2"][0][bass.ds(e, 1)].rearrange("o (k p) n -> p (o k) n", p=P)).then_inc(s[f"r_w3_{par}"], 16)
        if not first:
            sp.wait_ge(s["r_y"], 2 * (n - 1))
        sp.dma_start(self.w2[par][:, :].rearrange("p (k n) -> p k n", k=FC), a["w2_2"][0][bass.ds(e, 1)].rearrange("o (k p) n -> p (o k) n", p=P)).then_inc(s[f"r_w2_{par}"], 16)

    def gather(self, pool, col, n, par, half, first):
        s = self.s
        if not first:
            pool.wait_ge(s[f"r_x{par}"], half * 16)
            pool.wait_ge(s["r_xt"], 2 * (n - 1))
        pool.tensor_copy(self.idx[:, par:par + 1], self.slots[:, bass.ds(col, 1)]).then_inc(s["r_idx"], 1)
        pool.wait_ge(s["r_idx"], n + 1)
        pool.sem_inc(s["r_paced"], 1)
        pool.indirect_dma_start(out=self.rows[:, par, :], out_offset=None, in_=self.x_rows,
                                in_offset=bass.IndirectOffsetOnAxis(ap=self.idx[:, par:par + 1], axis=0)).then_inc(s[f"r_x{par}"], 16)

    def flip_rows(self, pe, n, par, half, first):
        s, g = self.s, self.g
        pe.wait_ge(s[f"r_x{par}"], (half + 1) * 16)
        for b in range(2):
            if not first:
                pe.wait_ge(s["r_xc"], 2 * (n - 1) + b + 1)
            for k in range(4):
                last = pe.transpose(g.bank[b][:, k * P:(k + 1) * P], self.rows[:, par, (4 * b + k) * P:(4 * b + k + 1) * P], g.ident[:, :])
            last.then_inc(s["r_xt"], 1)

    def up(self, pe, which, n, par, wait, first):
        s, g = self.s, self.g
        pe.wait_ge(s[f"r_w{which}_{par}"], wait)
        pe.wait_ge(s["r_xc"], 2 * n + 2)
        if not first:
            pe.wait_ge(s["r_act"] if which == 1 else s["r_z"], n)
        for k in range(DC):
            last = pe.matmul(g.bank[2 if which == 1 else 3][:, :], self.xt[:, par, k, :], self.w13[par][0 if which == 1 else 1][:, k, :],
                             start=(k == 0), stop=(k == DC - 1))
        last.then_inc(s[f"r_h{which}"], 1)

    def flip_z(self, pe, n, par, first):
        s, g = self.s, self.g
        pe.wait_ge(s["r_z"], n + 1)
        if not first:
            pe.wait_ge(s["r_zc"], n)
        for k in range(FC):
            last = pe.transpose(g.bank[4][:, k * P:(k + 1) * P], self.z[:, par, k * P:(k + 1) * P], g.ident[:, :])
        last.then_inc(s["r_zt"], 1)

    def down(self, pe, n, par, wait, first):
        s, g = self.s, self.g
        pe.wait_ge(s[f"r_w2_{par}"], wait)
        pe.wait_ge(s["r_zc"], n + 1)
        for c in range(2):
            if not first:
                pe.wait_ge(s["r_yc"], 2 * (n - 1) + c + 1)
            for k in range(FC):
                last = pe.matmul(g.bank[5 + c][:, :], self.zt[:, par, k, :], self.w2[par][:, k * D + c * BANK:k * D + (c + 1) * BANK],
                                 start=(k == 0), stop=(k == FC - 1))
            last.then_inc(s["r_y"], 1)

    def act_front(self, act, n, par, early):
        s, g = self.s, self.g
        act.wait_ge(s["r_h1"], n + 1)
        if not early:
            act.wait_ge(s["r_z"], n - 1)
        act.activation(self.sil[:, par, :], g.bank[2][:, :], ACT.Silu).then_inc(s["r_act"], 1)

    def act_back(self, act, n, par, half, early):
        s, g = self.s, self.g
        act.wait_ge(s["r_zt"], n + 1)
        if not early:
            act.wait_ge(s["r_y"], 2 * (n - 1))
        act.activation(self.zt[:, par, :, :].rearrange("p k t -> p (k t)"), g.bank[4][:, :], ACT.Copy).then_inc(s["r_zc"], 1)
        if not early:
            act.wait_ge(s[f"r_st{par}"], half * 16)
        for c in range(2):
            act.wait_ge(s["r_y"], 2 * n + c + 1)
            act.activation(self.y[:, par, c * BANK:(c + 1) * BANK], g.bank[5 + c][:, :], ACT.Copy).then_inc(s["r_yc"], 1)

    def dve_rows(self, dve, n, par, early):
        s, g = self.s, self.g
        if not early:
            dve.wait_ge(s["r_h3"], n - 1)
        for b in range(2):
            dve.wait_ge(s["r_xt"], 2 * n + b + 1)
            dve.tensor_tensor(self.xt[:, par, 4 * b:4 * b + 4, :], g.bank[b][:, :].rearrange("p (k t) -> p k t", t=P),
                              self.gain[:, 4 * b:4 * b + 4].unsqueeze(2).to_broadcast([P, 4, P]), ALU.mult).then_inc(s["r_xc"], 1)

    def dve_gate(self, dve, n, par, early):
        s, g = self.s, self.g
        dve.wait_ge(s["r_act"], n + 1)
        dve.wait_ge(s["r_h3"], n + 1)
        if not early:
            dve.wait_ge(s["r_zt"], n - 1)
        dve.tensor_tensor(self.z[:, par, :], g.bank[3][:, :], self.sil[:, par, :], ALU.mult).then_inc(s["r_z"], 1)

    def store(self, q, row, n, par):
        s = self.s
        q.wait_ge(s["r_yc"], 2 * n + 2)
        q.dma_start(self.y_rows[bass.ds(row, P), :], self.y[:, par, :]).then_inc(s[f"r_st{par}"], 16)


def run_experts(g, w13, w2, slots, x_rows, y_rows, gain):
    nc = g.nc
    BLOCKS = CAP // P
    PEEL = 4
    with ExitStack() as ctx, stage(nc, MOE_SEMS) as (block, s):
        m = Experts(g, ctx, s, w13, w2, slots, x_rows, y_rows, gain)

        @block.sync
        def _(sp):
            for n in range(PEEL):
                m.load(sp, n, n, n % 2, n < 2)
            with sp.Fori(PEEL // 2, NE // 2) as it:
                for par in range(2):
                    m.load(sp, it * 2 + par, it * 2 + par, par, False)

        @block.gpsimd
        def _(pool):
            for n in range(PEEL):
                m.gather(pool, n * BLOCKS, n, n % 2, n // 2, n < 2)
            with pool.Fori(PEEL // 2, NE // 2) as it:
                for par in range(2):
                    n = it * 2 + par
                    m.gather(pool, n * BLOCKS, n, par, it, False)

        def products(pe, n, par, half, first, one, last):
            m.up(pe, 1, n, par, (half + 1) * 16, first)
            if not first:
                m.flip_z(pe, n - 1, 1 - par, one)
            m.up(pe, 3, n, par, (half + 1) * 16, first)
            if not last:
                m.flip_rows(pe, n + 1, 1 - par, half + par, False)
            if not first:
                m.down(pe, n - 1, 1 - par, (half + par) * 16, one)

        @block.tensor
        def _(pe):
            m.flip_rows(pe, 0, 0, 0, True)
            for n in range(PEEL):
                products(pe, n, n % 2, n // 2, n == 0, n == 1, False)
            with pe.Fori(PEEL // 2, NE // 2 - 1) as it:
                for par in range(2):
                    products(pe, it * 2 + par, par, it, False, False, False)
            for n in (NE - 2, NE - 1):
                products(pe, n, n % 2, n // 2, False, False, n == NE - 1)
            m.flip_z(pe, NE - 1, 1, False)
            m.down(pe, NE - 1, 1, NE // 2 * 16, False)

        def act_block(act, n, par, half, early, before_early, first):
            m.act_front(act, n, par, early)
            if not first:
                m.act_back(act, n - 1, 1 - par, half + par - 1, before_early)
                m.store(act, (n - 1) * P, n - 1, 1 - par)

        @block.scalar
        def _(act):
            for n in range(PEEL):
                act_block(act, n, n % 2, n // 2, n < 2, n - 1 < 2, n == 0)
            with act.Fori(PEEL // 2, NE // 2) as it:
                for par in range(2):
                    act_block(act, it * 2 + par, par, it, False, False, False)
            m.act_back(act, NE - 1, 1, NE // 2 - 1, False)
            m.store(act, (NE - 1) * P, NE - 1, 1)
            for par in range(2):
                act.wait_ge(s[f"r_st{par}"], NE // 2 * 16)

        @block.vector
        def _(dve):
            m.dve_rows(dve, 0, 0, True)
            for n in range(1, PEEL):
                m.dve_rows(dve, n, n % 2, n < 2)
                m.dve_gate(dve, n - 1, 1 - n % 2, n - 1 < 2)
            with dve.Fori(PEEL // 2, NE // 2) as it:
                for par in range(2):
                    m.dve_rows(dve, it * 2 + par, par, False)
                    m.dve_gate(dve, it * 2 + par - 1, 1 - par, False)
            m.dve_gate(dve, NE - 1, 1, False)


def run_overflow(g, over, w13, w2, slots, x_rows, y_rows, gain):
    nc = g.nc
    BLOCKS = CAP // P
    MORE = BLOCKS - 1
    with ExitStack() as ctx, stage(nc, MOE_SEMS) as (block, s):
        m = Experts(g, ctx, s, w13, w2, slots, x_rows, y_rows, gain)

        def guarded(eng, body):
            flag = eng.value_load(over[0:1, 0:1], min_val=0, max_val=1)
            with eng.If(flag > 0):
                body(eng)
            with eng.Else():
                eng.nop()
            eng.nop()

        def blocks(eng, each):
            with eng.Fori(0, NE) as e:
                for r in range(MORE):
                    each(e, r, e * MORE + r, e * BLOCKS + r + 1)

        def load(sp):
            with sp.Fori(0, NE) as e:
                sp.wait_ge(s["r_st0"], (e * MORE + 1) * 16)
                m.load(sp, e, e, 0, True)

        def gather(pool):
            pool.sem_inc(s["r_st0"], 16)

            def each(e, r, n, col):
                pool.wait_ge(s["r_st0"], (n + 1) * 16)
                m.gather(pool, col, n, 0, n, True)
            blocks(pool, each)

        def products(pe):
            def each(e, r, n, col):
                m.flip_rows(pe, n, 0, n, True)
                m.up(pe, 1, n, 0, (e + 1) * 16, True)
                m.up(pe, 3, n, 0, (e + 1) * 16, True)
                m.flip_z(pe, n, 0, True)
                m.down(pe, n, 0, (e + 1) * 16, True)
            blocks(pe, each)

        def activations(act):
            def each(e, r, n, col):
                m.act_front(act, n, 0, True)
                m.act_back(act, n, 0, n, True)
                m.store(act, e * P + (r + 1) * NE * P, n, 0)
            blocks(act, each)
            act.wait_ge(s["r_st0"], (NE * MORE + 1) * 16)

        def gates(dve):
            def each(e, r, n, col):
                m.dve_rows(dve, n, 0, True)
                m.dve_gate(dve, n, 0, True)
            blocks(dve, each)

        @block.sync
        def _(sp):
            guarded(sp, load)

        @block.gpsimd
        def _(pool):
            guarded(pool, gather)

        @block.tensor
        def _(pe):
            guarded(pe, products)

        @block.scalar
        def _(act):
            guarded(act, activations)

        @block.vector
        def _(dve):
            guarded(dve, gates)


def finish(g, result, weight, y_rows, over, out):
    nc, a = g.nc, g.a
    with ExitStack() as ctx:
        def sb(name, shape, dt=F32):
            return ctx.enter_context(nc.sbuf_tensor(name, shape, dt))
        got = sb("got", [P, 4, D])
        sq = sb("out_sq", [P, TT, D])
        res = sb("out_rows", [P, TT, D])
        gain = sb("out_gain", [P, D])
        ss, rms, rs = (sb(n, [P, TT]) for n in ("out_ss", "out_rms", "out_rs"))
        with stage(nc, "t_gain t_g0 t_g1 t_g2 t_g3 t_add t_sq t_root t_rs t_out t_stored") as (block, s):
            @block.sync
            def _(sp):
                sp.dma_start(gain[:, :], a["norm_final_g_2"].unsqueeze(0).partition_broadcast(P)).then_inc(s["t_gain"], 16)
                rows = out[0].rearrange("(i p) d -> p i d", p=P)
                for i in range(TT):
                    sp.wait_ge(s["t_out"], i + 1)
                    sp.dma_start(rows[:, i, :], res[:, i, :]).then_inc(s["t_stored"], 16)
                sp.wait_ge(s["t_stored"], 16 * TT)

            @block.gpsimd
            def _(pool):
                def gather(rows):
                    for n in range(2 * TT):
                        if n >= 4:
                            pool.wait_ge(s["t_add"], n - 3)
                        i, c = n // 2, n % 2
                        pool.indirect_dma_start(out=got[:, n % 4, :], out_offset=None, in_=rows,
                                                in_offset=bass.IndirectOffsetOnAxis(ap=result[:, c, i:i + 1], axis=0)).then_inc(s[f"t_g{n % 4}"], 16)
                flag = pool.value_load(over[0:1, 0:1], min_val=0, max_val=1)
                with pool.If(flag > 0):
                    gather(y_rows)
                with pool.Else():
                    gather(y_rows[0:NE * P, :])
                pool.nop()

            @block.vector
            def _(dve):
                for n in range(2 * TT):
                    i, c = n // 2, n % 2
                    dve.wait_ge(s[f"t_g{n % 4}"], 16 * (n // 4 + 1))
                    if n:
                        dve.wait_ge(s["t_add"], n)
                    dve.scalar_tensor_tensor(g.x[:, i, :], got[:, n % 4, :], weight[:, i, c:c + 1], g.x[:, i, :], ALU.mult, ALU.add).then_inc(s["t_add"], 1)
                dve.wait_ge(s["t_gain"], 16)
                for i in range(TT):
                    dve.wait_ge(s["t_root"], i + 1)
                    dve.reciprocal(rs[:, i:i + 1], rms[:, i:i + 1]).then_inc(s["t_rs"], 1)
                    dve.wait_ge(s["t_rs"], i + 1)
                    dve.scalar_tensor_tensor(res[:, i, :], g.x[:, i, :], rs[:, i:i + 1], gain[:, :], ALU.mult, ALU.mult).then_inc(s["t_out"], 1)

            @block.scalar
            def _(act):
                for i in range(TT):
                    act.wait_ge(s["t_add"], 2 * i + 2)
                    act.activation(sq[:, i, :], g.x[:, i, :], ACT.Square, accum_out=ss[:, i:i + 1]).then_inc(s["t_sq"], 1)
                    act.wait_ge(s["t_sq"], i + 1)
                    act.activation(rms[:, i:i + 1], ss[:, i:i + 1], ACT.Sqrt, scale=1.0 / D, bias=g.eps[:, :]).then_inc(s["t_root"], 1)


def mixture(g, out):
    nc, a = g.nc, g.a
    table = nc.dram_tensor("lists", (NE * CAP, 1), F32).ap()
    x_rows = nc.dram_tensor("moe_x", (T, D), F32).ap()
    y_rows = nc.dram_tensor("moe_y_rows", (NE * CAP, D), F32).ap()
    with ExitStack() as ctx:
        def sb(name, shape, dt=F32):
            return ctx.enter_context(nc.sbuf_tensor(name, shape, dt))
        slot = sb("slot", [P, 2, TT], U32)
        result = sb("result_row", [P, 2, TT], U32)
        weight = sb("pair_weight", [P, TT, 2])
        slots = sb("slots", [P, P], U32)
        over = sb("over_flag", [P, 1], I32)
        gain = sb("moe_gain", [P, DC])
        with ExitStack() as local:
            xn = local.enter_context(nc.sbuf_tensor("moe_xn", [P, TT, D], F32))
            with ExitStack() as inner:
                norm_transposed(g, None, None, inner, gain_src=a["norm_ffn_g_2"][0], keep=xn, gain_keep=gain)
            route(g, xn, x_rows, table, slot, result, weight, slots, over)
        with ExitStack() as local:
            extra = [local.enter_context(nc.sbuf_tensor(f"w2_slot{i}", [P, FC * D], F32)) for i in range(2)]
            w13 = [(g.ring[0], g.ring[1]), (g.ring[2], g.ring[3])]
            run_experts(g, w13, extra, slots, x_rows, y_rows, gain)
            run_overflow(g, over, w13, extra, slots, x_rows, y_rows, gain)
        finish(g, result, weight, y_rows, over, out)


def plan_weights(g):
    a = g.a
    g.plan(a["w_in"][0], 0, C_RQ)
    for i in range(4):
        g.plan(a["w_in"][0], C_RQ + i * BANK, BANK)
    for i in range(2):
        g.plan(a["w_out"][0], i * BANK, BANK)
    for i in range(4):
        g.plan(a["w_query"][0], i * BANK, BANK)
    for c in (W2_MQ, W2_MK, W2_DQ, W2_DK, W2_DV, W2_MO, W2_MV):
        g.plan(a["w_in_2"][0], c, BANK)
    g.plan(a["w_in_2"][0], W2_GATES, 2 * ML_H, 2)
    for i in range(2):
        g.plan(a["w_out_2"][0], i * BANK, BANK)
    for name, groups in (("w_xq_2", 4), ("w_xk_2", 4), ("w_xv_2", MEM // P), ("w_xo_2", TT)):
        for i in range(2):
            g.plan(a[name][0], i * BANK, BANK, groups)


def second_mixer(g, first_unit):
    nc, a = g.nc, g.a
    with ExitStack() as local:
        norm_transposed(g, None, None, local, gain_src=a["norm_mix_g_2"][0])
    with ExitStack() as ctx:
        def sb(name, shape, dt=F32):
            return ctx.enter_context(nc.sbuf_tensor(name, shape, dt))
        tok = sb("tok", [P, TT, 4 * BANK])
        mv = sb("ml_v", [P, TT, ML_H, ML_D + 1])
        with ExitStack() as inner:
            conv = inner.enter_context(nc.sbuf_tensor("conv", [P, 8, T], F32))
            mi = inner.enter_context(nc.sbuf_tensor("ml_i", [ML_H, T], F32))
            mf = inner.enter_context(nc.sbuf_tensor("ml_f", [ML_H, T], F32))
            project_second(g, tok, mv, conv, mi, mf, first_unit)
            differential(g, tok)
            mlstm(g, tok, mv, conv, mi, mf)

        def mixed(k):
            c = k * P if k < 4 else 3 * BANK + (k - 4) * P
            return tok[:, :, c:c + P]
        with ExitStack() as local:
            mix_out(g, mixed, first_unit + 8, None, local)


def build(nc, a):
    PAST.clear()
    NAMED.clear()
    with ExitStack() as ctx:
        ctx.enter_context(nc.allow_non_contiguous_dma(reason="short columns of parameters"))
        g = Core(nc, ctx, a)
        plan_weights(g)
        first = ctx.enter_context(ExitStack())

        def sb(name, shape, dt=F32):
            return first.enter_context(nc.sbuf_tensor(name, shape, dt))
        col = sb("col", [P, 32])
        gate_row = sb("gate_row", [P, 2, D])
        c_act = sb("c_act", [P, DC])
        proj_ctx = ctx.enter_context(ExitStack())
        proj = proj_ctx.enter_context(nc.sbuf_tensor("proj", [P, TT, IN_COLS], F32))
        ada_loaded = [nc.alloc_semaphore(f"ada_loaded{i}") for i in range(ADA_SLOTS)]
        ada_used = nc.alloc_semaphore("ada_used")
        with ExitStack() as early:
            ada_acc = early.enter_context(nc.sbuf_tensor("ada_acc", [P, 6 * D], F32))
            ada_in = early.enter_context(nc.sbuf_tensor("ada_in", [P, ADA_SLOTS, ADA], F32))
            prelude(g, proj, ada_in, ada_acc, c_act, col, ada_loaded, ada_used)
            project(g, proj, ada_in, ada_acc, c_act, col, gate_row, ada_loaded, ada_used)
        g.taken = 5
        retention(g, proj)
        latent_attention(g, proj)

        def mixed(k):
            c = C_RQ + k * P if k < 4 else C_RG + (k - 4) * P
            return proj[:, :, c:c + P]
        with ExitStack() as local:
            mix_out(g, mixed, 5, gate_row[:, 0, :], local)
        with ExitStack() as local:
            norm_transposed(g, col[:, 24:32], col[:, 16:24], local, keep=proj[:, :, 0:D])
        proj_ctx.close()
        gates = nc.dram_tensor("gates_by_key", (PK, PK, T), F32).ap()
        with ExitStack() as peer:
            key1_t, key2_t, gate_t = (peer.enter_context(nc.sbuf_tensor(n, [P, T], F32)) for n in ("key1_t", "key2_t", "gate_t"))
            with ExitStack() as local:
                top_v = local.enter_context(nc.sbuf_tensor("top_v", [P, TT, 2 * PH, TOPK], F32))
                top_i = local.enter_context(nc.sbuf_tensor("top_i", [P, TT, 2 * PH, TOPK], U32))
                top_keys(g, top_v, top_i, 7)
                choose_experts(g, top_v, top_i, key1_t, key2_t, gate_t)
            spread_gates(g, key1_t, key2_t, gate_t, gates)
        with ExitStack() as peer:
            acc = peer.enter_context(nc.sbuf_tensor("peer_acc", [P, TT, D], F32))
            experts(g, gates, acc)
            close_first(g, acc, gate_row[:, 1, :], 0)
        first.close()
        second_mixer(g, 11)
        cross_attention(g, 21)
        mixture(g, a["out"])


def layout(inputs):
    out = dict(inputs)
    out["u_tiles"] = np.ascontiguousarray(out.pop("expert_u")[0].reshape(PK, PK, DC, P).transpose(0, 3, 2, 1))
    out["sub_keys_t"] = np.ascontiguousarray(out.pop("sub_keys")[0].transpose(0, 2, 1))
    return out



def kernel(**inputs):
    import concourse.bacc as bacc
    from concourse.bass_utils import run_bass_kernel_spmd

    arrays = layout({name: np.ascontiguousarray(value) for name, value in inputs.items()})
    nc = bacc.Bacc("TRN2", target_bir_lowering=False, num_devices=1)
    aps, fed = {}, {}
    for name, value in arrays.items():
        fed[f"in_{name}"] = value
        aps[name] = nc.dram_tensor(f"in_{name}", value.shape, mybir.dt.from_np(value.dtype), kind="ExternalInput").ap()
    aps["out"] = nc.dram_tensor("result", (1, T, D), F32, kind="ExternalOutput").ap()
    build(nc, aps)
    r = run_bass_kernel_spmd(nc, [fed], core_ids=[0])
    return r.results[0]["result"]
```

```python
from contextlib import ExitStack, contextmanager

import numpy as np

import concourse.bass as bass
from concourse import mybir

F32 = mybir.dt.float32
F32R = mybir.dt.float32r
I32 = mybir.dt.int32
U32 = mybir.dt.uint32
ALU = mybir.AluOpType
ACT = mybir.ActivationFunctionType
AX_X = mybir.AxisListType.X

P = 128
T = 512
TT = T // P
D = 1024
DC = D // P
EPS = 1e-6
THETA = 10000.0
NEG = -1e30
BANK = 512

HEADS = 8
NOPE, ROPE, VD = 64, 32, 64
QK = NOPE + ROPE
Q_RANK, KV_RANK = 256, 128
C_QL, C_KV, C_KR = 0, 256, 384
C_RQ, C_RK, C_RV, C_RG = 416, 928, 1440, 1952
IN_COLS = 2464
RD = 64
HALF = 32
PH, PK, TOPK = 8, 128, 16

DA_H, DV_W = 4, 128
ML_H, ML_D = 4, 128
CONV = 4
MEM = 256
X_H, X_D = 4, 256
NG, EG = 4, 8
NE = NG * EG
FE = 512
FC = FE // P
CAP = T

RING = 2


class InOrder:

    def __init__(self, eng, done):
        self.eng, self.done, self.count = eng, done, 0

    def __call__(self, ins):
        self.count += 1
        ins.then_inc(self.done, 1)
        self.eng.wait_ge(self.done, self.count)

    def put(self, ins):
        self.count += 1
        ins.then_inc(self.done, 1)
        return self.count

    def need(self, count):
        self.eng.wait_ge(self.done, count)


NAMED = {}


def fresh(name):
    NAMED[name] = NAMED.get(name, 0) + 1
    return f"{name}_{NAMED[name]}"


PAST = []


@contextmanager
def stage(nc, names):
    sems = {n: nc.alloc_semaphore(fresh(n)) for n in names.split()}
    if PAST:
        nc.clear_and_free_semaphores(list(PAST))
    PAST[:] = sems.values()
    with nc.Block() as block:
        yield block, sems


class Core:

    def __init__(self, nc, ctx, a):
        self.nc, self.a = nc, a
        self.bank = [ctx.enter_context(nc.psum_tensor(f"bank{i}", [P, BANK], F32)) for i in range(8)]

        def sb(name, shape, dt=F32):
            return ctx.enter_context(nc.sbuf_tensor(name, shape, dt))

        self.ident = sb("ident", [P, P])
        self.ones = sb("ones", [P, P])
        self.causal_neg = sb("causal_neg", [P, P])
        self.causal_t = sb("causal_t", [P, P])
        self.iota_p = sb("iota_p", [P, P])
        self.diff = sb("diff", [P, T])
        self.eps = sb("eps", [P, 1])
        self.inv_freq = sb("inv_freq", [P, HALF])
        self.cos = sb("cos", [P, 2, TT, HALF])
        self.sin = sb("sin", [P, 2, TT, HALF])
        self.x = sb("x_res", [P, TT, D])
        self.ht = sb("ht", [P, DC, T])
        self.ctx = ctx
        self.ring_loaded = [nc.alloc_semaphore(f"ring_loaded{i}") for i in range(RING)]
        self.dense = nc.alloc_semaphore("dense")
        self.units = []
        self.through = []
        self.loads = 0

    def open_ring(self):
        self.ring_ctx = self.ctx.enter_context(ExitStack())
        self.ring = [self.ring_ctx.enter_context(self.nc.sbuf_tensor(fresh("ring"), [P, DC, BANK], F32)) for _ in range(RING)]
        self.w_hi, self.w_lo = (self.ring_ctx.enter_context(self.nc.sbuf_tensor(fresh(n), [P, DC, BANK], F32R)) for n in ("w_hi", "w_lo"))

    def plan(self, w, c0, cols, groups=TT):
        rows = w.shape[0]
        src = w.rearrange("(k p) n -> p k n", p=P)[:, :, c0:c0 + cols]
        self.units.append((src, rows // P, cols))
        self.through.append((self.through[-1] if self.through else 0) + groups)

    def prefetch(self, sp, upto):
        while self.loads < min(upto, len(self.units)):
            u = self.loads
            src, k, cols = self.units[u]
            if u >= RING:
                sp.wait_ge(self.dense, self.through[u - RING])
            sp.dma_start(self.ring[u % RING][:, 0:k, 0:cols], src).then_inc(self.ring_loaded[u % RING], 16)
            self.loads += 1

    def before(self, u):
        return self.through[u - 1] if u else 0

    def weights(self, pe, u):
        pe.wait_ge(self.ring_loaded[u % RING], 16 * (u // RING + 1))
        return self.ring[u % RING]


class Products:
    SEMS = " z_hhi z_hlo z_whi z_wlo z_first z_used"

    def __init__(self, g, ctx, s, first_unit, groups):
        self.g, self.s, self.first_unit, self.groups = g, s, first_unit, groups
        self.units = groups[-1][0] + 1
        self.h_hi, self.h_lo = (ctx.enter_context(g.nc.sbuf_tensor(fresh(n), [P, DC, T], F32R)) for n in ("ht_hi", "ht_lo"))

    def act_start(self, act, source=None):
        for k in range(DC):
            self.act_chunk(act, 0, k)
            if source is not None:
                act.wait_ge(source, k + 1)
            act.activation(self.h_hi[:, k, :], self.h_source(k, source), ACT.Copy).then_inc(self.s["z_hhi"], 1)

    def h_source(self, k, source):
        return self.g.ht[:, k, :] if source is None else self.g.bank[4 + k % 4][:, :]

    def act_unit(self, act, n):
        if n < self.units:
            for k in range(DC):
                self.act_chunk(act, n, k)

    def act_chunk(self, act, n, k):
        g, s, u = self.g, self.s, self.first_unit + n
        cols = g.units[u][2]
        if k == 0:
            act.wait_ge(g.ring_loaded[u % RING], 16 * (u // RING + 1))
        if n and k < DC - 1:
            act.wait_ge(s["z_used"], (n - 1) * (DC - 1) + k + 1)
        elif n:
            act.wait_ge(g.dense, g.through[u - 1])
        act.activation(g.w_hi[:, k, 0:cols], g.ring[u % RING][:, k, 0:cols], ACT.Copy).then_inc(s["z_whi"], 1)

    def by_dve(self, n, k):
        return n == 0 and k % 2 == 1

    def low(self, eng, n, k):
        g, s, u = self.g, self.s, self.first_unit + n
        eng.wait_ge(s["z_whi"], n * DC + k + 1)
        cols = g.units[u][2]
        eng.tensor_tensor(g.w_lo[:, k, 0:cols], g.ring[u % RING][:, k, 0:cols], g.w_hi[:, k, 0:cols].bitcast(F32),
                          ALU.subtract).then_inc(s["z_first" if self.by_dve(n, k) else "z_wlo"], 1)

    def dve(self, dve, source=None):
        for k in range(DC):
            dve.wait_ge(self.s["z_hhi"], k + 1)
            dve.tensor_tensor(self.h_lo[:, k, :], self.h_source(k, source), self.h_hi[:, k, :].bitcast(F32), ALU.subtract).then_inc(self.s["z_hlo"], 1)
            if self.by_dve(0, k):
                self.low(dve, 0, k)

    def pool(self, pool):
        for n in range(self.units):
            for k in range(DC):
                if not self.by_dve(n, k):
                    self.low(pool, n, k)

    def wait_low(self, pe, n, k):
        if self.by_dve(n, k):
            pe.wait_ge(self.s["z_first"], (k + 1) // 2)
        else:
            pe.wait_ge(self.s["z_wlo"], k // 2 + 1 if n == 0 else DC // 2 + (n - 1) * DC + k + 1)

    def pe(self, pe, n, out):
        g, s = self.g, self.s
        unit, stationary, wc, hc = self.groups[n]
        first = n == 0 or self.groups[n - 1][0] != unit
        final = n == len(self.groups) - 1 or self.groups[n + 1][0] != unit
        for k in range(DC):
            if n == 0:
                pe.wait_ge(s["z_hlo"], k + 1)
            if first:
                self.wait_low(pe, unit, k)
            whi, wlo = g.w_hi[:, k, wc], g.w_lo[:, k, wc]
            hhi, hlo = self.h_hi[:, k, hc], self.h_lo[:, k, hc]
            for m, (w, h) in enumerate(((whi, hhi), (whi, hlo), (wlo, hhi))):
                x, y = (w, h) if stationary else (h, w)
                last = pe.matmul(out, x, y, start=(k == 0 and m == 0), stop=(k == DC - 1 and m == 2))
            if final and k < DC - 1:
                last.then_inc(s["z_used"], 1)
        last.then_inc(g.dense, 1)


def chunk(n):
    return slice(n * P, (n + 1) * P)


WHOLE = slice(0, BANK)


ADA = 1024
ADA_SLOTS = 3


def load_ada(sp, a, ada_in, ada_loaded, ada_used, group):
    for k in range(DC):
        n = DC * group + k
        if n >= ADA_SLOTS:
            sp.wait_ge(ada_used, n - ADA_SLOTS + 1)
        sp.dma_start(ada_in[:, n % ADA_SLOTS, :],
                     a["w_ada"][0, k * P:(k + 1) * P, group * ADA:(group + 1) * ADA]
                     ).then_inc(ada_loaded[n % ADA_SLOTS], 16)


def sum_ada(dve, c_act, ada_in, ada_acc, ada_loaded, ada_used, group):
    acc = ada_acc[:, group * ADA:(group + 1) * ADA]
    for k in range(DC):
        n = DC * group + k
        dve.wait_ge(ada_loaded[n % ADA_SLOTS], 16 * (n // ADA_SLOTS + 1))
        if k == 0:
            dve.tensor_scalar(acc, ada_in[:, n % ADA_SLOTS, :], c_act[:, k:k + 1], None,
                              ALU.mult).then_inc(ada_used, 1)
        else:
            dve.wait_ge(ada_used, n)
            dve.scalar_tensor_tensor(acc, ada_in[:, n % ADA_SLOTS, :], c_act[:, k:k + 1], acc,
                                     ALU.mult, ALU.add).then_inc(ada_used, 1)


def prelude(g, proj, ada_in, ada_acc, c_act, col, ada_loaded, ada_used):
    nc, a = g.nc, g.a
    with ExitStack() as ctx:
        def sb(name, shape, dt=F32):
            return ctx.enter_context(nc.sbuf_tensor(name, shape, dt))
        pos_i = sb("pos_i", [P, TT], I32)
        pos_f = sb("pos_f", [P, 2, TT])
        ang = sb("ang", [P, 2, TT, HALF])
        turn = sb("turn", [P, 2, TT, HALF])
        turn_i = sb("turn_i", [P, 2, TT, HALF], I32)
        over = sb("over", [P, 2, TT, HALF])
        iota_i = sb("iota_i", [P, T], I32)
        c_in = sb("c_in", [P, DC])
        bias = sb("bias", [P, 16])
        gain = sb("gain", [P, DC])
        ss = sb("ss", [P, TT])
        rstd = sb("rstd", [P, TT])
        rms = sb("rms", [P, TT])
        xn = proj[:, :, 0:D]
        with stage(nc, "a_x a_small a_pool a_consts a_dve a_c a_trig a_sq a_rstd a_root a_xn a_xt a_ev a_cols a_col_ready a_ht") as (block, s):
            @block.sync
            def _(sp):
                sp.dma_start(c_in[:, :], a["c"].rearrange("o (k p) -> p (o k)", p=P)).then_inc(s["a_c"], 16)
                sp.dma_start(g.x[:, :, :], a["x"][0].rearrange("(i p) d -> p i d", p=P)).then_inc(s["a_x"], 16)
                load_ada(sp, a, ada_in, ada_loaded, ada_used, 0)
                load_ada(sp, a, ada_in, ada_loaded, ada_used, 1)
                g.prefetch(sp, RING)

            @block.gpsimd
            def _(pool):
                pool.dma_start(pos_i[:, :], a["positions"][0].rearrange("(i p) -> p i", p=P)).then_inc(s["a_small"], 16)
                pool.dma_start(bias[:, :], a["b_ada"][0, 0:2 * D].rearrange("(j p) -> p j", p=P)).then_inc(s["a_small"], 16)
                pool.dma_start(gain[:, :], a["g_norm1"][0].rearrange("(k p) -> p k", p=P)).then_inc(s["a_small"], 16)
                step = InOrder(pool, s["a_pool"])
                for i in range(HALF):
                    f = float(np.float32(THETA) ** np.float32(-2 * i / 64))
                    pool.memset(g.inv_freq[:, i:i + 1], f)
                pool.memset(g.eps[:, :], EPS)
                step(pool.memset(g.ones[:, :], 1.0))
                step(pool.memset(g.ident[:, :], 0.0))
                step(pool.affine_select(out=g.ident[:, :], in_=g.ident[:, :], compare_op=ALU.not_equal,
                                        fill=1.0, base=0, pattern=[[-1, P]], channel_multiplier=1))
                step(pool.memset(g.causal_neg[:, :], 0.0))
                step(pool.affine_select(out=g.causal_neg[:, :], in_=g.causal_neg[:, :], compare_op=ALU.is_ge,
                                        fill=NEG, base=0, pattern=[[-1, P]], channel_multiplier=1))
                step(pool.affine_select(out=g.causal_t[:, :], in_=g.ones[:, :], compare_op=ALU.is_ge,
                                        fill=0.0, base=0, pattern=[[1, P]], channel_multiplier=-1))
                step(pool.iota(iota_i[:, :], pattern=[[1, T]], base=0, channel_multiplier=0))
                step(pool.tensor_copy(g.iota_p[:, :], iota_i[:, 0:P]))
                step(pool.iota(iota_i[:, :], pattern=[[1, T]], base=0, channel_multiplier=-1))
                step(pool.tensor_copy(g.diff[:, :], iota_i[:, :]))
                step(pool.iota(iota_i[:, 0:TT], pattern=[[P, TT]], base=0, channel_multiplier=1))
                step(pool.tensor_copy(pos_f[:, 1, :], iota_i[:, 0:TT]))
                pool.wait_ge(s["a_small"], 48)
                pool.tensor_copy(pos_f[:, 0, :], pos_i[:, :]).then_inc(s["a_consts"], 1)

            @block.vector
            def _(dve):
                step = InOrder(dve, s["a_dve"])
                dve.wait_ge(s["a_consts"], 1)
                two_pi = 2 * np.pi
                c1 = 6.28125
                c2 = float(np.float32(two_pi - c1))
                c3 = float(two_pi - c1 - np.float64(np.float32(two_pi - c1)))
                pi = float(np.nextafter(np.float32(np.pi), np.float32(0)))

                def wrap(v):
                    step(dve.tensor_scalar(over[:], v, pi, two_pi, ALU.is_gt, ALU.mult))
                    step(dve.tensor_tensor(v, v, over[:], ALU.subtract))
                    step(dve.tensor_scalar(over[:], v, -pi, two_pi, ALU.is_lt, ALU.mult))
                    step(dve.tensor_tensor(v, v, over[:], ALU.add))
                    step(dve.tensor_scalar(v, v, pi, -pi, ALU.min, ALU.max))

                step(dve.tensor_tensor(ang[:], pos_f[:].unsqueeze(3).to_broadcast([P, 2, TT, HALF]),
                                       g.inv_freq[:].unsqueeze(1).unsqueeze(1).to_broadcast([P, 2, TT, HALF]), ALU.mult))
                step(dve.tensor_scalar(turn[:], ang[:], 1.0 / two_pi, None, ALU.mult))
                step(dve.tensor_copy(turn_i[:], turn[:]))
                step(dve.tensor_copy(turn[:], turn_i[:]))
                for c in (c1, c2, c3):
                    step(dve.scalar_tensor_tensor(ang[:], turn[:], -c, ang[:], ALU.mult, ALU.add))
                wrap(ang[:])
                step(dve.tensor_scalar(turn[:], ang[:], float(np.pi / 2), None, ALU.add))
                wrap(turn[:])
                dve.tensor_copy(over[:], turn[:]).then_inc(s["a_trig"], 1)
                dve.wait_ge(s["a_root"], 1)
                dve.reciprocal(rstd[:, :], rms[:, :]).then_inc(s["a_rstd"], 1)
                dve.wait_ge(s["a_c"], 17)
                for group in range(2):
                    sum_ada(dve, c_act, ada_in, ada_acc, ada_loaded, ada_used, group)
                dve.wait_ge(s["a_cols"], 1)
                step(dve.tensor_tensor(col[:, 0:16], g.bank[6][:, 0:16], bias[:, :], ALU.add))
                dve.scalar_tensor_tensor(col[:, 8:16], col[:, 8:16], 1.0, gain[:, :], ALU.add,
                                         ALU.mult).then_inc(s["a_col_ready"], 1)

            @block.scalar
            def _(act):
                act.wait_ge(s["a_c"], 16)
                act.activation(c_act[:, :], c_in[:, :], ACT.Silu).then_inc(s["a_c"], 1)
                act.wait_ge(s["a_x"], 16)
                for i in range(TT):
                    act.activation(xn[:, i, :], g.x[:, i, :], ACT.Square, accum_out=ss[:, i:i + 1]).then_inc(s["a_sq"], 1)
                act.wait_ge(s["a_consts"], 1)
                act.wait_ge(s["a_sq"], TT)
                act.activation(rms[:, :], ss[:, :], ACT.Sqrt, scale=1.0 / D, bias=g.eps[:, :]).then_inc(s["a_root"], 1)
                act.wait_ge(s["a_rstd"], 1)
                for i in range(TT):
                    act.activation(xn[:, i, :], g.x[:, i, :], ACT.Copy, scale=rstd[:, i:i + 1]).then_inc(s["a_xn"], 1)
                act.wait_ge(s["a_trig"], 1)
                act.activation(g.sin[:], ang[:], ACT.Sin)
                act.activation(g.cos[:], over[:], ACT.Sin)
                act.wait_ge(s["a_col_ready"], 1)
                for k in range(DC):
                    act.wait_ge(s["a_xt"], k + 1)
                    act.activation(g.ht[:, k, :], g.bank[k % 6][:, :], ACT.Identity, bias=col[:, k:k + 1],
                                   scale=col[:, 8 + k:9 + k]).then_inc(s["a_ev"], 1)

            @block.tensor
            def _(pe):
                pe.wait_ge(s["a_consts"], 1)
                pe.wait_ge(s["a_xn"], TT)

                def flip(k):
                    if k >= 6:
                        pe.wait_ge(s["a_ev"], k - 5)
                    for i in range(TT):
                        last = pe.transpose(g.bank[k % 6][:, i * P:(i + 1) * P], xn[:, i, k * P:(k + 1) * P], g.ident[:, :])
                    last.then_inc(s["a_xt"], 1)
                for k in range(6):
                    flip(k)
                pe.wait_ge(ada_used, 2 * DC)
                for j in range(16):
                    last = pe.matmul(g.bank[6][:, j:j + 1], ada_acc[:, j * P:(j + 1) * P], g.ones[:, 0:1],
                                     start=True, stop=True)
                last.then_inc(s["a_cols"], 1)
                for k in range(6, DC):
                    flip(k)


def project(g, proj, ada_in, ada_acc, c_act, col, gate_row, ada_loaded, ada_used):
    nc, a = g.nc, g.a
    units = [(c0, n) for c0, n in [(0, C_RQ)] + [(C_RQ + i * BANK, BANK) for i in range(4)]]
    with ExitStack() as ctx:
        bias = ctx.enter_context(nc.sbuf_tensor("bias2", [P, 16], F32))
        gain = ctx.enter_context(nc.sbuf_tensor("gain2", [P, DC], F32))
        brow = ada_acc[:, 0:2 * D].rearrange("p (n d) -> p n d", d=D)
        with stage(nc, "b_small b_ev b_cols b_rows b_dve") as (block, s):
            @block.sync
            def _(sp):
                sp.dma_start(bias[:, :], a["b_ada"][0, 3 * D:5 * D].rearrange("(j p) -> p j", p=P)).then_inc(s["b_small"], 16)
                sp.dma_start(gain[:, :], a["g_norm2"][0].rearrange("(k p) -> p k", p=P)).then_inc(s["b_small"], 16)
                for n, c0 in enumerate((2 * D, 5 * D)):
                    sp.dma_start(brow[:, n, :], a["b_ada"][0:1, c0:c0 + D].partition_broadcast(P)).then_inc(s["b_small"], 16)
                for group in range(2, 6):
                    load_ada(sp, a, ada_in, ada_loaded, ada_used, group)
                    g.prefetch(sp, RING - 1 + group)
                g.prefetch(sp, 5 + RING)

            @block.tensor
            def _(pe):
                n = 0
                for u, (c0, cols) in enumerate(units):
                    w = g.weights(pe, u)
                    for i in range(TT):
                        if n >= 6:
                            pe.wait_ge(s["b_ev"], n - 5)
                        for k in range(DC):
                            last = pe.matmul(g.bank[n % 6][:, 0:cols], g.ht[:, k, i * P:(i + 1) * P], w[:, k, 0:cols],
                                             start=(k == 0), stop=(k == DC - 1))
                        last.then_inc(g.dense, 1)
                        n += 1
                pe.wait_ge(ada_used, 6 * DC)
                for j in range(16):
                    last = pe.matmul(g.bank[6][:, j:j + 1], ada_acc[:, 3 * D + j * P:3 * D + (j + 1) * P], g.ones[:, 0:1],
                                     start=True, stop=True)
                last.then_inc(s["b_cols"], 1)
                for n, c0 in enumerate((2 * D, 2 * D + BANK, 5 * D, 5 * D + BANK)):
                    if n:
                        pe.wait_ge(s["b_rows"], 2 * n)
                    pe.matmul(g.bank[7][:, :], g.ones[:, :], ada_acc[:, c0:c0 + BANK], start=True,
                              stop=True).then_inc(s["b_rows"], 1)

            @block.scalar
            def _(act):
                n = 0
                for u, (c0, cols) in enumerate(units):
                    for i in range(TT):
                        act.wait_ge(g.dense, n + 1)
                        act.activation(proj[:, i, c0:c0 + cols], g.bank[n % 6][:, 0:cols], ACT.Copy).then_inc(s["b_ev"], 1)
                        n += 1

            @block.vector
            def _(dve):
                step = InOrder(dve, s["b_dve"])
                for group in range(2, 6):
                    sum_ada(dve, c_act, ada_in, ada_acc, ada_loaded, ada_used, group)
                dve.wait_ge(s["b_small"], 64)
                dve.wait_ge(s["b_cols"], 1)
                step(dve.tensor_tensor(col[:, 16:32], g.bank[6][:, 0:16], bias[:, :], ALU.add))
                step(dve.scalar_tensor_tensor(col[:, 24:32], col[:, 24:32], 1.0, gain[:, :], ALU.add, ALU.mult))
                for n in range(4):
                    dve.wait_ge(s["b_rows"], 2 * n + 1)
                    dve.tensor_tensor(gate_row[:, n // 2, (n % 2) * BANK:(n % 2 + 1) * BANK], g.bank[7][:, :],
                                      brow[:, n // 2, (n % 2) * BANK:(n % 2 + 1) * BANK], ALU.add).then_inc(s["b_rows"], 1)


def rotate(eng, step, x1, x2, cos, sin, tmp):
    a, b, c, d = tmp
    step(eng.tensor_tensor(a, x1, cos, ALU.mult))
    step(eng.tensor_tensor(b, x2, sin, ALU.mult))
    step(eng.tensor_tensor(c, x1, sin, ALU.mult))
    step(eng.tensor_tensor(d, x2, cos, ALU.mult))
    step(eng.tensor_tensor(x1, a, b, ALU.subtract))
    step(eng.tensor_tensor(x2, c, d, ALU.add))


def rotate_heads(eng, step, x, table, g, tmp):
    v = x.rearrange("p i (h w) -> p i h w", w=RD)
    shape = [P, TT, HEADS, HALF]
    cos = g.cos[:, table].unsqueeze(2).to_broadcast(shape)
    sin = g.sin[:, table].unsqueeze(2).to_broadcast(shape)
    rotate(eng, step, v[:, :, :, 0:HALF], v[:, :, :, HALF:RD], cos, sin, tmp)


def flip_pairs(pe, g, s, q, k, n0=0):
    for n in range(8):
        x = q if n < 4 else k
        if n >= 4:
            pe.wait_ge(s["flip_out"], n - 3)
        for i in range(TT):
            last = pe.transpose(g.bank[n % 4][:, i * P:(i + 1) * P], x[:, i, (n % 4) * P:(n % 4 + 1) * P], g.ident[:, :])
        last.then_inc(s["flipped"], 1)


def retention(g, proj):
    nc, a = g.nc, g.a
    gamma = [1.0 - 2.0 ** (-5.0 - h) for h in range(HEADS)]
    qt, kt = g.ht[:, 0:4, :], g.ht[:, 4:8, :]
    with ExitStack() as ctx:
        def sb(name, shape, dt=F32):
            return ctx.enter_context(nc.sbuf_tensor(name, shape, dt))
        decay = sb("decay", [P, HEADS, T])
        span = sb("span", [P, T])
        y = sb("y_ret", [P, TT, BANK])
        sd = sb("sd", [P, 2, TT, T])
        gain = sb("ret_gain", [P, BANK])
        mu = sb("mu", [P, TT * HEADS])
        var = sb("var", [P, TT * HEADS])
        rms = sb("ret_rms", [P, TT * HEADS])
        rs = sb("ret_rs", [P, TT * HEADS])
        q, k, v, rg = (proj[:, :, c:c + BANK] for c in (C_RQ, C_RK, C_RV, C_RG))
        tmp = [sd[:, n // 2, 2 * (n % 2):2 * (n % 2) + 2, :].rearrange("p a (b c) -> p (a b) c", b=2).rearrange("p i (h w) -> p i h w", w=HALF)
               for n in range(4)]
        with stage(nc, "c_gain c_dve rotated span_ready exps decay_ready flipped flip_out scored weighed summed y_out sq_done root_done rs_ready gate_done") as (block, s):
            @block.sync
            def _(sp):
                sp.dma_start(gain[:, :], a["g_ret_norm"][0:1, :].partition_broadcast(P)).then_inc(s["c_gain"], 16)

            @block.vector
            def _(dve):
                step = InOrder(dve, s["c_dve"])
                dve.tensor_scalar(span[:, :], g.diff[:, :], 0.0, None, ALU.max).then_inc(s["span_ready"], 1)
                rotate_heads(dve, step, q, 0, g, tmp)
                dve.sem_inc(s["rotated"], 1)
                rotate_heads(dve, step, k, 0, g, tmp)
                dve.sem_inc(s["rotated"], 1)
                dve.wait_ge(s["decay_ready"], 1)
                for h in range(HEADS):
                    for j in range(TT):
                        n = TT * h + j
                        w = T - j * P
                        dve.wait_ge(s["scored"], n + 1)
                        if h >= 2 and j == 0:
                            dve.wait_ge(s["summed"], h - 1)
                        dve.scalar_tensor_tensor(sd[:, h % 2, j, 0:w], g.bank[n % 4][:, 0:w], RD ** -0.5,
                                                 decay[:, h, 0:w], ALU.mult, ALU.mult).then_inc(s["weighed"], 1)
                dve.wait_ge(s["y_out"], HEADS)
                yv = y[:, :, :].rearrange("p i (h w) -> p (i h) w", w=RD)
                whole = [P, TT * HEADS, RD]
                sq = q.rearrange("p i (h w) -> p i h w", w=RD)
                step(dve.tensor_reduce(mu[:, :], yv, AX_X, ALU.add))
                step(dve.tensor_scalar(mu[:, :], mu[:, :], 1.0 / RD, None, ALU.mult))
                step(dve.tensor_tensor(yv, yv, mu[:, :].unsqueeze(2).to_broadcast(whole), ALU.subtract))
                step(dve.tensor_tensor(q, y[:, :, :], y[:, :, :], ALU.mult))
                dve.tensor_reduce(var[:, :].rearrange("p (i h) -> p i h", h=HEADS), sq, AX_X, ALU.add).then_inc(s["sq_done"], 1)
                dve.wait_ge(s["root_done"], 1)
                step(dve.reciprocal(rs[:, :], rms[:, :]))
                step(dve.tensor_tensor(yv, yv, rs[:, :].unsqueeze(2).to_broadcast(whole), ALU.mult))
                dve.wait_ge(s["c_gain"], 16)
                step(dve.tensor_tensor(y[:, :, :], y[:, :, :], gain[:, :].unsqueeze(1).to_broadcast([P, TT, BANK]), ALU.mult))
                dve.wait_ge(s["gate_done"], 1)
                step(dve.tensor_tensor(rg, y[:, :, :], rg, ALU.mult))

            @block.gpsimd
            def _(pool):
                pool.wait_ge(s["exps"], HEADS)
                pool.tensor_tensor(decay[:, :, 0:P], decay[:, :, 0:P],
                                   g.causal_t[:, :].unsqueeze(1).to_broadcast([P, HEADS, P]), ALU.mult).then_inc(s["decay_ready"], 1)

            @block.scalar
            def _(act):
                act.wait_ge(s["span_ready"], 1)
                for h in range(HEADS):
                    act.activation(decay[:, h, :], span[:, :], ACT.Exp, scale=float(np.log(gamma[h]))).then_inc(s["exps"], 1)
                for n in range(8):
                    act.wait_ge(s["flipped"], n + 1)
                    act.activation(g.ht[:, n, :], g.bank[n % 4][:, :], ACT.Copy).then_inc(s["flip_out"], 1)
                for h in range(HEADS):
                    act.wait_ge(s["summed"], h + 1)
                    act.activation(y[:, :, h * RD:(h + 1) * RD], g.bank[4 + h % 2][:, 0:TT * RD].rearrange("p (i w) -> p i w", w=RD),
                                   ACT.Copy).then_inc(s["y_out"], 1)
                act.activation(rg, rg, ACT.Silu).then_inc(s["gate_done"], 1)
                act.wait_ge(s["sq_done"], 1)
                act.activation(rms[:, :], var[:, :], ACT.Sqrt, scale=1.0 / RD, bias=g.eps[:, :]).then_inc(s["root_done"], 1)

            @block.tensor
            def _(pe):
                pe.wait_ge(s["rotated"], 2)
                flip_pairs(pe, g, s, q, k)
                pe.wait_ge(s["flip_out"], 8)

                def sums(h):
                    pe.wait_ge(s["weighed"], TT * (h + 1))
                    if h >= 2:
                        pe.wait_ge(s["y_out"], h - 1)
                    for i in range(TT):
                        for j in range(i + 1):
                            last = pe.matmul(g.bank[4 + h % 2][:, i * RD:(i + 1) * RD], sd[:, h % 2, j, (i - j) * P:(i - j + 1) * P],
                                             v[:, j, h * RD:(h + 1) * RD], start=(j == 0), stop=(j == i))
                    last.then_inc(s["summed"], 1)
                for h in range(HEADS):
                    lo = RD * (h % 2)
                    for j in range(TT):
                        n = TT * h + j
                        if n >= 4:
                            pe.wait_ge(s["weighed"], n - 3)
                        pe.matmul(g.bank[n % 4][:, 0:T - j * P], kt[lo:lo + RD, h // 2, j * P:(j + 1) * P],
                                  qt[lo:lo + RD, h // 2, j * P:T], start=True, stop=True).then_inc(s["scored"], 1)
                    if h:
                        sums(h - 1)
                sums(HEADS - 1)


ATTN_SEMS = " at_scored at_max at_exp at_flipped at_pt at_summed at_out at_dve"


class Attention:

    def __init__(self, g, ctx, units, scale, s):
        self.g, self.units, self.scale, self.s = g, units, scale, s

        def sb(name, shape):
            return ctx.enter_context(g.nc.sbuf_tensor(fresh(name), shape, F32))
        self.p = sb("at_p", [P, 2, T])
        self.pt = sb("at_pt", [P, 2, T])
        n = len(units)
        self.mx = sb("at_mx", [P, n])
        self.nmx = sb("at_nmx", [P, n])
        self.sum = sb("at_sum", [P, n])
        self.inv = sb("at_inv", [P, n])

    def pe(self, pe):
        g, s, units = self.g, self.s, self.units

        def scores(u):
            q, k, keys, _, _, _ = units[u]
            if u >= 2:
                pe.wait_ge(s["at_exp"], u - 1)
            for n, (qc, kc) in enumerate(zip(q, k)):
                last = pe.matmul(g.bank[u % 2][:, 0:keys], qc, kc, start=(n == 0), stop=(n == len(q) - 1))
            last.then_inc(s["at_scored"], 1)

        def flip(u):
            keys = units[u][2]
            pe.wait_ge(s["at_exp"], u + 1)
            if u >= 2:
                pe.wait_ge(s["at_pt"], u - 1)
            for j in range(keys // P):
                last = pe.transpose(g.bank[2 + u % 2][:, j * P:(j + 1) * P], self.p[:, u % 2, j * P:(j + 1) * P], g.ident[:, :])
            last.then_inc(s["at_flipped"], 1)

        def sums(u):
            _, _, keys, _, v, out = units[u]
            pe.wait_ge(s["at_pt"], u + 1)
            if u >= 2:
                pe.wait_ge(s["at_out"], u - 1)
            for j in range(keys // P):
                last = pe.matmul(g.bank[4 + u % 2][:, 0:v[j].shape[-1]], self.pt[:, u % 2, j * P:(j + 1) * P], v[j],
                                 start=(j == 0), stop=(j == keys // P - 1))
            last.then_inc(s["at_summed"], 1)
        N = len(units)
        scores(0)
        scores(1)
        for u in range(N):
            if u + 2 < N:
                scores(u + 2)
            flip(u)
            if u:
                sums(u - 1)
        sums(N - 1)

    def dve(self, dve):
        g, s, units = self.g, self.s, self.units
        step = InOrder(dve, s["at_dve"])

        def mask(u):
            _, _, keys, causal, _, _ = units[u]
            dve.wait_ge(s["at_scored"], u + 1)
            if causal:
                at = g.bank[u % 2][:, keys - P:keys]
                step.put(dve.tensor_tensor(at, at, g.causal_neg[:, :], ALU.add))
            return step.count

        def maxima(u, masked):
            if masked:
                step.need(masked)
            step(dve.tensor_reduce(self.mx[:, u:u + 1], g.bank[u % 2][:, 0:units[u][2]], AX_X, ALU.max))
            dve.tensor_scalar(self.nmx[:, u:u + 1], self.mx[:, u:u + 1], -self.scale, None, ALU.mult).then_inc(s["at_max"], 1)

        def invert(u):
            dve.wait_ge(s["at_exp"], u + 1)
            return step.put(dve.reciprocal(self.inv[:, u:u + 1], self.sum[:, u:u + 1]))

        def finish(u, inverted):
            v, out = units[u][4:]
            step.need(inverted)
            dve.wait_ge(s["at_summed"], u + 1)
            dve.tensor_scalar(out, g.bank[4 + u % 2][:, 0:v[0].shape[-1]], self.inv[:, u:u + 1], None, ALU.mult).then_inc(s["at_out"], 1)
        N = len(units)
        maxima(0, mask(0))
        for u in range(N):
            masked = mask(u + 1) if u + 1 < N else 0
            inverted = invert(u - 1) if u else 0
            if u + 1 < N:
                maxima(u + 1, masked)
            if u:
                finish(u - 1, inverted)
        finish(N - 1, invert(N - 1))

    def act(self, act):
        g, s, units = self.g, self.s, self.units

        def exps(u):
            keys = units[u][2]
            act.wait_ge(s["at_max"], u + 1)
            if u >= 2:
                act.wait_ge(s["at_flipped"], u - 1)
            act.activation(self.p[:, u % 2, 0:keys], g.bank[u % 2][:, 0:keys], ACT.Exp, bias=self.nmx[:, u:u + 1],
                           scale=self.scale, accum_out=self.sum[:, u:u + 1]).then_inc(s["at_exp"], 1)

        def evac(u):
            keys = units[u][2]
            act.wait_ge(s["at_flipped"], u + 1)
            if u >= 2:
                act.wait_ge(s["at_summed"], u - 1)
            act.activation(self.pt[:, u % 2, 0:keys], g.bank[2 + u % 2][:, 0:keys], ACT.Copy).then_inc(s["at_pt"], 1)
        N = len(units)
        exps(0)
        for u in range(N):
            if u + 1 < N:
                exps(u + 1)
            evac(u)


def latent_attention(g, proj):
    nc, a = g.nc, g.a
    q = proj[:, :, C_RQ:C_RQ + HEADS * QK]
    k = proj[:, :, C_RQ + HEADS * QK:C_RQ + 2 * HEADS * QK]
    qh = q.rearrange("p i (h w) -> p i h w", w=QK)
    kh = k.rearrange("p i (h w) -> p i h w", w=QK)
    y = proj[:, :, C_RQ:C_RQ + BANK]
    with ExitStack() as ctx:
        def sb(name, shape, dt=F32):
            return ctx.enter_context(nc.sbuf_tensor(name, shape, dt))
        v = sb("mla_v", [P, TT, HEADS, VD])
        kt = sb("mla_kt", [P, HEADS, T])
        qt = g.ht
        with ExitStack() as early:
            def eb(name, shape, dt=F32):
                return early.enter_context(nc.sbuf_tensor(name, shape, dt))
            w_uq = eb("w_uq_sb", [P, 2, HEADS * QK])
            w_ukv = eb("w_ukv_sb", [P, HEADS * 2 * VD])
            lat = eb("lat", [P, 3, T])
            gains = eb("lat_gain", [P, 3])
            scratch = eb("lat_sq", [P, TT, C_KR])
            tmp = eb("mla_tmp", [P, 4, TT, HEADS, ROPE // 2])
            ss, rms, rs = (eb(n, [P, 2, TT]) for n in ("lat_ss", "lat_rms", "lat_rs"))
            with stage(nc, "d_w d_sq d_root d_scaled d_flipped d_lat d_mm d_qk d_v d_dve d_turned d_pt d_pc") as (block, s):
                @block.sync
                def _(sp):
                    sp.dma_start(w_uq[:, :, :], a["w_uq"][0].rearrange("(k p) n -> p k n", p=P)).then_inc(s["d_w"], 16)
                    sp.dma_start(w_ukv[:, :], a["w_ukv"][0]).then_inc(s["d_w"], 16)
                    sp.dma_start(gains[:, 0:2], a["g_q_norm"][0].rearrange("(k p) -> p k", p=P)).then_inc(s["d_w"], 16)
                    sp.dma_start(gains[:, 2:3], a["g_kv_norm"][0].rearrange("(k p) -> p k", p=P)).then_inc(s["d_w"], 16)

                @block.scalar
                def _(act):
                    for i in range(TT):
                        act.activation(scratch[:, i, 0:Q_RANK], proj[:, i, C_QL:C_KV], ACT.Square, accum_out=ss[:, 0, i:i + 1]).then_inc(s["d_sq"], 1)
                        act.activation(scratch[:, i, Q_RANK:C_KR], proj[:, i, C_KV:C_KR], ACT.Square, accum_out=ss[:, 1, i:i + 1]).then_inc(s["d_sq"], 1)
                    act.wait_ge(s["d_sq"], 2 * TT)
                    act.activation(rms[:, 0, :], ss[:, 0, :], ACT.Sqrt, scale=1.0 / Q_RANK, bias=g.eps[:, :]).then_inc(s["d_root"], 1)
                    act.activation(rms[:, 1, :], ss[:, 1, :], ACT.Sqrt, scale=1.0 / KV_RANK, bias=g.eps[:, :]).then_inc(s["d_root"], 1)
                    act.wait_ge(s["d_w"], 64)
                    for c in range(3):
                        act.wait_ge(s["d_flipped"], c + 1)
                        act.activation(lat[:, c, :], g.bank[c][:, :], ACT.Copy, scale=gains[:, c:c + 1]).then_inc(s["d_lat"], 1)
                    for n in range(8):
                        i, half = n // 2, n % 2
                        act.wait_ge(s["d_mm"], n + 1)
                        act.activation(q[:, i, half * 384:(half + 1) * 384], g.bank[3 + n % 4][:, 0:384], ACT.Copy).then_inc(s["d_qk"], 1)
                    for n in range(8):
                        i, half = n // 2, n % 2
                        act.wait_ge(s["d_mm"], 8 + n + 1)
                        act.activation(v[:, i, 4 * half:4 * half + 4, :],
                                       g.bank[3 + n % 4][:, :].rearrange("p (h w) -> p h w", w=2 * VD)[:, :, VD:2 * VD],
                                       ACT.Copy).then_inc(s["d_v"], 1)
                    for n in range(16):
                        act.wait_ge(s["d_pt"], n + 1)
                        dst = qt if n < 8 else kt
                        act.activation(dst[0:QK, n % 8, :], g.bank[n % 3][0:QK, :], ACT.Copy).then_inc(s["d_pc"], 1)

                @block.vector
                def _(dve):
                    step = InOrder(dve, s["d_dve"])
                    shape = [P, TT, ROPE // 2]
                    few = [tt[:, 0, :, 0:HALF:2] for tt in (g.cos, g.sin)]
                    kr = proj[:, :, C_KR:C_RQ]
                    rotate(dve, step, kr[:, :, 0:ROPE // 2], kr[:, :, ROPE // 2:ROPE], few[0], few[1],
                           [tmp[:, n, :, 0, :] for n in range(4)])
                    step(dve.tensor_copy(kh[:, :, :, NOPE:QK], kr.unsqueeze(2).to_broadcast([P, TT, HEADS, ROPE])))
                    dve.wait_ge(s["d_root"], 2)
                    step(dve.reciprocal(rs[:, :, :], rms[:, :, :]))
                    for i in range(TT):
                        dve.tensor_scalar(proj[:, i, C_QL:C_KV], proj[:, i, C_QL:C_KV], rs[:, 0, i:i + 1], None, ALU.mult).then_inc(s["d_scaled"], 1)
                        dve.tensor_scalar(proj[:, i, C_KV:C_KR], proj[:, i, C_KV:C_KR], rs[:, 1, i:i + 1], None, ALU.mult).then_inc(s["d_scaled"], 1)
                    dve.wait_ge(s["d_qk"], 8)
                    shape = [P, TT, HEADS, ROPE // 2]
                    rotate(dve, step, qh[:, :, :, NOPE:NOPE + ROPE // 2], qh[:, :, :, NOPE + ROPE // 2:QK],
                           few[0].unsqueeze(2).to_broadcast(shape), few[1].unsqueeze(2).to_broadcast(shape),
                           [tmp[:, n] for n in range(4)])
                    dve.sem_inc(s["d_turned"], 1)
                    for n in range(8):
                        i, half = n // 2, n % 2
                        dve.wait_ge(s["d_v"], n + 1)
                        dve.tensor_copy(kh[:, i, 4 * half:4 * half + 4, 0:NOPE],
                                        g.bank[3 + n % 4][:, :].rearrange("p (h w) -> p h w", w=2 * VD)[:, :, 0:NOPE]).then_inc(s["d_turned"], 1)

                @block.tensor
                def _(pe):
                    pe.wait_ge(s["d_scaled"], 2 * TT)
                    for c in range(3):
                        for i in range(TT):
                            last = pe.transpose(g.bank[c][:, i * P:(i + 1) * P], proj[:, i, c * P:(c + 1) * P], g.ident[:, :])
                        last.then_inc(s["d_flipped"], 1)
                    pe.wait_ge(s["d_lat"], 3)
                    for n in range(8):
                        i, half = n // 2, n % 2
                        if n >= 4:
                            pe.wait_ge(s["d_qk"], n - 3)
                        for c in range(2):
                            last = pe.matmul(g.bank[3 + n % 4][:, 0:384], lat[:, c, i * P:(i + 1) * P], w_uq[:, c, half * 384:(half + 1) * 384],
                                             start=(c == 0), stop=(c == 1))
                        last.then_inc(s["d_mm"], 1)
                    for n in range(8):
                        i, half = n // 2, n % 2
                        if n < 4:
                            pe.wait_ge(s["d_qk"], n + 5)
                        else:
                            pe.wait_ge(s["d_v"], n - 3)
                            pe.wait_ge(s["d_turned"], 1 + n - 3)
                        pe.matmul(g.bank[3 + n % 4][:, :], lat[:, 2, i * P:(i + 1) * P], w_ukv[:, half * BANK:(half + 1) * BANK],
                                  start=True, stop=True).then_inc(s["d_mm"], 1)
                    for n in range(16):
                        pe.wait_ge(s["d_turned"], 1 if n < 8 else 9)
                        if n >= 3:
                            pe.wait_ge(s["d_pc"], n - 2)
                        src = q if n < 8 else k
                        for i in range(TT):
                            last = pe.transpose(g.bank[n % 3][0:QK, i * P:(i + 1) * P], src[:, i, (n % 8) * QK:(n % 8 + 1) * QK], g.ident[:, :])
                        last.then_inc(s["d_pt"], 1)
        units = [([qt[0:QK, h, i * P:(i + 1) * P]], [kt[0:QK, h, 0:(i + 1) * P]], (i + 1) * P, True,
                  [v[:, j, h, :] for j in range(i + 1)], y[:, i, h * VD:(h + 1) * VD])
                 for h in range(HEADS) for i in range(TT)]
        with stage(nc, ATTN_SEMS) as (block, s):
            at = Attention(g, ctx, units, QK ** -0.5, s)

            @block.sync
            def _(sp):
                pass

            @block.tensor
            def _(pe):
                at.pe(pe)

            @block.vector
            def _(dve):
                at.dve(dve)

            @block.scalar
            def _(act):
                at.act(act)


def mix_out(g, chunks, first_unit, gate, local):
    nc = g.nc
    tmp = local.enter_context(nc.sbuf_tensor(fresh("mix_tmp"), [P, 2, BANK], F32))
    with stage(nc, "e_flipped e_added e_dve" + Products.SEMS) as (block, s):
        products = Products(g, local, s, first_unit, [(u, False, WHOLE, chunk(i)) for u in range(2) for i in range(TT)])

        @block.sync
        def _(sp):
            g.prefetch(sp, first_unit + 2 + RING)

        @block.tensor
        def _(pe):
            for k in range(DC):
                if k >= 4:
                    pe.wait_ge(s["z_hlo"], k - 3)
                for i in range(TT):
                    last = pe.transpose(g.bank[4 + k % 4][:, i * P:(i + 1) * P], chunks(k)[:, i, :], g.ident[:, :])
                last.then_inc(s["e_flipped"], 1)
            for n in range(2 * TT):
                if n >= 4:
                    pe.wait_ge(s["e_added"], n - 3)
                products.pe(pe, n, g.bank[n % 4][:, :])

        @block.gpsimd
        def _(pool):
            products.pool(pool)

        @block.scalar
        def _(act):
            products.act_start(act, s["e_flipped"])
            products.act_unit(act, 1)

        @block.vector
        def _(dve):
            products.dve(dve, s["e_flipped"])
            step = InOrder(dve, s["e_dve"])
            n = 0
            for u in range(2):
                for i in range(TT):
                    dve.wait_ge(g.dense, g.before(first_unit) + n + 1)
                    at = g.x[:, i, u * BANK:(u + 1) * BANK]
                    if gate is None:
                        dve.tensor_tensor(at, g.bank[n % 4][:, :], at, ALU.add).then_inc(s["e_added"], 1)
                    else:
                        if n >= 2:
                            dve.wait_ge(s["e_added"], n - 1)
                        step(dve.tensor_tensor(tmp[:, n % 2, :], g.bank[n % 4][:, :], gate[:, u * BANK:(u + 1) * BANK], ALU.mult))
                        dve.tensor_tensor(at, tmp[:, n % 2, :], at, ALU.add).then_inc(s["e_added"], 1)
                    n += 1


def norm_transposed(g, scale, shift, local, source=None, gain_src=None, keep=None, upto=0, tiles=TT, dst=None,
                    gain_keep=None):
    nc = g.nc
    x = g.x if source is None else source
    dst = g.ht if dst is None else dst
    gain = None
    if gain_src is not None:
        gain = gain_keep if gain_keep is not None else local.enter_context(nc.sbuf_tensor(fresh("nt_gain"), [P, DC], F32))
        scale = gain
    xn = local.enter_context(nc.sbuf_tensor(fresh("nt_xn"), [P, tiles, D], F32)) if keep is None else keep
    ss, rms, rs = (local.enter_context(nc.sbuf_tensor(fresh(n), [P, tiles], F32)) for n in ("nt_ss", "nt_rms", "nt_rs"))
    with stage(nc, "f_gain f_sq f_root f_rs f_xn f_flipped f_out") as (block, s):
        @block.sync
        def _(sp):
            if gain is not None:
                sp.dma_start(gain[:, :], gain_src.rearrange("(k p) -> p k", p=P)).then_inc(s["f_gain"], 16)
            g.prefetch(sp, upto)

        @block.vector
        def _(dve):
            for i in range(tiles):
                dve.wait_ge(s["f_root"], i + 1)
                dve.reciprocal(rs[:, i:i + 1], rms[:, i:i + 1]).then_inc(s["f_rs"], 1)
                dve.wait_ge(s["f_rs"], i + 1)
                dve.tensor_scalar(xn[:, i, :], x[:, i, :], rs[:, i:i + 1], None, ALU.mult).then_inc(s["f_xn"], 1)

        @block.scalar
        def _(act):
            for i in range(tiles):
                act.activation(xn[:, i, :], x[:, i, :], ACT.Square, accum_out=ss[:, i:i + 1]).then_inc(s["f_sq"], 1)
            for i in range(tiles):
                act.wait_ge(s["f_sq"], i + 1)
                act.activation(rms[:, i:i + 1], ss[:, i:i + 1], ACT.Sqrt, scale=1.0 / D, bias=g.eps[:, :]).then_inc(s["f_root"], 1)
            if gain is not None:
                act.wait_ge(s["f_gain"], 16)
            for k in range(DC):
                act.wait_ge(s["f_flipped"], k + 1)
                if shift is None:
                    act.activation(dst[:, k, 0:tiles * P], g.bank[k][:, 0:tiles * P], ACT.Copy, scale=scale[:, k:k + 1]).then_inc(s["f_out"], 1)
                else:
                    act.activation(dst[:, k, 0:tiles * P], g.bank[k][:, 0:tiles * P], ACT.Identity, bias=shift[:, k:k + 1],
                                   scale=scale[:, k:k + 1]).then_inc(s["f_out"], 1)

        @block.tensor
        def _(pe):
            pe.wait_ge(s["f_xn"], tiles)
            for k in range(DC):
                for i in range(tiles):
                    last = pe.transpose(g.bank[k][:, i * P:(i + 1) * P], xn[:, i, k * P:(k + 1) * P], g.ident[:, :])
                last.then_inc(s["f_flipped"], 1)


LOW = -3.0e38


def top16(dve, count, done, rows):
    def all_done():
        count[0] += len(rows)
        dve.wait_ge(done, count[0])
    for v, work, top, at in rows:
        dve.max(top[:, 0:8], v).then_inc(done, 1)
    all_done()
    for v, work, top, at in rows:
        dve.max_index(at[:, 0:8], top[:, 0:8], v).then_inc(done, 1)
    all_done()
    for v, work, top, at in rows:
        dve.match_replace(work, top[:, 0:8], v, LOW).then_inc(done, 1)
    all_done()
    for v, work, top, at in rows:
        dve.max(top[:, 8:16], work).then_inc(done, 1)
    all_done()
    for v, work, top, at in rows:
        dve.max_index(at[:, 8:16], top[:, 8:16], work).then_inc(done, 1)
    all_done()


def top_keys(g, top_v, top_i, first_unit):
    nc, a = g.nc, g.a
    HP = 2 * PH
    with ExitStack() as ctx:
        keys = ctx.enter_context(nc.sbuf_tensor("keys_t", [P, 2, PK], F32))
        qf = ctx.enter_context(nc.sbuf_tensor("peer_q", [P, 2, T], F32))
        work = ctx.enter_context(nc.sbuf_tensor("top_work", [P, TT, PK], F32))
        with stage(nc, "g_keys g_q g_scored g_topped g_dve" + Products.SEMS) as (block, s):
            products = Products(g, ctx, s, first_unit, [(n // 4, True, chunk(n % 4), WHOLE) for n in range(HP)])

            @block.gpsimd
            def _(pool):
                products.pool(pool)

            @block.sync
            def _(sp):
                sp.dma_start(keys[:, :, :], a["sub_keys_t"].rearrange("h d k -> d h k")).then_inc(s["g_keys"], 16)
                g.prefetch(sp, first_unit + 4 + RING)

            @block.tensor
            def _(pe):
                pe.wait_ge(s["g_keys"], 16)

                def scores(n):
                    pe.wait_ge(s["g_q"], n + 1)
                    if n >= 2:
                        pe.wait_ge(s["g_topped"], n - 1)
                    for i in range(TT):
                        last = pe.matmul(g.bank[2 + n % 2][:, i * PK:(i + 1) * PK], qf[:, n % 2, i * P:(i + 1) * P], keys[:, n % 2, :],
                                         start=True, stop=True)
                    last.then_inc(s["g_scored"], 1)
                for n in range(HP):
                    if n >= 2:
                        pe.wait_ge(s["g_q"], n - 1)
                    products.pe(pe, n, g.bank[n % 2][:, :])
                    if n:
                        scores(n - 1)
                scores(HP - 1)

            @block.scalar
            def _(act):
                products.act_start(act)
                for n in range(HP):
                    if n % 4 == 3:
                        products.act_unit(act, n // 4 + 1)
                    act.wait_ge(g.dense, g.before(first_unit) + n + 1)
                    if n >= 2:
                        act.wait_ge(s["g_scored"], n - 1)
                    act.activation(qf[:, n % 2, :], g.bank[n % 2][:, :], ACT.Copy).then_inc(s["g_q"], 1)

            @block.vector
            def _(dve):
                products.dve(dve)
                count = [0]
                for n in range(HP):
                    dve.wait_ge(s["g_scored"], n + 1)
                    top16(dve, count, s["g_dve"], [(g.bank[2 + n % 2][:, i * PK:(i + 1) * PK], work[:, i, :], top_v[:, i, n, :], top_i[:, i, n, :])
                                                   for i in range(TT)])
                    dve.sem_inc(s["g_topped"], 1)


class Memory:
    SEMS = " q_in q_sq q_root q_rs q_xn q_flipped q_out q_stored"
    FIRST_BANK, BANKS = 3, 5

    def __init__(self, g, ctx, s, first_unit, kt_out, v_out):
        self.g, self.s, self.first_unit, self.kt_out, self.v_out = g, s, first_unit, kt_out, v_out

        def sb(name, shape):
            return ctx.enter_context(g.nc.sbuf_tensor(name, shape, F32))
        MT = MEM // P
        self.rows = sb("mem_rows", [P, MT, D])
        self.xn = sb("mem_xn", [P, MT, D])
        self.t = sb("mem_t", [P, DC, MEM])
        self.kt = sb("mem_kt", [P, DC, MEM])
        self.v = self.rows
        self.gain = sb("mem_gain", [P, DC])
        self.ss, self.rms, self.rs = (sb(n, [P, MT]) for n in ("mem_ss", "mem_rms", "mem_rs"))
        self.groups = [("k", c) for c in range(DC)] + [("v", (h, i)) for h in range(2) for i in range(MT)]

    def bank(self, n):
        return self.g.bank[self.FIRST_BANK + n % self.BANKS]

    def sp(self, sp):
        s, a = self.s, self.g.a
        sp.dma_start(self.rows[:], a["mem_2"][0].rearrange("(i p) d -> p i d", p=P)).then_inc(s["q_in"], 16)
        sp.dma_start(self.gain[:, :], a["norm_mem_g_2"][0].rearrange("(k p) -> p k", p=P)).then_inc(s["q_in"], 16)
        self.g.prefetch(sp, self.first_unit + 4)
        for n, (dst, src) in enumerate(((self.kt_out, self.kt), (self.v_out, self.v))):
            sp.wait_ge(s["q_out"], DC + (DC if n == 0 else len(self.groups)))
            sp.dma_start(dst, src[:].rearrange("p a b -> p (a b)")).then_inc(s["q_stored"], 16)
        sp.wait_ge(s["q_stored"], 32)

    def dve(self, dve):
        dve.wait_ge(self.s["q_root"], 1)
        dve.reciprocal(self.rs[:, :], self.rms[:, :]).then_inc(self.s["q_rs"], 1)

    def act(self, act):
        g, s = self.g, self.s
        act.wait_ge(s["q_in"], 32)
        for i in range(MEM // P):
            act.activation(self.xn[:, i, :], self.rows[:, i, :], ACT.Square, accum_out=self.ss[:, i:i + 1]).then_inc(s["q_sq"], 1)
        act.wait_ge(s["q_sq"], MEM // P)
        act.activation(self.rms[:, :], self.ss[:, :], ACT.Sqrt, scale=1.0 / D, bias=g.eps[:, :]).then_inc(s["q_root"], 1)
        act.wait_ge(s["q_rs"], 1)
        for i in range(MEM // P):
            act.activation(self.xn[:, i, :], self.rows[:, i, :], ACT.Copy, scale=self.rs[:, i:i + 1]).then_inc(s["q_xn"], 1)
        for k in range(DC):
            act.wait_ge(s["q_flipped"], k + 1)
            act.activation(self.t[:, k, :], self.bank(k)[:, 0:MEM], ACT.Copy, scale=self.gain[:, k:k + 1]).then_inc(s["q_out"], 1)
        for n, (what, at) in enumerate(self.groups):
            act.wait_ge(g.dense, g.before(self.first_unit) + n + 1)
            if what == "k":
                dst, src = self.kt[:, at, :], self.bank(DC + n)[:, 0:MEM]
            else:
                dst, src = self.v[:, at[1], at[0] * BANK:(at[0] + 1) * BANK], self.bank(DC + n)[:, :]
            act.activation(dst, src, ACT.Copy).then_inc(s["q_out"], 1)

    def pe(self, pe):
        g, s = self.g, self.s
        pe.wait_ge(s["q_xn"], MEM // P)
        for k in range(DC):
            if k >= self.BANKS:
                pe.wait_ge(s["q_out"], k - self.BANKS + 1)
            for i in range(MEM // P):
                last = pe.transpose(self.bank(k)[:, i * P:(i + 1) * P], self.xn[:, i, k * P:(k + 1) * P], g.ident[:, :])
            last.then_inc(s["q_flipped"], 1)
        pe.wait_ge(s["q_out"], DC)
        for n, (what, at) in enumerate(self.groups):
            if what == "k":
                w = g.weights(pe, self.first_unit + at // 4)
            else:
                w = g.weights(pe, self.first_unit + 2 + at[0])
            if n >= self.BANKS:
                pe.wait_ge(s["q_out"], DC + n - self.BANKS + 1)
            for k in range(DC):
                if what == "k":
                    last = pe.matmul(self.bank(DC + n)[:, 0:MEM], w[:, k, at % 4 * P:(at % 4 + 1) * P], self.t[:, k, :], start=(k == 0), stop=(k == DC - 1))
                else:
                    last = pe.matmul(self.bank(DC + n)[:, :], self.t[:, k, at[1] * P:(at[1] + 1) * P], w[:, k, :], start=(k == 0), stop=(k == DC - 1))
            last.then_inc(g.dense, 1)


def choose_experts(g, top_v, top_i, key1_t, key2_t, gate_t, first_unit, mem_kt, mem_v):
    nc = g.nc
    with ExitStack() as ctx:
        def sb(name, shape, dt=F32):
            return ctx.enter_context(nc.sbuf_tensor(name, shape, dt))
        sums = sb("sums", [P, 2, PH, TOPK, TOPK])
        work = sb("sum_work", [P, 4, TOPK * TOPK])
        best = sb("best", [P, TT, PH, TOPK])
        place = sb("place", [P, TT, PH, TOPK], U32)
        rank_i = sb("rank_i", [P, 2, TT, PH, TOPK], U32)
        rank = sb("rank", [P, 2, TT, PH, TOPK])
        key_f = sb("key_f", [P, TT, 2 * PH, TOPK])
        hit = sums
        key = sb("key", [P, 2, TT, PH, TOPK])
        gate = sb("gate", [P, TT, PH, TOPK])
        total = sb("total", [P, TT, PH])
        inv = sb("inv_total", [P, TT, PH])
        v = top_v[:, :, :, :].rearrange("p i (h s) k -> p i h s k", s=2)
        kf = key_f[:, :, :, :].rearrange("p i (h s) k -> p i h s k", s=2)
        wide = [P, PH, TOPK, TOPK]
        with stage(nc, "h_sums h_dve h_chain h_top h_shift h_exp h_gate h_keyed h_red h_hit h_mul h_flipped h_out" + Memory.SEMS) as (block, s):
            memory = Memory(g, ctx, s, first_unit, mem_kt, mem_v)

            @block.sync
            def _(sp):
                memory.sp(sp)

            @block.gpsimd
            def _(pool):
                for i in range(TT):
                    if i >= 2:
                        pool.wait_ge(s["h_top"], i - 1)
                    pool.tensor_tensor(sums[:, i % 2], v[:, i, :, 0, :].unsqueeze(3).to_broadcast(wide),
                                       v[:, i, :, 1, :].unsqueeze(2).to_broadcast(wide), ALU.add).then_inc(s["h_sums"], 1)
                pool.tensor_copy(key_f[:, :, :, :], top_i[:, :, :, :]).then_inc(s["h_keyed"], 1)
                pool.wait_ge(s["h_keyed"], 1)
                for n in range(2 * TT):
                    i, half = n // 2, n % 2
                    pool.wait_ge(s["h_hit"], n + 1)
                    pool.tensor_tensor(hit[:, half], hit[:, half], kf[:, i, :, half, :].unsqueeze(2).to_broadcast(wide), ALU.mult).then_inc(s["h_mul"], 1)

            @block.vector
            def _(dve):
                count = [0]
                for i in range(TT):
                    dve.wait_ge(s["h_sums"], i + 1)
                    for h in range(0, PH, 4):
                        top16(dve, count, s["h_dve"], [(sums[:, i % 2, h + j].rearrange("p a b -> p (a b)"), work[:, j, :],
                                                        best[:, i, h + j, :], place[:, i, h + j, :]) for j in range(4)])
                    dve.sem_inc(s["h_top"], 1)
                    if i == 0:
                        memory.dve(dve)
                step = InOrder(dve, s["h_chain"])
                dve.tensor_tensor(gate[:], best[:], best[:, :, :, 0:1].to_broadcast([P, TT, PH, TOPK]), ALU.subtract).then_inc(s["h_shift"], 1)
                step(dve.tensor_scalar(rank_i[:, 0], place[:], 4, None, ALU.arith_shift_right))
                step(dve.tensor_scalar(rank_i[:, 1], place[:], 15, None, ALU.bitwise_and))
                step(dve.tensor_copy(rank[:], rank_i[:]))
                for n in range(2 * TT + 1):
                    if n < 2 * TT:
                        dve.tensor_tensor(hit[:, n % 2], rank[:, n % 2, n // 2].unsqueeze(3).to_broadcast(wide),
                                          g.iota_p[:, 0:TOPK].unsqueeze(1).unsqueeze(1).to_broadcast(wide), ALU.is_equal).then_inc(s["h_hit"], 1)
                    if n:
                        m = n - 1
                        dve.wait_ge(s["h_mul"], m + 1)
                        dve.tensor_reduce(key[:, m % 2, m // 2], hit[:, m % 2], AX_X, ALU.add).then_inc(s["h_red"], 1)
                        dve.wait_ge(s["h_red"], m + 1)
                dve.wait_ge(s["h_exp"], 1)
                step(dve.tensor_reduce(total[:], gate[:], AX_X, ALU.add))
                step(dve.reciprocal(inv[:], total[:]))
                dve.tensor_tensor(gate[:], gate[:], inv[:].unsqueeze(3).to_broadcast([P, TT, PH, TOPK]), ALU.mult).then_inc(s["h_gate"], 1)

            @block.scalar
            def _(act):
                memory.act(act)
                act.wait_ge(s["h_shift"], 1)
                act.activation(gate[:], gate[:], ACT.Exp).then_inc(s["h_exp"], 1)
                for n, dst in enumerate((key1_t, key2_t, gate_t)):
                    act.wait_ge(s["h_flipped"], n + 1)
                    act.activation(dst[:, :], g.bank[n][:, :], ACT.Copy).then_inc(s["h_out"], 1)

            @block.tensor
            def _(pe):
                memory.pe(pe)
                pe.wait_ge(s["h_red"], 2 * TT)
                for n, src in enumerate((key[:, 0], key[:, 1], gate[:])):
                    if n == 2:
                        pe.wait_ge(s["h_gate"], 1)
                    for i in range(TT):
                        last = pe.transpose(g.bank[n][:, i * P:(i + 1) * P], src[:, i].rearrange("p h k -> p (h k)"), g.ident[:, :])
                    last.then_inc(s["h_flipped"], 1)


GB = 128
GT4 = 4
GQ = GB // GT4


def spread_gates(g, key1_t, key2_t, gate_t, gates):
    nc = g.nc
    SLOTS = 4
    group = [P, GT4, P]

    def wide(x):
        return x.unsqueeze(2).to_broadcast(group)
    with ExitStack() as ctx:
        def sb(name, shape, dt=F32):
            return ctx.enter_context(nc.sbuf_tensor(name, shape, dt))
        now = sb("now", [P, 2, 3, GB])
        one1 = sb("one1", [P, SLOTS, GT4, P])
        one2 = sb("one2", [P, SLOTS, GT4, P])
        out = sb("spread", [P, 2, P, GB])
        with stage(nc, "i_now i_hit1 i_one1 i_one2 i_mm i_out i_stored0 i_stored1 i_paced") as (block, s):
            stored = (s["i_stored0"], s["i_stored1"])

            @block.vector
            def _(dve):
                with dve.Fori(0, T // GB // 2) as it:
                    for b in range(2):
                        blk = it * 2 + b
                        for n, src in enumerate((key1_t, key2_t, gate_t)):
                            dve.tensor_copy(now[:, b, n, :], src[:, bass.ds(blk * GB, GB)]).then_inc(s["i_now"], 1)
                        dve.wait_ge(s["i_now"], blk * 3 + 3)
                        for q in range(GQ):
                            n = blk * GQ + q
                            dve.wait_ge(s["i_mm"], n + 1)
                            c = slice(q * GT4, (q + 1) * GT4)
                            for one, which, done in ((one1, 0, "i_hit1"), (one2, 1, "i_one2")):
                                dve.tensor_tensor(one[:, q % SLOTS], g.iota_p[:, :].unsqueeze(1).to_broadcast(group),
                                                  wide(now[:, b, which, c]), ALU.is_equal).then_inc(s[done], 1)

            @block.gpsimd
            def _(pool):
                with pool.Fori(0, T // GB // 2) as it:
                    for b in range(2):
                        blk = it * 2 + b
                        for q in range(GQ):
                            pool.wait_ge(s["i_hit1"], blk * GQ + q + 1)
                            pool.sem_inc(s["i_paced"], 1)
                            pool.tensor_tensor(one1[:, q % SLOTS], one1[:, q % SLOTS], wide(now[:, b, 2, q * GT4:(q + 1) * GT4]),
                                               ALU.mult).then_inc(s["i_one1"], 1)

            @block.tensor
            def _(pe):
                pe.sem_inc(s["i_mm"], SLOTS)
                with pe.Fori(0, T // GB // 2) as it:
                    for b in range(2):
                        blk = it * 2 + b
                        for q in range(GQ):
                            n = blk * GQ + q
                            pe.wait_ge(s["i_one1"], n + 1)
                            pe.wait_ge(s["i_one2"], n + 1)
                            pe.wait_ge(s["i_out"], n + 1)
                            for j in range(GT4):
                                last = pe.matmul(g.bank[q % 4][:, j * P:(j + 1) * P], one2[:, q % SLOTS, j, :], one1[:, q % SLOTS, j, :],
                                                 start=True, stop=True)
                            last.then_inc(s["i_mm"], 1)

            @block.scalar
            def _(act):
                act.sem_inc(s["i_out"], 4)
                with act.Fori(0, T // GB // 2) as it:
                    for b in range(2):
                        blk = it * 2 + b
                        act.wait_ge(stored[b], it * 16 + 16)
                        for q in range(GQ):
                            n = blk * GQ + q
                            act.wait_ge(s["i_mm"], n + 1 + SLOTS)
                            act.activation(out[:, b, :, q * GT4:(q + 1) * GT4].rearrange("p k t -> p t k"),
                                           g.bank[q % 4][:, :].rearrange("p (t k) -> p t k", k=P), ACT.Copy).then_inc(s["i_out"], 1)

            @block.sync
            def _(sp):
                for b in range(2):
                    sp.sem_inc(stored[b], 16)
                with sp.Fori(0, T // GB // 2) as it:
                    for b in range(2):
                        blk = it * 2 + b
                        sp.wait_ge(s["i_out"], (blk + 1) * GQ + 4)
                        sp.dma_start(gates[:, :, bass.ds(blk * GB, GB)].rearrange("k p t -> p k t"), out[:, b]).then_inc(stored[b], 16)
                for b in range(2):
                    sp.wait_ge(stored[b], 16 * (T // GB // 2 + 1))


def reached(q, n):
    return q >= n if isinstance(q, int) else True


def experts(g, gates, acc):
    nc, a = g.nc, g.a
    GT = 2
    Q = PK // GT
    NO = 2 * TT
    with ExitStack() as ctx:
        def sb(name, shape, dt=F32):
            return ctx.enter_context(nc.sbuf_tensor(name, shape, dt))
        h_hi, h_lo = sb("h_hi", [P, DC, T], F32R), sb("h_lo", [P, DC, T], F32R)
        u_in, v_in = sb("u_in", [P, GT, D]), sb("v_in", [P, GT, D])
        u_hi, u_lo = sb("u_hi", [P, GT, D], F32R), sb("u_lo", [P, GT, D], F32R)
        v_hi, v_lo = sb("v_hi", [P, 2, GT, D], F32R), sb("v_lo", [P, 2, GT, D], F32R)
        gate_in = sb("gate_in", [P, 2, GT, T])
        gel = sb("gel", [P, GT, T])
        w = sb("peer_w", [P, GT, T])
        w_hi, w_lo = sb("peer_w_hi", [P, 2, GT, T], F32R), sb("peer_w_lo", [P, 2, GT, T], F32R)
        names = "j_u0 j_u1 j_v0 j_v1 j_g00 j_g01 j_g10 j_g11"
        with stage(nc, names + " j_zero j_hhi j_hlo j_uhi j_ulo j_vhi j_vlo j_a j_gelu j_w j_whi j_wlo j_o j_added") as (block, s):

            def load(sp, q, par):
                for e in range(GT):
                    n = (q - 1) * GT + e + 1
                    if reached(q, 1):
                        sp.wait_ge(s["j_ulo"], n)
                    sp.dma_start(u_in[:, e, :], a["u_tiles"][bass.ds(q * GT + e, 1)].rearrange("o p c e -> p (o c e)")).then_inc(s[f"j_u{e}"], 16)
                    if reached(q, 1):
                        sp.wait_ge(s["j_vlo"], n)
                    sp.dma_start(v_in[:, e, :], a["expert_v"][0].rearrange("(t p) d -> t p d", p=P)[bass.ds(q * GT + e, 1)].rearrange("o p d -> p (o d)")).then_inc(s[f"j_v{e}"], 16)
                    if reached(q, 2):
                        sp.wait_ge(s["j_w"], n - GT)
                    sp.dma_start(gate_in[:, par, e, :], gates[bass.ds(q * GT + e, 1)].rearrange("o p t -> p (o t)")).then_inc(s[f"j_g{par}{e}"], 16)

            @block.sync
            def _(sp):
                for q in range(2):
                    load(sp, q, q)
                with sp.Fori(1, Q // 2) as it:
                    for par in range(2):
                        load(sp, it * 2 + par, par)

            @block.gpsimd
            def _(pool):
                pool.memset(acc[:, :, :], 0.0).then_inc(s["j_zero"], 1)

            def up(pe, q, par):
                for e in range(GT):
                    pe.wait_ge(s["j_ulo"], q * GT + e + 1)
                    if reached(q, 2):
                        pe.wait_ge(s["j_gelu"], (q - 2) * GT + e + 1)
                    n = 0
                    for k in range(DC):
                        c = slice(k * P, (k + 1) * P)
                        for u, h in ((u_hi, h_hi), (u_hi, h_lo), (u_lo, h_hi)):
                            last = pe.matmul(g.bank[2 * par + e][:, :], u[:, e, c], h[:, k, :], start=(n == 0), stop=(n == 3 * DC - 1))
                            n += 1
                    last.then_inc(s["j_a"], 1)

            def down(pe, q, par):
                pe.wait_ge(s["j_wlo"], (q + 1) * GT)
                pe.wait_ge(s["j_vlo"], (q + 1) * GT)
                for o in range(NO):
                    i, c = o // 2, slice(o % 2 * BANK, (o % 2 + 1) * BANK)
                    if reached(q, 1) or o >= 4:
                        pe.wait_ge(s["j_added"], q * NO + o - 3)
                    n = 0
                    for e in range(GT):
                        for x, v in ((w_hi, v_hi), (w_hi, v_lo), (w_lo, v_hi)):
                            last = pe.matmul(g.bank[4 + o % 4][:, :], x[:, par, e, i * P:(i + 1) * P], v[:, par, e, c],
                                             start=(n == 0), stop=(n == 3 * GT - 1))
                            n += 1
                    last.then_inc(s["j_o"], 1)

            @block.tensor
            def _(pe):
                pe.wait_ge(s["j_hlo"], DC)
                up(pe, 0, 0)
                up(pe, 1, 1)
                down(pe, 0, 0)
                with pe.Fori(1, Q // 2) as it:
                    up(pe, it * 2, 0)
                    down(pe, it * 2 - 1, 1)
                    up(pe, it * 2 + 1, 1)
                    down(pe, it * 2, 0)
                down(pe, Q - 1, 1)

            def act_u(act, q, e):
                act.wait_ge(s[f"j_u{e}"], (q + 1) * 16)
                if reached(q, 1):
                    act.wait_ge(s["j_a"], (q - 1) * GT + e + 1)
                act.activation(u_hi[:, e, :], u_in[:, e, :], ACT.Copy).then_inc(s["j_uhi"], 1)

            def act_group(act, q, par, more):
                for e in range(GT):
                    act.wait_ge(s[f"j_v{e}"], (q + 1) * 16)
                    if reached(q, 2):
                        act.wait_ge(s["j_o"], (q - 1) * NO)
                    act.activation(v_hi[:, par, e, :], v_in[:, e, :], ACT.Copy).then_inc(s["j_vhi"], 1)
                for e in range(GT):
                    act.wait_ge(s["j_a"], q * GT + e + 1)
                    if reached(q, 1):
                        act.wait_ge(s["j_w"], (q - 1) * GT + e + 1)
                    act.activation(gel[:, e, :], g.bank[2 * par + e][:, :], ACT.Gelu).then_inc(s["j_gelu"], 1)
                    if more:
                        act_u(act, q + 1, e)
                    act.wait_ge(s["j_w"], q * GT + e + 1)
                    act.activation(w_hi[:, par, e, :], w[:, e, :], ACT.Copy).then_inc(s["j_whi"], 1)

            @block.scalar
            def _(act):
                for k in range(DC):
                    act.activation(h_hi[:, k, :], g.ht[:, k, :], ACT.Copy).then_inc(s["j_hhi"], 1)
                for e in range(GT):
                    act_u(act, 0, e)
                for q in range(2):
                    act_group(act, q, q, True)
                with act.Fori(1, Q // 2 - 1) as it:
                    for par in range(2):
                        act_group(act, it * 2 + par, par, True)
                for q in (Q - 2, Q - 1):
                    act_group(act, q, q % 2, q < Q - 1)

            def dve_u(dve, q, e):
                dve.wait_ge(s["j_uhi"], q * GT + e + 1)
                dve.tensor_tensor(u_lo[:, e, :], u_in[:, e, :], u_hi[:, e, :].bitcast(F32), ALU.subtract).then_inc(s["j_ulo"], 1)

            def dve_group(dve, q, par, half, more):
                for e in range(GT):
                    dve.wait_ge(s["j_vhi"], q * GT + e + 1)
                    dve.tensor_tensor(v_lo[:, par, e, :], v_in[:, e, :], v_hi[:, par, e, :].bitcast(F32), ALU.subtract).then_inc(s["j_vlo"], 1)
                for e in range(GT):
                    dve.wait_ge(s["j_gelu"], q * GT + e + 1)
                    dve.wait_ge(s[f"j_g{par}{e}"], (half + 1) * 16)
                    if reached(q, 1):
                        dve.wait_ge(s["j_wlo"], (q - 1) * GT + e + 1)
                    dve.tensor_tensor(w[:, e, :], gel[:, e, :], gate_in[:, par, e, :], ALU.mult).then_inc(s["j_w"], 1)
                    if more:
                        dve_u(dve, q + 1, e)
                    dve.wait_ge(s["j_whi"], q * GT + e + 1)
                    dve.tensor_tensor(w_lo[:, par, e, :], w[:, e, :], w_hi[:, par, e, :].bitcast(F32), ALU.subtract).then_inc(s["j_wlo"], 1)
                if reached(q, 1):
                    add(dve, q - 1)

            def add(dve, q):
                for o in range(NO):
                    dve.wait_ge(s["j_o"], q * NO + o + 1)
                    at = acc[:, o // 2, o % 2 * BANK:(o % 2 + 1) * BANK]
                    dve.tensor_tensor(at, g.bank[4 + o % 4][:, :], at, ALU.add).then_inc(s["j_added"], 1)

            @block.vector
            def _(dve):
                for k in range(DC):
                    dve.wait_ge(s["j_hhi"], k + 1)
                    dve.tensor_tensor(h_lo[:, k, :], g.ht[:, k, :], h_hi[:, k, :].bitcast(F32), ALU.subtract).then_inc(s["j_hlo"], 1)
                for e in range(GT):
                    dve_u(dve, 0, e)
                dve.wait_ge(s["j_zero"], 1)
                for q in range(2):
                    dve_group(dve, q, q, 0, True)
                with dve.Fori(1, Q // 2 - 1) as it:
                    for par in range(2):
                        dve_group(dve, it * 2 + par, par, it, True)
                for q in (Q - 2, Q - 1):
                    dve_group(dve, q, q % 2, Q // 2 - 1, q < Q - 1)
                add(dve, Q - 1)


def close_first(g, acc, gate):
    nc, a = g.nc, g.a
    with ExitStack() as ctx:
        gain = ctx.enter_context(nc.sbuf_tensor("final_gain", [P, D], F32))
        sq = ctx.enter_context(nc.sbuf_tensor("final_sq", [P, TT, D], F32))
        ss, rms, rs = (ctx.enter_context(nc.sbuf_tensor(n, [P, TT], F32)) for n in ("fin_ss", "fin_rms", "fin_rs"))
        with stage(nc, "k_gain k_dve k_sum k_sq k_root k_end") as (block, s):
            @block.sync
            def _(sp):
                sp.dma_start(gain[:, :], a["g_final"].unsqueeze(0).partition_broadcast(P)).then_inc(s["k_gain"], 16)

            @block.vector
            def _(dve):
                step = InOrder(dve, s["k_dve"])
                for i in range(TT):
                    step(dve.tensor_tensor(acc[:, i, :], acc[:, i, :], gate, ALU.mult))
                    dve.tensor_tensor(g.x[:, i, :], acc[:, i, :], g.x[:, i, :], ALU.add).then_inc(s["k_sum"], 1)
                dve.wait_ge(s["k_gain"], 16)
                for i in range(TT):
                    dve.wait_ge(s["k_root"], i + 1)
                    step(dve.reciprocal(rs[:, i:i + 1], rms[:, i:i + 1]))
                    dve.scalar_tensor_tensor(g.x[:, i, :], g.x[:, i, :], rs[:, i:i + 1], gain[:, :], ALU.mult, ALU.mult).then_inc(s["k_end"], 1)

            @block.scalar
            def _(act):
                for i in range(TT):
                    act.wait_ge(s["k_sum"], i + 1)
                    act.activation(sq[:, i, :], g.x[:, i, :], ACT.Square, accum_out=ss[:, i:i + 1]).then_inc(s["k_sq"], 1)
                for i in range(TT):
                    act.wait_ge(s["k_sq"], i + 1)
                    act.activation(rms[:, i:i + 1], ss[:, i:i + 1], ACT.Sqrt, scale=1.0 / D, bias=g.eps[:, :]).then_inc(s["k_root"], 1)


W2_DQ, W2_DK, W2_DV, W2_MQ, W2_MK, W2_MV, W2_MO, W2_GATES = (i * BANK for i in range(8))


def project_second(g, tok, mv, conv, mi, mf, first_unit):
    nc, a = g.nc, g.a
    with ExitStack() as ctx:
        def sb(name, shape, dt=F32):
            return ctx.enter_context(nc.sbuf_tensor(name, shape, dt))
        raw = sb("conv_in", [P, 4, T])
        taps = sb("taps", [P, CONV, 8])
        cbias = sb("conv_bias", [P, 8])
        gbias = sb("gate_bias", [ML_H, 2])
        with stage(nc, "l_par l_raw l_conv l_cdone l_tok l_small l_ones l_dve l_rot" + Products.SEMS) as (block, s):
            products = Products(g, ctx, s, first_unit, [(n // 4, True, chunk(n % 4), WHOLE) for n in range(8)]
                                + [(2 + n // TT, False, WHOLE, chunk(n % TT)) for n in range(5 * TT)]
                                + [(7, True, slice(c * ML_H, (c + 1) * ML_H), WHOLE) for c in range(2)])

            @block.sync
            def _(sp):
                sp.dma_start(taps[:, :, :], a["ml_conv_w_2"][0].rearrange("j o (c p) -> p (j o) c", p=P)).then_inc(s["l_par"], 16)
                sp.dma_start(cbias[:, :], a["ml_conv_b_2"][0].rearrange("(c p) -> p c", p=P)).then_inc(s["l_par"], 16)
                sp.dma_start(gbias[:, :], a["ml_gate_b_2"][0].rearrange("g h -> h g")).then_inc(s["l_par"], 16)
                g.prefetch(sp, first_unit + 8 + RING)

            @block.gpsimd
            def _(pool):
                pool.memset(mv[:, :, :, ML_D:ML_D + 1], 1.0).then_inc(s["l_ones"], 1)
                products.pool(pool)

            @block.tensor
            def _(pe):
                for n in range(8 + 5 * TT):
                    if 6 <= n < 6 + 8:
                        pe.wait_ge(s["l_raw"], n - 5)
                    elif n >= 6:
                        pe.wait_ge(s["l_tok"], n - 6 - 8 + 1)
                    products.pe(pe, n, g.bank[n % 6][:, :])
                for c in range(2):
                    products.pe(pe, 8 + 5 * TT + c, g.bank[6 + c][0:ML_H, :])

            @block.scalar
            def _(act):
                base = g.before(first_unit)
                products.act_start(act)
                n = 0
                for c in range(8):
                    if c % 4 == 3:
                        products.act_unit(act, c // 4 + 1)
                    act.wait_ge(g.dense, base + n + 1)
                    if c >= 4:
                        act.wait_ge(s["l_conv"], 4 * (c - 3))
                    act.activation(raw[:, c % 4, :], g.bank[n % 6][:, :], ACT.Copy).then_inc(s["l_raw"], 1)
                    n += 1
                for u in range(5):
                    for i in range(TT):
                        if i == TT - 1:
                            products.act_unit(act, 3 + u)
                        act.wait_ge(g.dense, base + n + 1)
                        if u < 4:
                            act.activation(tok[:, i, u * BANK:(u + 1) * BANK], g.bank[n % 6][:, :], ACT.Copy).then_inc(s["l_tok"], 1)
                        else:
                            act.activation(mv[:, i, :, 0:ML_D], g.bank[n % 6][:, :].rearrange("p (h w) -> p h w", w=ML_D), ACT.Copy).then_inc(s["l_tok"], 1)
                        n += 1
                act.wait_ge(s["l_par"], 48)
                for c, dst in enumerate((mi, mf)):
                    act.wait_ge(g.dense, base + n + c + 1)
                    act.activation(dst[:, :], g.bank[6 + c][0:ML_H, :], ACT.Identity, bias=gbias[:, c:c + 1]).then_inc(s["l_small"], 1)
                act.wait_ge(s["l_conv"], 4 * 8)
                for c in range(8):
                    act.activation(conv[:, c, :], conv[:, c, :], ACT.Silu).then_inc(s["l_cdone"], 1)

            @block.vector
            def _(dve):
                products.dve(dve)
                dve.wait_ge(s["l_par"], 48)
                for c in range(8):
                    dve.wait_ge(s["l_raw"], c + 1)
                    dve.tensor_scalar(conv[:, c, :], raw[:, c % 4, :], taps[:, 3, c:c + 1], cbias[:, c:c + 1], ALU.mult, ALU.add).then_inc(s["l_conv"], 1)
                    for back in range(1, CONV):
                        dve.wait_ge(s["l_conv"], 4 * c + back)
                        dve.scalar_tensor_tensor(conv[:, c, back:T], raw[:, c % 4, 0:T - back], taps[:, 3 - back, c:c + 1], conv[:, c, back:T],
                                                 ALU.mult, ALU.add).then_inc(s["l_conv"], 1)
                step = InOrder(dve, s["l_dve"])
                dve.wait_ge(s["l_conv"], 4 * 8)
                shape = [P, TT, 4, HALF]
                tmp = [raw[:, n, :].rearrange("p (i h w) -> p i h w", i=TT, w=HALF) for n in range(4)]
                for half in range(4):
                    dve.wait_ge(s["l_tok"], 4 if half < 2 else 8)
                    v = tok[:, :, half * 256:(half + 1) * 256].rearrange("p i (h w) -> p i h w", w=RD)
                    rotate(dve, step, v[:, :, :, 0:HALF], v[:, :, :, HALF:RD], g.cos[:, 1].unsqueeze(2).to_broadcast(shape),
                           g.sin[:, 1].unsqueeze(2).to_broadcast(shape), tmp)
                dve.sem_inc(s["l_rot"], 1)


def differential(g, tok):
    nc, a = g.nc, g.a
    q, k, v, y = tok[:, :, 0:BANK], tok[:, :, BANK:2 * BANK], tok[:, :, 2 * BANK:3 * BANK], tok[:, :, 0:BANK]
    qt, kt = g.ht[:, 0:4, :], g.ht[:, 4:8, :]
    units = [(h, i) for h in range(DA_H) for i in range(TT)]
    N = len(units)
    LAM0 = 0.8 - 0.6
    with ExitStack() as ctx:
        def sb(name, shape, dt=F32):
            return ctx.enter_context(nc.sbuf_tensor(name, shape, dt))
        p = sb("da_p", [P, 2, 2, T])
        diff = sb("da_a", [P, 2, T])
        pt = sb("da_pt", [P, 2, T])
        nmx, tot, inv = (sb(n, [P, 2, N]) for n in ("da_nmx", "da_sum", "da_inv"))
        lv = sb("da_lv", [P, 4, RD])
        prod = sb("da_prod", [P, 2, RD])
        dots, nlam = sb("da_dots", [P, 2]), sb("da_nlam", [P, 2])
        gain = sb("subln", [P, DV_W])
        ms, rms, rs = (sb(n, [P, TT * DA_H]) for n in ("da_ms", "da_rms", "da_rs"))
        with stage(nc, "m_par m_dve m_lam m_lexp flipped flip_out m_s0 m_s1 m_max m_e0 m_e1 m_a m_t m_pt m_o m_y m_sq m_root m_gain") as (block, s):
            @block.sync
            def _(sp):
                sp.dma_start(lv[:, :, :], a["da_lambda_2"][0:1].rearrange("o j w -> o (j w)").partition_broadcast(P)).then_inc(s["m_par"], 16)
                sp.dma_start(gain[:, :], a["da_subln_g_2"][0:1, :].partition_broadcast(P)).then_inc(s["m_par"], 16)

            @block.tensor
            def _(pe):
                flip_pairs(pe, g, s, q, k)
                pe.wait_ge(s["flip_out"], 8)

                def scores(u):
                    h, i = units[u]
                    keys = (i + 1) * P
                    for m in range(2):
                        if u >= 2:
                            pe.wait_ge(s[f"m_e{m}"], u - 1)
                        lo = RD * m
                        pe.matmul(g.bank[2 * m + u % 2][:, 0:keys], qt[lo:lo + RD, h, i * P:(i + 1) * P], kt[lo:lo + RD, h, 0:keys],
                                  start=True, stop=True).then_inc(s[f"m_s{m}"], 1)

                def flip(u):
                    keys = (units[u][1] + 1) * P
                    pe.wait_ge(s["m_a"], u + 1)
                    if u >= 2:
                        pe.wait_ge(s["m_pt"], u - 1)
                    for j in range(keys // P):
                        last = pe.transpose(g.bank[4 + u % 2][:, j * P:(j + 1) * P], diff[:, u % 2, j * P:(j + 1) * P], g.ident[:, :])
                    last.then_inc(s["m_t"], 1)

                def sums(u):
                    h, i = units[u]
                    pe.wait_ge(s["m_pt"], u + 1)
                    if u >= 2:
                        pe.wait_ge(s["m_y"], u - 1)
                    for j in range(i + 1):
                        last = pe.matmul(g.bank[6 + u % 2][:, 0:DV_W], pt[:, u % 2, j * P:(j + 1) * P], v[:, j, h * DV_W:(h + 1) * DV_W],
                                         start=(j == 0), stop=(j == i))
                    last.then_inc(s["m_o"], 1)
                scores(0)
                scores(1)
                for u in range(N):
                    if u + 2 < N:
                        scores(u + 2)
                    flip(u)
                    if u:
                        sums(u - 1)
                sums(N - 1)

            @block.scalar
            def _(act):
                act.wait_ge(s["m_lam"], 1)
                act.activation(nlam[:, :], dots[:, :], ACT.Exp).then_inc(s["m_lexp"], 1)
                for n in range(8):
                    act.wait_ge(s["flipped"], n + 1)
                    act.activation(g.ht[:, n, :], g.bank[n % 4][:, :], ACT.Copy, scale=RD ** -0.5 if n < 4 else 1.0).then_inc(s["flip_out"], 1)

                def exps(u):
                    keys = (units[u][1] + 1) * P
                    for m in range(2):
                        act.wait_ge(s["m_max"], 2 * u + m + 1)
                        if u >= 2:
                            act.wait_ge(s["m_a"], u - 1)
                        act.activation(p[:, u % 2, m, 0:keys], g.bank[2 * m + u % 2][:, 0:keys], ACT.Exp, bias=nmx[:, m, u:u + 1],
                                       accum_out=tot[:, m, u:u + 1]).then_inc(s[f"m_e{m}"], 1)

                def evac(u):
                    keys = (units[u][1] + 1) * P
                    act.wait_ge(s["m_t"], u + 1)
                    if u >= 2:
                        act.wait_ge(s["m_o"], u - 1)
                    act.activation(pt[:, u % 2, 0:keys], g.bank[4 + u % 2][:, 0:keys], ACT.Copy).then_inc(s["m_pt"], 1)

                def out(u):
                    h, i = units[u]
                    act.wait_ge(s["m_o"], u + 1)
                    act.activation(y[:, i, h * DV_W:(h + 1) * DV_W], g.bank[6 + u % 2][:, 0:DV_W], ACT.Copy).then_inc(s["m_y"], 1)
                exps(0)
                for u in range(N):
                    if u + 1 < N:
                        exps(u + 1)
                    evac(u)
                    if u:
                        out(u - 1)
                out(N - 1)
                act.wait_ge(s["m_sq"], 1)
                act.activation(rms[:, :], ms[:, :], ACT.Sqrt, scale=1.0 / DV_W, bias=g.eps[:, :]).then_inc(s["m_root"], 1)

            @block.vector
            def _(dve):
                step = InOrder(dve, s["m_dve"])
                dve.wait_ge(s["m_par"], 32)
                step(dve.tensor_tensor(prod[:, :, :], lv[:, 0:4:2, :], lv[:, 1:4:2, :], ALU.mult))
                dve.tensor_reduce(dots[:, :], prod[:, :, :], AX_X, ALU.add).then_inc(s["m_lam"], 1)
                dve.wait_ge(s["m_lexp"], 1)
                step(dve.tensor_tensor(nlam[:, 0:1], nlam[:, 1:2], nlam[:, 0:1], ALU.subtract))
                step(dve.tensor_scalar(nlam[:, 0:1], nlam[:, 0:1], LAM0, None, ALU.subtract))

                def mask(u):
                    at = slice(units[u][1] * P, (units[u][1] + 1) * P)
                    counts = []
                    for m in range(2):
                        b = g.bank[2 * m + u % 2]
                        dve.wait_ge(s[f"m_s{m}"], u + 1)
                        counts.append(step.put(dve.tensor_tensor(b[:, at], b[:, at], g.causal_neg[:, :], ALU.add)))
                    return counts

                def maxima(u, masked):
                    keys = (units[u][1] + 1) * P
                    for m in range(2):
                        step.need(masked[m])
                        dve.tensor_reduce(nmx[:, m, u:u + 1], g.bank[2 * m + u % 2][:, 0:keys], AX_X, ALU.max, negate=True).then_inc(s["m_max"], 1)
                maxima(0, mask(0))
                for u in range(N):
                    keys = (units[u][1] + 1) * P
                    if u + 1 < N:
                        masked = mask(u + 1)
                    dve.wait_ge(s["m_e0"], u + 1)
                    dve.wait_ge(s["m_e1"], u + 1)
                    inverse = step.put(dve.reciprocal(inv[:, :, u:u + 1], tot[:, :, u:u + 1]))
                    if u + 1 < N:
                        maxima(u + 1, masked)
                    step.need(inverse)
                    signed = step.put(dve.tensor_tensor(inv[:, 1, u:u + 1], inv[:, 1, u:u + 1], nlam[:, 0:1], ALU.mult))
                    if u >= 2:
                        dve.wait_ge(s["m_t"], u - 1)
                    first = step.put(dve.tensor_scalar(diff[:, u % 2, 0:keys], p[:, u % 2, 0, 0:keys], inv[:, 0, u:u + 1], None, ALU.mult))
                    step.need(max(signed, first))
                    dve.scalar_tensor_tensor(diff[:, u % 2, 0:keys], p[:, u % 2, 1, 0:keys], inv[:, 1, u:u + 1], diff[:, u % 2, 0:keys],
                                             ALU.mult, ALU.add).then_inc(s["m_a"], 1)
                dve.wait_ge(s["m_y"], N)
                whole = [P, TT, DA_H, DV_W]
                yv = y.rearrange("p i (h w) -> p i h w", w=DV_W)
                sq = k
                step(dve.tensor_tensor(sq, y, y, ALU.mult))
                dve.tensor_reduce(ms[:, :].rearrange("p (i h) -> p i h", h=DA_H), sq.rearrange("p i (h w) -> p i h w", w=DV_W), AX_X, ALU.add).then_inc(s["m_sq"], 1)
                dve.wait_ge(s["m_root"], 1)
                step(dve.reciprocal(rs[:, :], rms[:, :]))
                step(dve.tensor_scalar(gain[:, :], gain[:, :], 1.0 - LAM0, None, ALU.mult))
                step(dve.tensor_tensor(yv, yv, rs[:, :].rearrange("p (i h) -> p i h", h=DA_H).unsqueeze(3).to_broadcast(whole), ALU.mult))
                step(dve.tensor_tensor(yv, yv, gain[:, :].unsqueeze(1).unsqueeze(1).to_broadcast(whole), ALU.mult))


def mlstm(g, tok, mv, conv, mi, mf):
    nc, a = g.nc, g.a
    qt, kt = conv[:, 0:4, :], conv[:, 4:8, :]
    mo = tok[:, :, 3 * BANK:4 * BANK]
    with ExitStack() as ctx:
        def sb(name, shape, dt=F32):
            return ctx.enter_context(nc.sbuf_tensor(name, shape, dt))
        row = [sb(f"ml_row{n}", [ML_H, T]) for n in range(6)]
        sel = sb("ml_sel", [ML_H, ML_H, P])
        key_u = sb("ml_u", [P, TT, ML_H])
        floor = sb("ml_floor", [P, TT, ML_H])
        gap = sb("ml_gap", [P, 2, T])
        sd = sb("ml_sd", [P, 2, TT, T])
        y = sb("ml_y", [P, TT, ML_H, ML_D + 1])
        gain = sb("ml_gain", [P, BANK])
        den, neg, mu, var, rms, rs = (sb(n, [P, TT, ML_H]) for n in ("ml_den", "ml_neg", "ml_mu", "ml_var", "ml_rms", "ml_rs"))
        ones_row, absf, ex, logs, cum, run = row
        with stage(nc, "n_par n_pool n_sel n_abs n_exp n_log n_dve n_u n_m n_em n_em2 n_t n_tc n_mb n_gap n_e n_diag n_s n_sd n_o n_y n_sq n_root n_gate") as (block, s):
            @block.sync
            def _(sp):
                sp.dma_start(gain[:, :], a["ml_norm_g_2"][0:1, :].partition_broadcast(P)).then_inc(s["n_par"], 16)

            @block.gpsimd
            def _(pool):
                step = InOrder(pool, s["n_pool"])
                step(pool.memset(ones_row[:, :], 1.0))
                step(pool.memset(sel[:, :, :], 0.0))
                pool.affine_select(out=sel[:, :, :], in_=sel[:, :, :], compare_op=ALU.not_equal, fill=1.0, base=0,
                                   pattern=[[-1, ML_H], [0, P]], channel_multiplier=1).then_inc(s["n_sel"], 1)
                for h in range(ML_H):
                    for j in range(TT):
                        n = TT * h + j
                        pool.wait_ge(s["n_e"], n + 1)
                        pool.tensor_tensor(sd[:, h % 2, j, 0:P], sd[:, h % 2, j, 0:P], g.causal_t[:, :], ALU.mult).then_inc(s["n_diag"], 1)

            def weigh(dve, n):
                h, j = n // TT, n % TT
                w = T - j * P
                dve.wait_ge(s["n_s"], n + 1)
                dve.wait_ge(s["n_diag"], n + 1)
                at = sd[:, h % 2, j, 0:w]
                dve.scalar_tensor_tensor(at, g.bank[2 + n % 2][:, 0:w], ML_D ** -0.5, at, ALU.mult, ALU.mult).then_inc(s["n_sd"], 1)

            @block.vector
            def _(dve):
                step = InOrder(dve, s["n_dve"])
                dve.wait_ge(s["n_sel"], 1)
                dve.wait_ge(s["n_log"], 1)
                step(dve.tensor_scalar(absf[:, :], mf[:, :], 0.0, None, ALU.min))
                step(dve.tensor_tensor(logs[:, :], absf[:, :], logs[:, :], ALU.subtract))
                step(dve.tensor_tensor_scan(cum[:, :], ones_row[:, :], logs[:, :], 0.0, ALU.mult, ALU.add))
                step(dve.tensor_tensor(ex[:, :], mi[:, :], cum[:, :], ALU.subtract))
                step(dve.tensor_tensor_scan(run[:, :], ones_row[:, :], ex[:, :], 0.0, ALU.mult, ALU.max))
                dve.tensor_tensor(cum[:, :], cum[:, :], run[:, :], ALU.add).then_inc(s["n_m"], 1)
                dve.wait_ge(s["n_tc"], 2)
                for h in range(ML_H):
                    for j in range(TT):
                        n = TT * h + j
                        w = T - j * P
                        dve.wait_ge(s["n_mb"], h + 1)
                        if n >= 2:
                            dve.wait_ge(s["n_e"], n - 1)
                        dve.tensor_scalar(gap[:, n % 2, 0:w], g.bank[h % 2][:, j * P:T], key_u[:, j, h:h + 1], 0.0, ALU.subtract, ALU.max).then_inc(s["n_gap"], 1)
                        if n:
                            weigh(dve, n - 1)
                weigh(dve, ML_H * TT - 1)
                dve.wait_ge(s["n_y"], 2 * ML_H)
                whole = [P, TT, ML_H, ML_D]
                num = y[:, :, :, 0:ML_D]
                step(dve.tensor_scalar(neg[:], y[:, :, :, ML_D:ML_D + 1].rearrange("p i h o -> p i (h o)"), -1.0, None, ALU.mult))
                step(dve.tensor_tensor(den[:], neg[:], y[:, :, :, ML_D:ML_D + 1].rearrange("p i h o -> p i (h o)"), ALU.max))
                step(dve.tensor_tensor(den[:], den[:], floor[:], ALU.max))
                step(dve.reciprocal(neg[:], den[:]))
                step(dve.tensor_tensor(num, num, neg[:].unsqueeze(3).to_broadcast(whole), ALU.mult))
                step(dve.tensor_reduce(mu[:], num, AX_X, ALU.add))
                step(dve.tensor_scalar(mu[:], mu[:], 1.0 / ML_D, None, ALU.mult))
                step(dve.tensor_tensor(num, num, mu[:].unsqueeze(3).to_broadcast(whole), ALU.subtract))
                sq = sd[:, 0].rearrange("p i (h w) -> p i h w", w=ML_D)
                step(dve.tensor_tensor(sq, num, num, ALU.mult))
                dve.tensor_reduce(var[:], sq, AX_X, ALU.add).then_inc(s["n_sq"], 1)
                dve.wait_ge(s["n_root"], 1)
                step(dve.reciprocal(rs[:], rms[:]))
                step(dve.tensor_tensor(num, num, rs[:].unsqueeze(3).to_broadcast(whole), ALU.mult))
                dve.wait_ge(s["n_par"], 16)
                step(dve.tensor_tensor(num, num, gain[:, :].rearrange("p (h w) -> p h w", w=ML_D).unsqueeze(1).to_broadcast(whole), ALU.mult))
                dve.wait_ge(s["n_gate"], 1)
                mo4 = mo.rearrange("p i (h w) -> p i h w", w=ML_D)
                step(dve.tensor_tensor(mo4, num, mo4, ALU.mult))

            def outs(act, h):
                for b in range(2):
                    act.wait_ge(s["n_o"], 2 * h + b + 1)
                    act.activation(y[:, 2 * b:2 * b + 2, h, :], g.bank[4 + 2 * (h % 2) + b][:, 0:2 * (ML_D + 1)].rearrange("p (i w) -> p i w", w=ML_D + 1),
                                   ACT.Copy).then_inc(s["n_y"], 1)

            @block.scalar
            def _(act):
                act.activation(absf[:, :], mf[:, :], ACT.Abs).then_inc(s["n_abs"], 1)
                act.wait_ge(s["n_abs"], 1)
                act.activation(ex[:, :], absf[:, :], ACT.Exp, scale=-1.0).then_inc(s["n_exp"], 1)
                act.wait_ge(s["n_exp"], 1)
                act.activation(logs[:, :], ex[:, :], ACT.Ln, bias=g.ones[0:ML_H, 0:1]).then_inc(s["n_log"], 1)
                act.wait_ge(s["n_m"], 1)
                act.activation(cum[:, :], cum[:, :], ACT.Exp, scale=-1.0).then_inc(s["n_em"], 1)
                act.wait_ge(s["n_t"], 1)
                act.activation(key_u[:], g.bank[4][:, 0:TT * ML_H].rearrange("p (i h) -> p i h", h=ML_H), ACT.Copy).then_inc(s["n_tc"], 1)
                act.activation(floor[:], g.bank[4][:, 256:256 + TT * ML_H].rearrange("p (i h) -> p i h", h=ML_H), ACT.Copy).then_inc(s["n_tc"], 1)
                for h in range(ML_H):
                    for j in range(TT):
                        n = TT * h + j
                        w = T - j * P
                        act.wait_ge(s["n_gap"], n + 1)
                        if h >= 2 and j == 0:
                            act.wait_ge(s["n_o"], 2 * (h - 1))
                        act.activation(sd[:, h % 2, j, 0:w], gap[:, n % 2, 0:w], ACT.Exp, scale=-1.0).then_inc(s["n_e"], 1)
                    if h:
                        outs(act, h - 1)
                outs(act, ML_H - 1)
                act.activation(mo, mo, ACT.Sigmoid).then_inc(s["n_gate"], 1)
                act.wait_ge(s["n_sq"], 1)
                act.activation(rms[:], var[:], ACT.Sqrt, scale=1.0 / ML_D, bias=g.eps[:, :]).then_inc(s["n_root"], 1)

            @block.tensor
            def _(pe):
                pe.wait_ge(s["n_em"], 1)
                for i in range(TT):
                    pe.transpose(g.bank[4][:, i * ML_H:(i + 1) * ML_H], ex[:, i * P:(i + 1) * P], g.ident[0:ML_H, 0:ML_H])
                    last = pe.transpose(g.bank[4][:, 256 + i * ML_H:256 + (i + 1) * ML_H], cum[:, i * P:(i + 1) * P], g.ident[0:ML_H, 0:ML_H])
                last.then_inc(s["n_t"], 1)

                def rows(h):
                    if h >= 2:
                        pe.wait_ge(s["n_gap"], TT * (h - 1))
                    pe.matmul(g.bank[h % 2][:, :], sel[:, h, :], run[:, :], start=True, stop=True).then_inc(s["n_mb"], 1)

                def sums(h):
                    pe.wait_ge(s["n_sd"], TT * (h + 1))
                    if h >= 2:
                        pe.wait_ge(s["n_y"], 2 * (h - 1))
                    for b in range(2):
                        for i in (2 * b, 2 * b + 1):
                            for j in range(i + 1):
                                last = pe.matmul(g.bank[4 + 2 * (h % 2) + b][:, (i % 2) * (ML_D + 1):(i % 2 + 1) * (ML_D + 1)],
                                                 sd[:, h % 2, j, (i - j) * P:(i - j + 1) * P], mv[:, j, h, :], start=(j == 0), stop=(j == i))
                        last.then_inc(s["n_o"], 1)
                rows(0)
                rows(1)
                pe.wait_ge(s["n_tc"], 2)
                for h in range(ML_H):
                    for j in range(TT):
                        n = TT * h + j
                        if n >= 2:
                            pe.wait_ge(s["n_sd"], n - 1)
                        pe.matmul(g.bank[2 + n % 2][:, 0:T - j * P], kt[:, h, j * P:(j + 1) * P], qt[:, h, j * P:T], start=True, stop=True).then_inc(s["n_s"], 1)
                    if h + 2 < ML_H:
                        rows(h + 2)
                    if h:
                        sums(h - 1)
                sums(ML_H - 1)


def cross_attention(g, first_unit, mem_kt, mem_v):
    nc, a = g.nc, g.a
    MT = MEM // P
    base = g.before(first_unit)
    with ExitStack() as ctx:
        def sb(name, shape, dt=F32):
            return ctx.enter_context(nc.sbuf_tensor(name, shape, dt))
        kt = sb("x_kt", [P, DC, MEM])
        v = sb("x_v", [P, MT, D])
        qt = sb("x_qt", [P, DC, T])
        with ExitStack() as inner:
            norm_transposed(g, None, None, inner, gain_src=a["norm_x_g_2"][0])
        with ExitStack() as local, stage(nc, "p_out p_kv" + Products.SEMS) as (block, s):
            products = Products(g, local, s, first_unit, [(n // 4, True, chunk(n % 4), WHOLE) for n in range(DC)])

            @block.gpsimd
            def _(pool):
                products.pool(pool)

            @block.vector
            def _(dve):
                products.dve(dve)

            @block.sync
            def _(sp):
                sp.dma_start(kt[:].rearrange("p a b -> p (a b)"), mem_kt).then_inc(s["p_kv"], 16)
                sp.dma_start(v[:].rearrange("p a b -> p (a b)"), mem_v).then_inc(s["p_kv"], 16)
                g.prefetch(sp, first_unit + 2 + RING)
                sp.wait_ge(s["p_kv"], 32)

            @block.tensor
            def _(pe):
                for n in range(DC):
                    products.pe(pe, n, g.bank[n][:, :])

            @block.scalar
            def _(act):
                products.act_start(act)
                for n in range(DC):
                    if n == 3:
                        products.act_unit(act, 1)
                    act.wait_ge(g.dense, base + n + 1)
                    act.activation(qt[:, n, :], g.bank[n][:, :], ACT.Copy).then_inc(s["p_out"], 1)
        y = sb("x_y", [P, TT, D])
        units = [([qt[:, 2 * h + c, i * P:(i + 1) * P] for c in range(2)], [kt[:, 2 * h + c, :] for c in range(2)], MEM, False,
                  [v[:, j, h * X_D:(h + 1) * X_D] for j in range(MT)], y[:, i, h * X_D:(h + 1) * X_D])
                 for h in range(X_H) for i in range(TT)]
        with stage(nc, ATTN_SEMS) as (block, s):
            at = Attention(g, ctx, units, X_D ** -0.5, s)

            @block.sync
            def _(sp):
                pass

            @block.tensor
            def _(pe):
                at.pe(pe)

            @block.vector
            def _(dve):
                at.dve(dve)

            @block.scalar
            def _(act):
                at.act(act)
        with ExitStack() as local:
            mix_out(g, lambda k: y[:, :, k * P:(k + 1) * P], first_unit + 2, None, local)


RG = NG + NE


def route(g, xn_tiles, x_rows, table, slot, result, weight, slots, over):
    nc, a = g.nc, g.a
    with ExitStack() as ctx:
        def sb(name, shape, dt=F32):
            return ctx.enter_context(nc.sbuf_tensor(name, shape, dt))
        w = sb("router_w", [P, DC, RG])
        bias = sb("router_b", [P, RG])
        logit = sb("logit", [P, TT, RG])
        gl = sb("group_logit", [P, TT, 8])
        g_top, e_top = sb("g_top", [P, TT, 8]), sb("e_top", [P, TT, 8])
        g_at, e_at = sb("g_at", [P, TT, 8], U32), sb("e_at", [P, TT, 8], U32)
        g_num, e_num = sb("g_num", [P, TT, 1]), sb("e_num", [P, TT, 2])
        ex = sb("g_exp", [P, TT, NG])
        gw, ratio, one_plus = sb("g_w", [P, TT, 1]), sb("ratio", [P, TT, 1]), sb("one_plus", [P, TT, 1])
        pick = sb("pick", [P, TT, NG])
        cross = sb("cross", [P, TT, EG, NG])
        el = sb("e_logit", [P, TT, EG])
        hit = sb("e_hit", [P, 2, TT, NE])
        both = sb("e_both", [P, TT, NE])
        before = sb("strictly_before", [P, P])
        pos = sb("e_pos", [P, TT, NE])
        prod = sb("e_prod", [P, TT, NE])
        place = sb("e_place", [P, TT, 2])
        at_row, blk = sb("e_row", [P, TT, 2]), sb("e_blk", [P, TT, 2])
        token = sb("token", [P, TT])
        token_i = sb("token_i", [P, TT], I32)
        zero = sb("zeros", [P, P])
        rows = sb("list_rows", [P, P])
        count, most = sb("count", [P, NE]), sb("most", [P, 1])
        whole8 = [P, TT, 8]
        with stage(nc, "q_w q_pool q_ready q_zero q_mm q_dve q_pair q_red q_exp q_exp2 q_hits q_pos q_slot q_sent q_clear q_rows q_flip q_x") as (block, s):
            @block.sync
            def _(sp):
                sp.dma_start(w[:, :, 0:NG], a["w_router_group_2"][0].rearrange("(k p) n -> p k n", p=P)).then_inc(s["q_w"], 16)
                sp.dma_start(w[:, :, NG:RG], a["w_router_expert_2"][0].rearrange("(k p) n -> p k n", p=P)).then_inc(s["q_w"], 16)
                sp.dma_start(bias[:, 0:NG], a["b_router_group_2"][0:1, :].partition_broadcast(P)).then_inc(s["q_w"], 16)
                sp.dma_start(bias[:, NG:RG], a["b_router_expert_2"][0:1, :].partition_broadcast(P)).then_inc(s["q_w"], 16)
                sp.dma_start(x_rows.rearrange("(i p) d -> p i d", p=P), xn_tiles[:, :, :]).then_inc(s["q_x"], 16)
                sp.wait_ge(s["q_zero"], 1)
                sp.dma_start(table.rearrange("(r p) o -> r (p o)", p=P), zero[:, :]).then_inc(s["q_clear"], 16)
                sp.wait_ge(s["q_sent"], 16 * 2 * TT)
                sp.dma_start(rows[:, :], table.rearrange("(r p) o -> r (p o)", p=P)).then_inc(s["q_rows"], 16)
                sp.wait_ge(s["q_x"], 16)

            @block.gpsimd
            def _(pool):
                step = InOrder(pool, s["q_pool"])
                pool.memset(zero[:, :], 0.0).then_inc(s["q_zero"], 1)
                step(pool.memset(gl[:, :, :], LOW))
                step(pool.iota(token_i[:, :], pattern=[[P, TT]], base=0, channel_multiplier=1))
                step(pool.tensor_copy(token[:, :], token_i[:, :]))
                pool.tensor_tensor(before[:, :], g.causal_t[:, :], g.ident[:, :], ALU.subtract).then_inc(s["q_ready"], 1)
                pool.wait_ge(s["q_slot"], 1)
                pool.wait_ge(s["q_clear"], 16)
                for i in range(TT):
                    for c in range(2):
                        pool.indirect_dma_start(out=table, out_offset=bass.IndirectOffsetOnAxis(ap=slot[:, c, i:i + 1], axis=0),
                                                in_=token[:, i:i + 1], in_offset=None).then_inc(s["q_sent"], 16)

            @block.tensor
            def _(pe):
                pe.wait_ge(s["q_w"], 64)
                for i in range(TT):
                    for k in range(DC):
                        last = pe.matmul(g.bank[0][:, i * 64:i * 64 + RG], g.ht[:, k, i * P:(i + 1) * P], w[:, k, :], start=(k == 0), stop=(k == DC - 1))
                last.then_inc(s["q_mm"], 1)
                pe.wait_ge(s["q_hits"], 1)
                pe.wait_ge(s["q_ready"], 1)
                for i in range(TT):
                    for j in range(i + 1):
                        pe.matmul(g.bank[1][:, i * NE:(i + 1) * NE], before[:, :] if j == i else g.ones[:, :], both[:, j, :],
                                  start=(j == 0), stop=(j == i))
                for j in range(TT):
                    last = pe.matmul(g.bank[1][:, TT * NE:(TT + 1) * NE], g.ones[:, :], both[:, j, :], start=(j == 0), stop=(j == TT - 1))
                last.then_inc(s["q_pos"], 1)
                pe.wait_ge(s["q_rows"], 16)
                pe.transpose(g.bank[2][:, 0:P], rows[:, :], g.ident[:, :]).then_inc(s["q_flip"], 1)

            @block.scalar
            def _(act):
                act.wait_ge(s["q_exp"], 1)
                act.activation(ex[:], ex[:], ACT.Exp).then_inc(s["q_exp"], 1)
                act.wait_ge(s["q_exp2"], 1)
                act.activation(ratio[:], ratio[:], ACT.Exp).then_inc(s["q_exp2"], 1)

            @block.vector
            def _(dve):
                step = InOrder(dve, s["q_dve"])
                dve.wait_ge(s["q_mm"], 1)
                step(dve.tensor_tensor(logit[:], g.bank[0][:, 0:TT * 64].rearrange("p (i n) -> p i n", n=64)[:, :, 0:RG],
                                       bias[:, :].unsqueeze(1).to_broadcast([P, TT, RG]), ALU.add))
                dve.wait_ge(s["q_ready"], 1)
                step(dve.tensor_copy(gl[:, :, 0:NG], logit[:, :, 0:NG]))
                for i in range(TT):
                    step(dve.max(g_top[:, i, :], gl[:, i, :]))
                    step(dve.max_index(g_at[:, i, :], g_top[:, i, :], gl[:, i, :]))
                dve.tensor_tensor(ex[:], logit[:, :, 0:NG], g_top[:, :, 0:1].to_broadcast([P, TT, NG]), ALU.subtract).then_inc(s["q_exp"], 1)
                step(dve.tensor_copy(g_num[:], g_at[:, :, 0:1]))
                step(dve.tensor_tensor(pick[:], g.iota_p[:, 0:NG].unsqueeze(1).to_broadcast([P, TT, NG]), g_num[:].to_broadcast([P, TT, NG]), ALU.is_equal))
                step(dve.tensor_tensor(cross[:], logit[:, :, NG:RG].rearrange("p i (g e) -> p i e g", e=EG),
                                       pick[:].unsqueeze(2).to_broadcast([P, TT, EG, NG]), ALU.mult))
                step(dve.tensor_reduce(el[:], cross[:], AX_X, ALU.add))
                for i in range(TT):
                    step(dve.max(e_top[:, i, :], el[:, i, :]))
                    step(dve.max_index(e_at[:, i, :], e_top[:, i, :], el[:, i, :]))
                dve.tensor_tensor(ratio[:], e_top[:, :, 1:2], e_top[:, :, 0:1], ALU.subtract).then_inc(s["q_exp2"], 1)
                step(dve.tensor_copy(e_num[:], e_at[:, :, 0:2]))
                step(dve.scalar_tensor_tensor(e_num[:], g_num[:].to_broadcast([P, TT, 2]), float(EG), e_num[:], ALU.mult, ALU.add))
                for c in range(2):
                    step(dve.tensor_tensor(hit[:, c], g.iota_p[:, 0:NE].unsqueeze(1).to_broadcast([P, TT, NE]),
                                           e_num[:, :, c:c + 1].to_broadcast([P, TT, NE]), ALU.is_equal))
                dve.tensor_tensor(both[:], hit[:, 0], hit[:, 1], ALU.add).then_inc(s["q_hits"], 1)
                dve.wait_ge(s["q_exp"], 2)
                step(dve.tensor_reduce(gw[:].rearrange("p i o -> p (i o)"), ex[:], AX_X, ALU.add))
                dve.wait_ge(s["q_exp2"], 2)
                step(dve.tensor_scalar(one_plus[:], ratio[:], 1.0, None, ALU.add))
                step(dve.tensor_tensor(one_plus[:], one_plus[:], gw[:], ALU.mult))
                step(dve.reciprocal(weight[:, :, 0:1], one_plus[:]))
                step(dve.tensor_tensor(weight[:, :, 1:2], weight[:, :, 0:1], ratio[:], ALU.mult))
                dve.wait_ge(s["q_pos"], 1)
                step(dve.tensor_copy(pos[:], g.bank[1][:, 0:TT * NE].rearrange("p (i e) -> p i e", e=NE)))
                step(dve.tensor_copy(count[:, :], g.bank[1][:, TT * NE:(TT + 1) * NE]))
                for c in range(2):
                    step(dve.tensor_tensor(prod[:], hit[:, c], pos[:], ALU.mult))
                    step(dve.tensor_reduce(place[:, :, c:c + 1].rearrange("p i o -> p (i o)"), prod[:], AX_X, ALU.add))
                step(dve.tensor_copy(at_row[:], place[:]))
                step(dve.scalar_tensor_tensor(place[:], e_num[:], float(CAP), place[:], ALU.mult, ALU.add))
                dve.tensor_copy(slot[:, :, :], place[:].rearrange("p i c -> p c i")).then_inc(s["q_slot"], 1)
                step(dve.tensor_scalar(blk[:], at_row[:], float(P), None, ALU.is_ge))
                for b in range(2, CAP // P):
                    step(dve.scalar_tensor_tensor(blk[:], at_row[:], float(b * P), blk[:], ALU.is_ge, ALU.add))
                step(dve.scalar_tensor_tensor(at_row[:], blk[:], float((NE - 1) * P), at_row[:], ALU.mult, ALU.add))
                step(dve.scalar_tensor_tensor(at_row[:], e_num[:], float(P), at_row[:], ALU.mult, ALU.add))
                step(dve.tensor_copy(result[:, :, :], at_row[:].rearrange("p i c -> p c i")))
                step(dve.tensor_reduce(most[:, :], count[:, :], AX_X, ALU.max))
                step(dve.tensor_scalar(most[:, :], most[:, :], float(P), None, ALU.is_gt))
                step(dve.tensor_copy(over[:, :], most[:, :]))
                dve.wait_ge(s["q_flip"], 1)
                step(dve.tensor_copy(slots[:, :], g.bank[2][:, 0:P]))


MOE_SEMS = (" r_w1_0 r_w1_1 r_w3_0 r_w3_1 r_w2_0 r_w2_1 r_x0 r_x1 r_st0 r_st1 r_paced r_idx r_xt r_xc r_h1 r_h3"
            " r_act r_z r_zt r_zc r_y r_yc")


class Experts:

    def __init__(self, g, ctx, s, w13, w2, slots, x_rows, y_rows, gain):
        self.g, self.s, self.w13, self.w2, self.slots = g, s, w13, w2, slots
        self.x_rows, self.y_rows, self.gain = x_rows, y_rows, gain

        def sb(name, shape, dt=F32):
            return ctx.enter_context(g.nc.sbuf_tensor(fresh(name), shape, dt))
        self.idx = sb("moe_idx", [P, 2], U32)
        self.rows = sb("moe_rows", [P, 2, D])
        self.xt = sb("moe_xt", [P, 2, DC, P])
        self.sil = sb("moe_silu", [P, 2, FE])
        self.z = sb("moe_z", [P, 2, FE])
        self.zt = sb("moe_zt", [P, 2, FC, P])
        self.y = sb("moe_y", [P, 2, D])

    def load(self, sp, e, n, par, first):
        s, a = self.s, self.g.a
        if not first:
            sp.wait_ge(s["r_h1"], n - 1)
        sp.dma_start(self.w13[par][0][:, :, :], a["w1_2"][0][bass.ds(e, 1)].rearrange("o (k p) n -> p (o k) n", p=P)).then_inc(s[f"r_w1_{par}"], 16)
        if not first:
            sp.wait_ge(s["r_h3"], n - 1)
        sp.dma_start(self.w13[par][1][:, :, :], a["w3_2"][0][bass.ds(e, 1)].rearrange("o (k p) n -> p (o k) n", p=P)).then_inc(s[f"r_w3_{par}"], 16)
        if not first:
            sp.wait_ge(s["r_y"], 2 * (n - 1))
        sp.dma_start(self.w2[par][:, :].rearrange("p (k n) -> p k n", k=FC), a["w2_2"][0][bass.ds(e, 1)].rearrange("o (k p) n -> p (o k) n", p=P)).then_inc(s[f"r_w2_{par}"], 16)

    def gather(self, pool, col, n, par, half, first):
        s = self.s
        if not first:
            pool.wait_ge(s[f"r_x{par}"], half * 16)
            pool.wait_ge(s["r_xt"], 2 * (n - 1))
        pool.tensor_copy(self.idx[:, par:par + 1], self.slots[:, bass.ds(col, 1)]).then_inc(s["r_idx"], 1)
        pool.wait_ge(s["r_idx"], n + 1)
        pool.sem_inc(s["r_paced"], 1)
        pool.indirect_dma_start(out=self.rows[:, par, :], out_offset=None, in_=self.x_rows,
                                in_offset=bass.IndirectOffsetOnAxis(ap=self.idx[:, par:par + 1], axis=0)).then_inc(s[f"r_x{par}"], 16)

    def flip_rows(self, pe, n, par, half, first):
        s, g = self.s, self.g
        pe.wait_ge(s[f"r_x{par}"], (half + 1) * 16)
        for b in range(2):
            if not first:
                pe.wait_ge(s["r_xc"], 2 * (n - 1) + b + 1)
            for k in range(4):
                last = pe.transpose(g.bank[b][:, k * P:(k + 1) * P], self.rows[:, par, (4 * b + k) * P:(4 * b + k + 1) * P], g.ident[:, :])
            last.then_inc(s["r_xt"], 1)

    def up(self, pe, which, n, par, wait, first):
        s, g = self.s, self.g
        pe.wait_ge(s[f"r_w{which}_{par}"], wait)
        pe.wait_ge(s["r_xc"], 2 * n + 2)
        if not first:
            pe.wait_ge(s["r_act"] if which == 1 else s["r_z"], n)
        for k in range(DC):
            last = pe.matmul(g.bank[2 if which == 1 else 3][:, :], self.xt[:, par, k, :], self.w13[par][0 if which == 1 else 1][:, k, :],
                             start=(k == 0), stop=(k == DC - 1))
        last.then_inc(s[f"r_h{which}"], 1)

    def flip_z(self, pe, n, par, first):
        s, g = self.s, self.g
        pe.wait_ge(s["r_z"], n + 1)
        if not first:
            pe.wait_ge(s["r_zc"], n)
        for k in range(FC):
            last = pe.transpose(g.bank[4][:, k * P:(k + 1) * P], self.z[:, par, k * P:(k + 1) * P], g.ident[:, :])
        last.then_inc(s["r_zt"], 1)

    def down(self, pe, n, par, wait, first):
        s, g = self.s, self.g
        pe.wait_ge(s[f"r_w2_{par}"], wait)
        pe.wait_ge(s["r_zc"], n + 1)
        for c in range(2):
            if not first:
                pe.wait_ge(s["r_yc"], 2 * (n - 1) + c + 1)
            for k in range(FC):
                last = pe.matmul(g.bank[5 + c][:, :], self.zt[:, par, k, :], self.w2[par][:, k * D + c * BANK:k * D + (c + 1) * BANK],
                                 start=(k == 0), stop=(k == FC - 1))
            last.then_inc(s["r_y"], 1)

    def act_front(self, act, n, par, early):
        s, g = self.s, self.g
        act.wait_ge(s["r_h1"], n + 1)
        if not early:
            act.wait_ge(s["r_z"], n - 1)
        act.activation(self.sil[:, par, :], g.bank[2][:, :], ACT.Silu).then_inc(s["r_act"], 1)

    def act_back(self, act, n, par, half, early):
        s, g = self.s, self.g
        act.wait_ge(s["r_zt"], n + 1)
        if not early:
            act.wait_ge(s["r_y"], 2 * (n - 1))
        act.activation(self.zt[:, par, :, :].rearrange("p k t -> p (k t)"), g.bank[4][:, :], ACT.Copy).then_inc(s["r_zc"], 1)
        if not early:
            act.wait_ge(s[f"r_st{par}"], half * 16)
        for c in range(2):
            act.wait_ge(s["r_y"], 2 * n + c + 1)
            act.activation(self.y[:, par, c * BANK:(c + 1) * BANK], g.bank[5 + c][:, :], ACT.Copy).then_inc(s["r_yc"], 1)

    def dve_rows(self, dve, n, par, early):
        s, g = self.s, self.g
        if not early:
            dve.wait_ge(s["r_h3"], n - 1)
        for b in range(2):
            dve.wait_ge(s["r_xt"], 2 * n + b + 1)
            dve.tensor_tensor(self.xt[:, par, 4 * b:4 * b + 4, :], g.bank[b][:, :].rearrange("p (k t) -> p k t", t=P),
                              self.gain[:, 4 * b:4 * b + 4].unsqueeze(2).to_broadcast([P, 4, P]), ALU.mult).then_inc(s["r_xc"], 1)

    def dve_gate(self, dve, n, par, early):
        s, g = self.s, self.g
        dve.wait_ge(s["r_act"], n + 1)
        dve.wait_ge(s["r_h3"], n + 1)
        if not early:
            dve.wait_ge(s["r_zt"], n - 1)
        dve.tensor_tensor(self.z[:, par, :], g.bank[3][:, :], self.sil[:, par, :], ALU.mult).then_inc(s["r_z"], 1)

    def store(self, q, row, n, par):
        s = self.s
        q.wait_ge(s["r_yc"], 2 * n + 2)
        q.dma_start(self.y_rows[bass.ds(row, P), :], self.y[:, par, :]).then_inc(s[f"r_st{par}"], 16)


def run_experts(g, w13, w2, slots, x_rows, y_rows, gain):
    nc = g.nc
    BLOCKS = CAP // P
    PEEL = 4
    with ExitStack() as ctx, stage(nc, MOE_SEMS) as (block, s):
        m = Experts(g, ctx, s, w13, w2, slots, x_rows, y_rows, gain)

        @block.sync
        def _(sp):
            for n in range(PEEL):
                m.load(sp, n, n, n % 2, n < 2)
            with sp.Fori(PEEL // 2, NE // 2) as it:
                for par in range(2):
                    m.load(sp, it * 2 + par, it * 2 + par, par, False)

        @block.gpsimd
        def _(pool):
            for n in range(PEEL):
                m.gather(pool, n * BLOCKS, n, n % 2, n // 2, n < 2)
            with pool.Fori(PEEL // 2, NE // 2) as it:
                for par in range(2):
                    n = it * 2 + par
                    m.gather(pool, n * BLOCKS, n, par, it, False)

        def products(pe, n, par, half, first, one, last):
            m.up(pe, 1, n, par, (half + 1) * 16, first)
            if not first:
                m.flip_z(pe, n - 1, 1 - par, one)
            m.up(pe, 3, n, par, (half + 1) * 16, first)
            if not last:
                m.flip_rows(pe, n + 1, 1 - par, half + par, False)
            if not first:
                m.down(pe, n - 1, 1 - par, (half + par) * 16, one)

        @block.tensor
        def _(pe):
            m.flip_rows(pe, 0, 0, 0, True)
            for n in range(PEEL):
                products(pe, n, n % 2, n // 2, n == 0, n == 1, False)
            with pe.Fori(PEEL // 2, NE // 2 - 1) as it:
                for par in range(2):
                    products(pe, it * 2 + par, par, it, False, False, False)
            for n in (NE - 2, NE - 1):
                products(pe, n, n % 2, n // 2, False, False, n == NE - 1)
            m.flip_z(pe, NE - 1, 1, False)
            m.down(pe, NE - 1, 1, NE // 2 * 16, False)

        def act_block(act, n, par, half, early, before_early, first):
            m.act_front(act, n, par, early)
            if not first:
                m.act_back(act, n - 1, 1 - par, half + par - 1, before_early)
                m.store(act, (n - 1) * P, n - 1, 1 - par)

        @block.scalar
        def _(act):
            for n in range(PEEL):
                act_block(act, n, n % 2, n // 2, n < 2, n - 1 < 2, n == 0)
            with act.Fori(PEEL // 2, NE // 2) as it:
                for par in range(2):
                    act_block(act, it * 2 + par, par, it, False, False, False)
            m.act_back(act, NE - 1, 1, NE // 2 - 1, False)
            m.store(act, (NE - 1) * P, NE - 1, 1)
            for par in range(2):
                act.wait_ge(s[f"r_st{par}"], NE // 2 * 16)

        @block.vector
        def _(dve):
            m.dve_rows(dve, 0, 0, True)
            for n in range(1, PEEL):
                m.dve_rows(dve, n, n % 2, n < 2)
                m.dve_gate(dve, n - 1, 1 - n % 2, n - 1 < 2)
            with dve.Fori(PEEL // 2, NE // 2) as it:
                for par in range(2):
                    m.dve_rows(dve, it * 2 + par, par, False)
                    m.dve_gate(dve, it * 2 + par - 1, 1 - par, False)
            m.dve_gate(dve, NE - 1, 1, False)


def run_overflow(g, over, w13, w2, slots, x_rows, y_rows, gain):
    nc = g.nc
    BLOCKS = CAP // P
    MORE = BLOCKS - 1
    with ExitStack() as ctx, stage(nc, MOE_SEMS) as (block, s):
        m = Experts(g, ctx, s, w13, w2, slots, x_rows, y_rows, gain)

        def guarded(eng, body):
            flag = eng.value_load(over[0:1, 0:1], min_val=0, max_val=1)
            with eng.If(flag > 0):
                body(eng)
            with eng.Else():
                eng.nop()
            eng.nop()

        def blocks(eng, each):
            with eng.Fori(0, NE) as e:
                for r in range(MORE):
                    each(e, r, e * MORE + r, e * BLOCKS + r + 1)

        def load(sp):
            with sp.Fori(0, NE) as e:
                sp.wait_ge(s["r_st0"], (e * MORE + 1) * 16)
                m.load(sp, e, e, 0, True)

        def gather(pool):
            pool.sem_inc(s["r_st0"], 16)

            def each(e, r, n, col):
                pool.wait_ge(s["r_st0"], (n + 1) * 16)
                m.gather(pool, col, n, 0, n, True)
            blocks(pool, each)

        def products(pe):
            def each(e, r, n, col):
                m.flip_rows(pe, n, 0, n, True)
                m.up(pe, 1, n, 0, (e + 1) * 16, True)
                m.up(pe, 3, n, 0, (e + 1) * 16, True)
                m.flip_z(pe, n, 0, True)
                m.down(pe, n, 0, (e + 1) * 16, True)
            blocks(pe, each)

        def activations(act):
            def each(e, r, n, col):
                m.act_front(act, n, 0, True)
                m.act_back(act, n, 0, n, True)
                m.store(act, e * P + (r + 1) * NE * P, n, 0)
            blocks(act, each)
            act.wait_ge(s["r_st0"], (NE * MORE + 1) * 16)

        def gates(dve):
            def each(e, r, n, col):
                m.dve_rows(dve, n, 0, True)
                m.dve_gate(dve, n, 0, True)
            blocks(dve, each)

        @block.sync
        def _(sp):
            guarded(sp, load)

        @block.gpsimd
        def _(pool):
            guarded(pool, gather)

        @block.tensor
        def _(pe):
            guarded(pe, products)

        @block.scalar
        def _(act):
            guarded(act, activations)

        @block.vector
        def _(dve):
            guarded(dve, gates)


def finish(g, result, weight, y_rows, over, out):
    nc, a = g.nc, g.a
    with ExitStack() as ctx:
        def sb(name, shape, dt=F32):
            return ctx.enter_context(nc.sbuf_tensor(name, shape, dt))
        got = sb("got", [P, 4, D])
        sq = sb("out_sq", [P, TT, D])
        res = sb("out_rows", [P, TT, D])
        gain = sb("out_gain", [P, D])
        ss, rms, rs = (sb(n, [P, TT]) for n in ("out_ss", "out_rms", "out_rs"))
        with stage(nc, "t_gain t_g0 t_g1 t_g2 t_g3 t_add t_sq t_root t_rs t_out t_stored") as (block, s):
            @block.sync
            def _(sp):
                sp.dma_start(gain[:, :], a["norm_final_g_2"].unsqueeze(0).partition_broadcast(P)).then_inc(s["t_gain"], 16)
                rows = out[0].rearrange("(i p) d -> p i d", p=P)
                for i in range(TT):
                    sp.wait_ge(s["t_out"], i + 1)
                    sp.dma_start(rows[:, i, :], res[:, i, :]).then_inc(s["t_stored"], 16)
                sp.wait_ge(s["t_stored"], 16 * TT)

            @block.gpsimd
            def _(pool):
                def gather(rows):
                    for n in range(2 * TT):
                        if n >= 4:
                            pool.wait_ge(s["t_add"], n - 3)
                        i, c = n // 2, n % 2
                        pool.indirect_dma_start(out=got[:, n % 4, :], out_offset=None, in_=rows,
                                                in_offset=bass.IndirectOffsetOnAxis(ap=result[:, c, i:i + 1], axis=0)).then_inc(s[f"t_g{n % 4}"], 16)
                flag = pool.value_load(over[0:1, 0:1], min_val=0, max_val=1)
                with pool.If(flag > 0):
                    gather(y_rows)
                with pool.Else():
                    gather(y_rows[0:NE * P, :])
                pool.nop()

            @block.vector
            def _(dve):
                for n in range(2 * TT):
                    i, c = n // 2, n % 2
                    dve.wait_ge(s[f"t_g{n % 4}"], 16 * (n // 4 + 1))
                    if n:
                        dve.wait_ge(s["t_add"], n)
                    dve.scalar_tensor_tensor(g.x[:, i, :], got[:, n % 4, :], weight[:, i, c:c + 1], g.x[:, i, :], ALU.mult, ALU.add).then_inc(s["t_add"], 1)
                dve.wait_ge(s["t_gain"], 16)
                for i in range(TT):
                    dve.wait_ge(s["t_root"], i + 1)
                    dve.reciprocal(rs[:, i:i + 1], rms[:, i:i + 1]).then_inc(s["t_rs"], 1)
                    dve.wait_ge(s["t_rs"], i + 1)
                    dve.scalar_tensor_tensor(res[:, i, :], g.x[:, i, :], rs[:, i:i + 1], gain[:, :], ALU.mult, ALU.mult).then_inc(s["t_out"], 1)

            @block.scalar
            def _(act):
                for i in range(TT):
                    act.wait_ge(s["t_add"], 2 * i + 2)
                    act.activation(sq[:, i, :], g.x[:, i, :], ACT.Square, accum_out=ss[:, i:i + 1]).then_inc(s["t_sq"], 1)
                    act.wait_ge(s["t_sq"], i + 1)
                    act.activation(rms[:, i:i + 1], ss[:, i:i + 1], ACT.Sqrt, scale=1.0 / D, bias=g.eps[:, :]).then_inc(s["t_root"], 1)


def mixture(g, out):
    nc, a = g.nc, g.a
    table = nc.dram_tensor("lists", (NE * CAP, 1), F32).ap()
    x_rows = nc.dram_tensor("moe_x", (T, D), F32).ap()
    y_rows = nc.dram_tensor("moe_y_rows", (NE * CAP, D), F32).ap()
    g.ring_ctx.close()
    with ExitStack() as ctx:
        def sb(name, shape, dt=F32):
            return ctx.enter_context(nc.sbuf_tensor(name, shape, dt))
        slot = sb("slot", [P, 2, TT], U32)
        result = sb("result_row", [P, 2, TT], U32)
        weight = sb("pair_weight", [P, TT, 2])
        slots = sb("slots", [P, P], U32)
        over = sb("over_flag", [P, 1], I32)
        gain = sb("moe_gain", [P, DC])
        with ExitStack() as local:
            xn = local.enter_context(nc.sbuf_tensor("moe_xn", [P, TT, D], F32))
            with ExitStack() as inner:
                norm_transposed(g, None, None, inner, gain_src=a["norm_ffn_g_2"][0], keep=xn, gain_keep=gain)
            route(g, xn, x_rows, table, slot, result, weight, slots, over)
        with ExitStack() as local:
            extra = [local.enter_context(nc.sbuf_tensor(f"w2_slot{i}", [P, FC * D], F32)) for i in range(2)]
            w13 = [tuple(local.enter_context(nc.sbuf_tensor(fresh("w13"), [P, DC, BANK], F32)) for _ in range(2)) for _ in range(2)]
            run_experts(g, w13, extra, slots, x_rows, y_rows, gain)
            run_overflow(g, over, w13, extra, slots, x_rows, y_rows, gain)
        finish(g, result, weight, y_rows, over, out)


def plan_weights(g):
    a = g.a
    g.plan(a["w_in"][0], 0, C_RQ)
    for i in range(4):
        g.plan(a["w_in"][0], C_RQ + i * BANK, BANK)
    for i in range(2):
        g.plan(a["w_out"][0], i * BANK, BANK)
    for i in range(4):
        g.plan(a["w_query"][0], i * BANK, BANK)
    for name, groups in (("w_xk_2", 4), ("w_xv_2", MEM // P)):
        for i in range(2):
            g.plan(a[name][0], i * BANK, BANK, groups)
    for c in (W2_MQ, W2_MK, W2_DQ, W2_DK, W2_DV, W2_MO, W2_MV):
        g.plan(a["w_in_2"][0], c, BANK)
    g.plan(a["w_in_2"][0], W2_GATES, 2 * ML_H, 2)
    for i in range(2):
        g.plan(a["w_out_2"][0], i * BANK, BANK)
    for name, groups in (("w_xq_2", 4), ("w_xo_2", TT)):
        for i in range(2):
            g.plan(a[name][0], i * BANK, BANK, groups)


def second_mixer(g, first_unit):
    nc, a = g.nc, g.a
    with ExitStack() as local:
        norm_transposed(g, None, None, local, gain_src=a["norm_mix_g_2"][0], upto=first_unit + RING)
    with ExitStack() as ctx:
        def sb(name, shape, dt=F32):
            return ctx.enter_context(nc.sbuf_tensor(name, shape, dt))
        tok = sb("tok", [P, TT, 4 * BANK])
        mv = sb("ml_v", [P, TT, ML_H, ML_D + 1])
        with ExitStack() as inner:
            conv = inner.enter_context(nc.sbuf_tensor("conv", [P, 8, T], F32))
            mi = inner.enter_context(nc.sbuf_tensor("ml_i", [ML_H, T], F32))
            mf = inner.enter_context(nc.sbuf_tensor("ml_f", [ML_H, T], F32))
            project_second(g, tok, mv, conv, mi, mf, first_unit)
            differential(g, tok)
            mlstm(g, tok, mv, conv, mi, mf)

        def mixed(k):
            c = k * P if k < 4 else 3 * BANK + (k - 4) * P
            return tok[:, :, c:c + P]
        with ExitStack() as local:
            mix_out(g, mixed, first_unit + 8, None, local)


def build(nc, a):
    PAST.clear()
    NAMED.clear()
    with ExitStack() as ctx:
        ctx.enter_context(nc.allow_non_contiguous_dma(reason="short columns of parameters"))
        g = Core(nc, ctx, a)
        plan_weights(g)
        first = ctx.enter_context(ExitStack())

        def sb(name, shape, dt=F32):
            return first.enter_context(nc.sbuf_tensor(name, shape, dt))
        col = sb("col", [P, 32])
        gate_row = sb("gate_row", [P, 2, D])
        c_act = sb("c_act", [P, DC])
        key1_t, key2_t, gate_t = g.diff, sb("key2_t", [P, T]), sb("gate_t", [P, T])
        g.open_ring()
        proj_ctx = ctx.enter_context(ExitStack())
        proj = proj_ctx.enter_context(nc.sbuf_tensor("proj", [P, TT, IN_COLS], F32))
        ada_loaded = [nc.alloc_semaphore(f"ada_loaded{i}") for i in range(ADA_SLOTS)]
        ada_used = nc.alloc_semaphore("ada_used")
        with ExitStack() as early:
            ada_acc = early.enter_context(nc.sbuf_tensor("ada_acc", [P, 6 * D], F32))
            ada_in = early.enter_context(nc.sbuf_tensor("ada_in", [P, ADA_SLOTS, ADA], F32))
            prelude(g, proj, ada_in, ada_acc, c_act, col, ada_loaded, ada_used)
            project(g, proj, ada_in, ada_acc, c_act, col, gate_row, ada_loaded, ada_used)
        retention(g, proj)
        latent_attention(g, proj)

        def mixed(k):
            c = C_RQ + k * P if k < 4 else C_RG + (k - 4) * P
            return proj[:, :, c:c + P]
        with ExitStack() as local:
            mix_out(g, mixed, 5, gate_row[:, 0, :], local)
        with ExitStack() as local:
            norm_transposed(g, col[:, 24:32], col[:, 16:24], local, keep=proj[:, :, 0:D])
        proj_ctx.close()
        mem_kt, mem_v = (nc.dram_tensor(n, (P, MEM * DC), F32).ap() for n in ("memory_keys", "memory_values"))
        gates = nc.dram_tensor("gates_by_key", (PK, PK, T), F32).ap()
        with ExitStack() as local:
            top_v = local.enter_context(nc.sbuf_tensor("top_v", [P, TT, 2 * PH, TOPK], F32))
            top_i = local.enter_context(nc.sbuf_tensor("top_i", [P, TT, 2 * PH, TOPK], U32))
            top_keys(g, top_v, top_i, 7)
            choose_experts(g, top_v, top_i, key1_t, key2_t, gate_t, 11, mem_kt, mem_v)
        g.ring_ctx.close()
        spread_gates(g, key1_t, key2_t, gate_t, gates)
        with ExitStack() as peer:
            acc = peer.enter_context(nc.sbuf_tensor("peer_acc", [P, TT, D], F32))
            experts(g, gates, acc)
            close_first(g, acc, gate_row[:, 1, :])
        first.close()
        g.open_ring()
        second_mixer(g, 15)
        cross_attention(g, 25, mem_kt, mem_v)
        mixture(g, a["out"])


def layout(inputs):
    out = dict(inputs)
    out["u_tiles"] = np.ascontiguousarray(out.pop("expert_u")[0].reshape(PK, PK, DC, P).transpose(0, 3, 2, 1))
    out["sub_keys_t"] = np.ascontiguousarray(out.pop("sub_keys")[0].transpose(0, 2, 1))
    return out



def kernel(**inputs):
    import concourse.bacc as bacc
    from concourse.bass_utils import run_bass_kernel_spmd

    arrays = layout({name: np.ascontiguousarray(value) for name, value in inputs.items()})
    nc = bacc.Bacc("TRN2", target_bir_lowering=False, num_devices=1)
    aps, fed = {}, {}
    for name, value in arrays.items():
        fed[f"in_{name}"] = value
        aps[name] = nc.dram_tensor(f"in_{name}", value.shape, mybir.dt.from_np(value.dtype), kind="ExternalInput").ap()
    aps["out"] = nc.dram_tensor("result", (1, T, D), F32, kind="ExternalOutput").ap()
    build(nc, aps)
    r = run_bass_kernel_spmd(nc, [fed], core_ids=[0])
    return r.results[0]["result"]
```
